# Optimizing a Trainium2 kernel written in Bass

```python
import math
import jax, jax.numpy as jnp
from jax import lax
import numpy as np

D_MODEL = 1024
BATCH = 1
SEQ = 1024
DEPTH = 2
DEC_BATCH = 8
DEC_SEQ = 1
PAST_LEN = 2048
PAGE_SIZE = 128

N_EVEN = (DEPTH + 1) // 2
N_ODD = DEPTH // 2
H_A = 4
DK_A = D_MODEL // 8
DV_A = D_MODEL // 8
CONV_A = 4
CHUNK_A = 64
H_B = 8
DH_B = D_MODEL // 16
Q_BLOCK = 128
FORGET_BIAS = 9.0
D_CONV = D_MODEL
CONV_C = 31
N_MEM = 256
H_X = 4
DH_X = D_MODEL // H_X
D_FF = 4 * D_MODEL
EPS = 1e-6

W_QK_A = H_A * DK_A
W_V_A = H_A * DV_A
W_B = H_B * DH_B
W_CONV_A = 2 * W_QK_A + W_V_A
OFF_ZA = W_CONV_A
OFF_AA = OFF_ZA + W_V_A
OFF_BA = OFF_AA + H_A
OFF_QB = OFF_BA + H_A
OFF_KB = OFF_QB + W_B
OFF_VB = OFF_KB + W_B
OFF_FB = OFF_VB + W_B
P_EVEN = OFF_FB + H_B

kernel_name = 'hybrid_gdn_fox_conformer_step'

F32 = jnp.float32

def rmsnorm(x, g):
    xf = x.astype(F32)
    y = xf * lax.rsqrt(jnp.mean(xf * xf, axis=-1, keepdims=True) + EPS)
    return (y * g.astype(F32)).astype(x.dtype)

def layernorm(x, g, b):
    xf = x.astype(F32)
    mu = jnp.mean(xf, axis=-1, keepdims=True)
    xc = xf - mu
    y = xc * lax.rsqrt(jnp.mean(xc * xc, axis=-1, keepdims=True) + EPS)
    return (y * g.astype(F32) + b.astype(F32)).astype(x.dtype)

def l2norm(x):
    xf = x.astype(F32)
    return xf * lax.rsqrt(jnp.sum(xf * xf, axis=-1, keepdims=True) + EPS)

def causal_dwconv(buf, x, w):
    full = jnp.concatenate([buf.astype(x.dtype), x], axis=1)
    y = lax.conv_general_dilated(full, w[:, None, :].astype(x.dtype), window_strides=(1,), padding='VALID',
                                 dimension_numbers=('NWC', 'WIO', 'NWC'), feature_group_count=x.shape[-1])
    return y, full[:, -(w.shape[0] - 1):]

def gated_delta_rule(q, k, v, g, beta, s0):
    B, L, H, DK = q.shape
    DV = v.shape[-1]
    C = min(CHUNK_A, L)
    pad = (-L) % C
    N = (L + pad) // C

    def prep(t):
        t = jnp.pad(t, [(0, 0), (0, pad)] + [(0, 0)] * (t.ndim - 2))
        t = t.reshape((B, N, C) + t.shape[2:])
        return jnp.transpose(t, (1, 0, 3, 2, 4)) if t.ndim == 5 else jnp.transpose(t, (1, 0, 3, 2))

    qc, kc, vc, bc = prep(q), prep(k), prep(v), prep(beta)
    gc = jnp.cumsum(prep(g), axis=-1)
    idx = jnp.arange(C)
    causal = idx[:, None] >= idx[None, :]
    strict = idx[:, None] > idx[None, :]
    decay = jnp.exp(jnp.where(causal, gc[..., :, None] - gc[..., None, :], -jnp.inf))
    kb = kc * bc[..., None]
    vb = vc * bc[..., None]
    lmat = jnp.where(strict, jnp.einsum('nbhid,nbhjd->nbhij', kb, kc) * decay, 0.0)
    eye = jnp.eye(C, dtype=F32)
    t_inv = lax.linalg.triangular_solve(eye + lmat, jnp.broadcast_to(eye, lmat.shape), left_side=True,
                                        lower=True, unit_diagonal=True)
    u = jnp.einsum('nbhij,nbhje->nbhie', t_inv, vb)
    w = jnp.einsum('nbhij,nbhjd->nbhid', t_inv, kb * jnp.exp(gc)[..., None])
    a_qk = jnp.where(causal, jnp.einsum('nbhid,nbhjd->nbhij', qc, kc) * decay, 0.0)

    def step(s, xs):
        q_i, k_i, u_i, w_i, g_i, a_i = xs
        v_new = u_i - jnp.einsum('bhcd,bhde->bhce', w_i, s)
        o_i = jnp.einsum('bhcd,bhde->bhce', q_i * jnp.exp(g_i)[..., None], s) + jnp.einsum('bhij,bhje->bhie', a_i, v_new)
        g_last = g_i[..., -1]
        s = s * jnp.exp(g_last)[..., None, None] + jnp.einsum(
            'bhcd,bhce->bhde', k_i * jnp.exp(g_last[..., None] - g_i)[..., None], v_new)
        return s, o_i

    s_fin, o = lax.scan(step, s0, (qc, kc, u, w, gc, a_qk))
    o = jnp.transpose(o, (1, 0, 3, 2, 4)).reshape(B, N * C, H, DV)[:, :L]
    return o, s_fin

def fox_prompt(q, k, v, logf):
    B, L, H, D = q.shape
    nq = L // Q_BLOCK
    c = jnp.cumsum(logf, axis=1)
    c_t = jnp.transpose(c, (0, 2, 1))
    qs = jnp.transpose(q.reshape(B, nq, Q_BLOCK, H, D), (1, 0, 2, 3, 4))
    cs = jnp.transpose(c_t.reshape(B, H, nq, Q_BLOCK), (2, 0, 1, 3))
    kpos = jnp.arange(L)
    scale = D ** -0.5

    def block(args):
        q_blk, c_blk, i = args
        s = jnp.einsum('bqhd,bkhd->bhqk', q_blk, k, preferred_element_type=F32) * scale
        s = s + c_blk[..., :, None] - c_t[:, :, None, :]
        qpos = i * Q_BLOCK + jnp.arange(Q_BLOCK)
        s = jnp.where(kpos[None, :] <= qpos[:, None], s, -jnp.inf)
        p = jax.nn.softmax(s, axis=-1)
        return jnp.einsum('bhqk,bkhd->bqhd', p.astype(v.dtype), v)

    o = lax.map(block, (qs, cs, jnp.arange(nq)))
    return jnp.transpose(o, (1, 0, 2, 3, 4)).reshape(B, L, H, D)

def fox_sample(q, k, v, logf, ck, cv, clf, page_table):
    DB, T, H, D = q.shape
    kp = ck[page_table].reshape(DB, -1, H, D)
    vp = cv[page_table].reshape(DB, -1, H, D)
    lfp = clf[page_table].reshape(DB, -1, H).astype(F32)
    past = kp.shape[1]
    c_past = lfp - lax.cumsum(lfp, axis=1, reverse=True)
    c_new = jnp.cumsum(logf, axis=1)
    scale = D ** -0.5
    cq = jnp.transpose(c_new, (0, 2, 1))[..., :, None]
    s_past = jnp.einsum('bthd,bshd->bhts', q, kp, preferred_element_type=F32) * scale \
        + cq - jnp.transpose(c_past, (0, 2, 1))[:, :, None, :]
    s_new = jnp.einsum('bthd,bshd->bhts', q, k, preferred_element_type=F32) * scale \
        + cq - jnp.transpose(c_new, (0, 2, 1))[:, :, None, :]
    tpos = jnp.arange(T)
    s_new = jnp.where(tpos[None, :] <= tpos[:, None], s_new, -jnp.inf)
    p = jax.nn.softmax(jnp.concatenate([s_past, s_new], axis=-1), axis=-1)
    return jnp.einsum('bhts,bshd->bthd', p[..., :past].astype(v.dtype), vp) \
        + jnp.einsum('bhts,bshd->bthd', p[..., past:].astype(v.dtype), v)

def even_mixer(h, e, s0, buf0, fox_past, P):
    B, L, _ = h.shape
    proj = h @ P['w_in_e'][e]
    conv_out, new_buf = causal_dwconv(buf0, proj[..., :W_CONV_A], P['conv_a'][e])
    conv_out = jax.nn.silu(conv_out)
    qa = l2norm(conv_out[..., :W_QK_A].reshape(B, L, H_A, DK_A)) * (DK_A ** -0.5)
    ka = l2norm(conv_out[..., W_QK_A:2 * W_QK_A].reshape(B, L, H_A, DK_A))
    va = conv_out[..., 2 * W_QK_A:].reshape(B, L, H_A, DV_A).astype(F32)
    za = proj[..., OFF_ZA:OFF_AA].reshape(B, L, H_A, DV_A).astype(F32)
    a_in = proj[..., OFF_AA:OFF_BA].astype(F32)
    g = -jnp.exp(P['a_log'][e].astype(F32)) * jax.nn.softplus(a_in + P['dt_bias'][e].astype(F32))
    beta = jax.nn.sigmoid(proj[..., OFF_BA:OFF_QB].astype(F32))
    oa, s_fin = gated_delta_rule(qa, ka, va, g, beta, s0.astype(F32))
    oa = (rmsnorm(oa, P['gnorm_a'][e]) * jax.nn.silu(za)).astype(h.dtype).reshape(B, L, W_V_A)
    qb = proj[..., OFF_QB:OFF_KB].reshape(B, L, H_B, DH_B)
    kb = proj[..., OFF_KB:OFF_VB].reshape(B, L, H_B, DH_B)
    vb = proj[..., OFF_VB:OFF_FB].reshape(B, L, H_B, DH_B)
    logf = jax.nn.log_sigmoid(proj[..., OFF_FB:].astype(F32) + P['b_f'][e].astype(F32))
    if fox_past is None:
        ob = fox_prompt(qb, kb, vb, logf)
    else:
        ob = fox_sample(qb, kb, vb, logf, *fox_past)
    out = jnp.concatenate([oa, ob.reshape(B, L, W_B).astype(h.dtype)], axis=-1) @ P['w_out_e'][e]
    return out, s_fin.astype(h.dtype), new_buf, kb, vb, logf.astype(h.dtype)

def odd_mixer(h, o, buf0, P):
    u = h @ P['w_pw1'][o] + P['b_pw1'][o]
    glu = u[..., :D_CONV] * jax.nn.sigmoid(u[..., D_CONV:])
    y, new_buf = causal_dwconv(buf0, glu, P['w_dw'][o])
    y = jax.nn.silu(layernorm(y + P['b_dw'][o], P['ln_g'][o], P['ln_b'][o]))
    return y @ P['w_pw2'][o], new_buf

def mem_kv(mem, l, P):
    B = mem.shape[0]
    kv = rmsnorm(mem, P['norm_mem'][l]) @ P['w_xkv'][l]
    return kv[..., :D_MODEL].reshape(B, N_MEM, H_X, DH_X), kv[..., D_MODEL:].reshape(B, N_MEM, H_X, DH_X)

def cross_attn(h, mk, mv, l, P):
    B, L, _ = h.shape
    q = (h @ P['w_xq'][l]).reshape(B, L, H_X, DH_X)
    s = jnp.einsum('blhd,bmhd->bhlm', q, mk, preferred_element_type=F32) * (DH_X ** -0.5)
    p = jax.nn.softmax(s, axis=-1)
    o = jnp.einsum('bhlm,bmhd->blhd', p.astype(mv.dtype), mv)
    return o.reshape(B, L, D_MODEL) @ P['w_xo'][l]

def mlp(h, l, P):
    return jnp.square(jax.nn.relu(h @ P['w_up'][l])) @ P['w_down'][l]

def trunk(x, mem_k, mem_v, gdn_s, gdn_buf, cfm_buf, fox_past, P):
    s_l, gb_l, cb_l, fk_l, fv_l, flf_l = [], [], [], [], [], []
    for l in range(DEPTH):
        h = rmsnorm(x, P['norm_mix'][l])
        if l % 2 == 0:
            e = l // 2
            past = None if fox_past is None else (fox_past[0][e], fox_past[1][e], fox_past[2][e], fox_past[3])
            out, s_new, gb, fk, fv, flf = even_mixer(h, e, gdn_s[e], gdn_buf[e], past, P)
            s_l.append(s_new); gb_l.append(gb); fk_l.append(fk); fv_l.append(fv); flf_l.append(flf)
        else:
            o = l // 2
            out, cb = odd_mixer(h, o, cfm_buf[o], P)
            cb_l.append(cb)
        x = x + out
        x = x + cross_attn(rmsnorm(x, P['norm_x'][l]), mem_k[l], mem_v[l], l, P)
        x = x + mlp(rmsnorm(x, P['norm_f'][l]), l, P)
    y = rmsnorm(x, P['norm_out'])
    return y, jnp.stack(s_l), jnp.stack(gb_l), jnp.stack(cb_l), jnp.stack(fk_l), jnp.stack(fv_l), jnp.stack(flf_l)

def setup_inputs(seed: int = 0) -> dict:
    key = jax.random.key(seed)
    ks = iter(jax.random.split(key, 48))
    n_pages = PAST_LEN // PAGE_SIZE
    n_pool = (5 * DEC_BATCH * n_pages) // 4

    def nrm(shape, scale=1.0):
        return scale * jax.random.normal(next(ks), shape, F32)

    def gain(shape):
        return 1.0 + nrm(shape, 0.02)

    inp = {}
    inp['x_prompt'] = nrm((BATCH, SEQ, D_MODEL))
    inp['x_sample'] = nrm((DEC_BATCH, DEC_SEQ, D_MODEL))
    inp['mem_prompt'] = nrm((BATCH, N_MEM, D_MODEL))
    inp['cache_fox_k'] = nrm((N_EVEN, n_pool, PAGE_SIZE, H_B, DH_B))
    inp['cache_fox_v'] = nrm((N_EVEN, n_pool, PAGE_SIZE, H_B, DH_B))
    inp['cache_fox_logf'] = jax.nn.log_sigmoid(FORGET_BIAS + nrm((N_EVEN, n_pool, PAGE_SIZE, H_B)))
    inp['page_table'] = jax.random.permutation(next(ks), n_pool)[:DEC_BATCH * n_pages].reshape(
        DEC_BATCH, n_pages).astype(jnp.int32)
    inp['state_gdn'] = nrm((N_EVEN, DEC_BATCH, H_A, DK_A, DV_A), 0.1)
    inp['state_gdn_conv'] = nrm((N_EVEN, DEC_BATCH, CONV_A - 1, W_CONV_A))
    inp['state_cfm_conv'] = nrm((N_ODD, DEC_BATCH, CONV_C - 1, D_CONV), 0.5)
    inp['cache_mem_k'] = nrm((DEPTH, DEC_BATCH, N_MEM, H_X, DH_X))
    inp['cache_mem_v'] = nrm((DEPTH, DEC_BATCH, N_MEM, H_X, DH_X))
    inp['norm_mix'] = gain((DEPTH, D_MODEL))
    inp['w_in_e'] = nrm((N_EVEN, D_MODEL, P_EVEN), D_MODEL ** -0.5)
    inp['conv_a'] = nrm((N_EVEN, CONV_A, W_CONV_A), CONV_A ** -0.5)
    inp['a_log'] = jnp.log(jax.random.uniform(next(ks), (N_EVEN, H_A), F32, 1.0, 16.0))
    dt = jnp.exp(jax.random.uniform(next(ks), (N_EVEN, H_A), F32, math.log(1e-3), math.log(1e-1)))
    inp['dt_bias'] = dt + jnp.log(-jnp.expm1(-dt))
    inp['gnorm_a'] = gain((N_EVEN, DV_A))
    inp['b_f'] = FORGET_BIAS + nrm((N_EVEN, H_B), 0.1)
    inp['w_out_e'] = nrm((N_EVEN, W_V_A + W_B, D_MODEL), (W_V_A + W_B) ** -0.5)
    inp['w_pw1'] = nrm((N_ODD, D_MODEL, 2 * D_CONV), D_MODEL ** -0.5)
    inp['b_pw1'] = nrm((N_ODD, 2 * D_CONV), 0.02)
    inp['w_dw'] = nrm((N_ODD, CONV_C, D_CONV), CONV_C ** -0.5)
    inp['b_dw'] = nrm((N_ODD, D_CONV), 0.02)
    inp['ln_g'] = gain((N_ODD, D_CONV))
    inp['ln_b'] = nrm((N_ODD, D_CONV), 0.02)
    inp['w_pw2'] = nrm((N_ODD, D_CONV, D_MODEL), D_CONV ** -0.5)
    inp['norm_mem'] = gain((DEPTH, D_MODEL))
    inp['norm_x'] = gain((DEPTH, D_MODEL))
    inp['w_xq'] = nrm((DEPTH, D_MODEL, D_MODEL), D_MODEL ** -0.5)
    inp['w_xkv'] = nrm((DEPTH, D_MODEL, 2 * D_MODEL), D_MODEL ** -0.5)
    inp['w_xo'] = nrm((DEPTH, D_MODEL, D_MODEL), D_MODEL ** -0.5)
    inp['norm_f'] = gain((DEPTH, D_MODEL))
    inp['w_up'] = nrm((DEPTH, D_MODEL, D_FF), D_MODEL ** -0.5)
    inp['w_down'] = nrm((DEPTH, D_FF, D_MODEL), D_FF ** -0.5)
    inp['norm_out'] = gain((D_MODEL,))
    return inp

def reference(x_prompt, x_sample, mem_prompt, cache_fox_k, cache_fox_v, cache_fox_logf, page_table,
              state_gdn, state_gdn_conv, state_cfm_conv, cache_mem_k, cache_mem_v,
              norm_mix, w_in_e, conv_a, a_log, dt_bias, gnorm_a, b_f, w_out_e,
              w_pw1, b_pw1, w_dw, b_dw, ln_g, ln_b, w_pw2,
              norm_mem, norm_x, w_xq, w_xkv, w_xo, norm_f, w_up, w_down, norm_out):
    P = dict(norm_mix=norm_mix, w_in_e=w_in_e, conv_a=conv_a, a_log=a_log, dt_bias=dt_bias, gnorm_a=gnorm_a,
             b_f=b_f, w_out_e=w_out_e, w_pw1=w_pw1, b_pw1=b_pw1, w_dw=w_dw, b_dw=b_dw, ln_g=ln_g, ln_b=ln_b,
             w_pw2=w_pw2, norm_mem=norm_mem, norm_x=norm_x, w_xq=w_xq, w_xkv=w_xkv, w_xo=w_xo,
             norm_f=norm_f, w_up=w_up, w_down=w_down, norm_out=norm_out)
    mkv = [mem_kv(mem_prompt, l, P) for l in range(DEPTH)]
    mem_k_prompt = jnp.stack([kv[0] for kv in mkv])
    mem_v_prompt = jnp.stack([kv[1] for kv in mkv])
    dt = x_prompt.dtype
    s0 = jnp.zeros((N_EVEN, BATCH, H_A, DK_A, DV_A), dt)
    gb0 = jnp.zeros((N_EVEN, BATCH, CONV_A - 1, W_CONV_A), dt)
    cb0 = jnp.zeros((N_ODD, BATCH, CONV_C - 1, D_CONV), dt)
    y_prompt, gdn_p, gconv_p, cconv_p, fk_p, fv_p, flf_p = trunk(
        x_prompt, mem_k_prompt, mem_v_prompt, s0, gb0, cb0, None, P)
    y_sample, gdn_s, gconv_s, cconv_s, fk_s, fv_s, flf_s = trunk(
        x_sample, cache_mem_k, cache_mem_v, state_gdn, state_gdn_conv, state_cfm_conv,
        (cache_fox_k, cache_fox_v, cache_fox_logf, page_table), P)
    return (y_prompt, y_sample, fk_p, fv_p, flf_p, fk_s, fv_s, flf_s,
            gdn_p, gconv_p, gdn_s, gconv_s, cconv_p, cconv_s, mem_k_prompt, mem_v_prompt)


_drawn_inputs = setup_inputs


def setup_inputs(seed=0):
    import zlib

    import numpy as np

    out = dict(_drawn_inputs(seed))
    spreads = {}
    factors = {'cache_fox_k': 2.736,
     'cache_fox_logf': 8.0,
     'gnorm_a': 5.79,
     'b_dw': 4.108,
     'ln_g': 6.296,
     'ln_b': 7.498,
     'norm_mem': 2.824,
     'norm_x': 8.0,
     'norm_out': 2.893}
    for name, (base, spread) in spreads.items():
        noise = np.random.default_rng([zlib.crc32(name.encode()), seed]).standard_normal(out[name].shape)
        drawn = base * np.exp(spread * noise) if base else spread * noise
        out[name] = __import__('jax').numpy.asarray(drawn.astype(out[name].dtype))
    for name, factor in factors.items():
        out[name] = (out[name] * factor).astype(out[name].dtype)
    return out
```

```python
from contextlib import ExitStack, contextmanager

import concourse.bass as bass
from concourse import mybir

P = 128
D = 1024
KC = D // P
SEQ, NB = 1024, 8
T = SEQ + NB
N3 = T // 3
QT = SEQ // P
PAST, PAGE = 2048, 128
NPG = PAST // PAGE
HA, HB, DHB = 4, 8, 64
HX, DHX, NMEM = 4, 256, 256
CA, CC = 4, 31
EPS = 1e-6
NEG = -1e30
FF_GROUPS = 4

F32 = mybir.dt.float32
I32 = mybir.dt.int32
ACT = mybir.ActivationFunctionType
ALU = mybir.AluOpType
AX = mybir.AxisListType
ds = bass.ds

VECS = [("norm_mix0", 8), ("norm_mix1", 8), ("norm_x0", 8), ("norm_x1", 8), ("norm_f0", 8), ("norm_f1", 8),
        ("norm_mem0", 8), ("norm_mem1", 8), ("norm_out", 8), ("b_pw1", 16), ("b_dw", 8), ("ln_g", 8), ("ln_b", 8),
        ("gnorm", 1), ("conv_a", 48), ("w_dw", 248), ("gate_bias", 16), ("gate_alog", 16)]
VOFF, _o = {}, 0
for _n, _w in VECS:
    VOFF[_n] = (_o, _w)
    _o += _w
NVEC = _o

STREAM = [("v_fox", 1), ("k_fox", 1), ("q_fox", 1), ("conv", 3), ("z", 1), ("out", 2)]
for _l in range(2):
    if _l == 1:
        STREAM += [("pw1", 4), ("pw2", 2)]
    STREAM += [(f"mk{_l}", 2), (f"mv{_l}", 2), (f"xq{_l}", 2), (f"xo{_l}", 2)]
    for _g in range(FF_GROUPS):
        STREAM += [(f"up{_l}{_g}", 2), (f"down{_l}{_g}", 2)]
PAIR0, GROUP0, _p, _g = {}, {}, 0, 0
for _n, _w in STREAM:
    PAIR0[_n], GROUP0[_n] = _p, _g
    _p += _w
    _g += 18 if _n == "v_fox" else 4 * _w
NPAIRS = _p
G_V = 18


class Steps:

    def __init__(self, eng, sem):
        self.eng, self.sem, self.n, self.at = eng, sem, 0, None

    def link(self, ins):
        self.n += 1
        ins.then_inc(self.sem, 1)
        self.eng.wait_ge(self.sem, self.n if self.at is None else self.at + self.n)

    @contextmanager
    def loop(self, trips, per):
        entry = self.n
        with self.eng.Fori(0, trips) as i:
            self.at, self.n = i * per + entry, 0
            yield i
            assert self.n == per, f"{self.n} linked steps in a round, not {per}"
        self.at, self.n = None, entry + trips * per


def build(nc, xT_in, memT_in, vecs_in, wall, wgate_in, st_gconv_in, st_cconv_in, pages_in, kpool, vpool, fpool, st_gdn,
          cmk, cmv, yT, fkT, fv, flf, gdn_p, gconv, gkeep, gdn_s, cconv, ckeep, mkT, mv):
    ctx = ExitStack()
    with ctx:
        def sb(name, shape, dt=F32):
            return ctx.enter_context(nc.sbuf_tensor(name, shape, dt))

        def sem(name):
            return ctx.enter_context(nc.semaphore(name))

        xT = sb("xT", [P, KC, T])
        hT = sb("hT", [P, KC, T])
        aT = sb("aT", [P, KC, T])
        big = sb("big", [P, 12, T])
        w = sb("w", [P, 2, KC, 256])
        wk = sb("wk", [P, 8850])
        vec = sb("vec", [P, NVEC])
        ident = sb("ident", [P, P])
        ones = sb("ones", [P, P])
        upper = sb("upper", [P, P])
        later = sb("later", [P, P])
        strict = sb("strict", [P, P])
        neg_qk = sb("neg_qk", [P, P])
        neg_ji = sb("neg_ji", [P, P])
        lev = sb("lev", [P, 7, P])
        page_later = sb("page_later", [P, P])
        lev0T = sb("lev0T", [P, P])
        eps = sb("eps", [P, 1])
        gt = sb("gt", [P, 9, 11, 4])
        lf = sb("lf", [P, 9, 8])
        cf = sb("cf", [P, 8, 8])
        sm = sb("sm", [P, 32])
        gcoef = sb("gcoef", [P, 16])
        pages = wk[0:1, 8550:8550 + NB * NPG].bitcast(I32)
        pagec = sb("pagec", [P, 1], I32)
        ps = ctx.enter_context(nc.psum_tensor("ps", [P, 8, 512], F32))

        def v(name, c=0, n=1):
            return vec[:, VOFF[name][0] + c:VOFF[name][0] + c + n]

        def part(buf, off, *shape):
            n = 1
            for s in shape:
                n *= s
            flat = buf[:, off:off + n]
            if len(shape) == 1:
                return flat
            names = "abcd"[:len(shape)]
            return flat.rearrange(f"p ({' '.join(names)}) -> p {' '.join(names)}",
                                  **{a: s for a, s in zip(names[1:], shape[1:])})

        bigf = big[:, :, :].rearrange("p a b -> p (a b)")
        hTf = hT[:, :, :].rearrange("p a b -> p (a b)")
        aTf = aT[:, :, :].rearrange("p a b -> p (a b)")
        psf = ps[:, :, :].rearrange("p a b -> p (a b)")

        def thirds(ap):
            return ap.rearrange("p (a n) -> p a n", a=3)

        def psum_set(s):
            return ps[:, 3 * s:3 * s + 3, 0:N3]

        in_loaded = sem("in_loaded")
        w_loaded = [sem("w_loaded0"), sem("w_loaded1")]
        consts_ready = sem("consts_ready")
        psum_ready = sem("psum_ready")
        psum_free = sem("psum_free")
        stored = sem("stored")
        act_steps, dve_steps, pool_steps, pe_steps = sem("act_steps"), sem("dve_steps"), sem("pool_steps"), sem("pe_steps")
        nm_sq, nm_add, nm_sum, nm_rt, nm_rc, nm_bc, nm_cp, nm_out = (sem("nm_" + n) for n in (
            "sq", "add", "sum", "rt", "rc", "bc", "cp", "out"))
        n_stored = [0]

        S = {}

        def pool_consts(pool):
            link = S["pool"].link
            g = nc.gpsimd
            link(g.memset(ident[:], 0.0))
            link(g.affine_select(out=ident[:], in_=ident[:], compare_op=ALU.not_equal, fill=1.0, base=0,
                                 pattern=[[-1, P]], channel_multiplier=1))
            for m, start, op, fill, step in ((upper, 1.0, ALU.is_ge, 0.0, 1), (later, 1.0, ALU.is_gt, 0.0, -1),
                                             (strict, 1.0, ALU.is_gt, 0.0, 1), (neg_qk, 0.0, ALU.is_ge, NEG, -1),
                                             (neg_ji, 0.0, ALU.is_ge, NEG, 1)):
                link(g.memset(m[:], start))
                link(g.affine_select(out=m[:], in_=m[:], compare_op=op, fill=fill, base=0, pattern=[[step, P]],
                                     channel_multiplier=-step))
            link(g.memset(lev[:], 0.0))
            link(g.memset(lev0T[:], 0.0))
            for s in range(7):
                b = 1 << s
                half = lev[:, s, :].rearrange("p (k t r) -> p k t r", t=2, r=b)[:, :, 0, :]
                link(g.memset(half, 1.0))
                link(g.affine_select(out=half, in_=half, compare_op=ALU.is_ge, fill=0.0, base=-b,
                                     pattern=[[-2 * b, P // (2 * b)], [0, b]], channel_multiplier=1))
                link(g.affine_select(out=half, in_=half, compare_op=ALU.is_ge, fill=0.0, base=2 * b - 1,
                                     pattern=[[2 * b, P // (2 * b)], [0, b]], channel_multiplier=-1))
            odd = lev0T[:, :].rearrange("p (k t) -> p k t", t=2)[:, :, 1]
            link(g.memset(odd, 1.0))
            link(g.affine_select(out=odd, in_=odd, compare_op=ALU.is_equal, fill=0.0, base=0,
                                 pattern=[[-2, P // 2]], channel_multiplier=1))
            link(g.memset(page_later[:], 1.0))
            pl = page_later[:, :].rearrange("p (b g) -> p b g", g=NPG)
            link(g.affine_select(out=pl, in_=pl, compare_op=ALU.is_gt, fill=0.0, base=0,
                                 pattern=[[-NPG, NB], [-1, NPG]], channel_multiplier=1))
            link(g.affine_select(out=pl, in_=pl, compare_op=ALU.is_ge, fill=0.0, base=NPG - 1,
                                 pattern=[[NPG, NB], [0, NPG]], channel_multiplier=-1))
            link(g.memset(eps[:], EPS))
            link(g.memset(gt[:], 0.0))
            g.memset(ones[:], 1.0).then_inc(consts_ready, 1)

        wgate = part(wk, 8700, KC, 16)

        def sp_loads(sp):
            for dst, src in ((xT[:], xT_in), (vec[:], vecs_in), (wgate, wgate_in),
                             (pages, pages_in), (pagec[:], pages_in.rearrange("a (p b) -> (a p) b", b=1))):
                sp.dma_start(dst, src).then_inc(in_loaded, 16)

            def load(i, s):
                sp.dma_start(w[:, s, :, :], wall[ds(2 * i + s, 1)].rearrange("a p (k n) -> p (a k) n", k=KC))\
                    .then_inc(w_loaded[s], 16)

            for s in range(2):
                load(0, s)
            for s in range(2):
                sp.wait_ge(psum_ready, 9 * (s + 1))
                load(1, s)
            with sp.Fori(2, NPAIRS) as i:
                for s in range(2):
                    sp.wait_ge(psum_ready, i * 4 + (G_V - 8 + 2 * (s + 1)))
                    load(i, s)

        sq = part(wk, 0, 2, T)
        acc = part(wk, 2 * T, T)
        rbc = part(wk, 3 * T, T)

        def tiles_of(width):
            out = [(t * P, P, 0, (t // 4) * 512 + (t % 4) * P) for t in range(width // P)]
            if width % P:
                out.append((width - P, width % P, P - width % P, (width // P // 4) * 512))
            return out

        def pe_norm(pe, n, width, ready_adds=True):
            pe.wait_ge(nm_add, 8 * (n + 1))
            tl = tiles_of(width)
            for j, (at, cnt, skip, _) in enumerate(tl):
                ins = nc.tensor.matmul(ps[:, 6, j:j + 1], acc[:, at:at + P], ones[:, 0:1], start=True, stop=True)
            ins.then_inc(nm_sum, 1)
            pe.wait_ge(nm_rc, n + 1)
            for j, (at, cnt, skip, to) in enumerate(tl):
                ins = nc.tensor.matmul(psf[:, to:to + cnt], sm[:, 16 + j:17 + j].to_broadcast([P, P]),
                                       ident[:, skip:skip + cnt], start=True, stop=True)
            ins.then_inc(nm_bc, 1)

        def act_norm(act, n, src, width, wait):
            wait(act)
            for c in range(KC):
                if c >= 2:
                    act.wait_ge(nm_add, 8 * n + c - 1)
                nc.scalar.activation(sq[:, c % 2, 0:width], src[:, c, :], ACT.Square).then_inc(nm_sq, 1)
            k = len(tiles_of(width))
            act.wait_ge(nm_sum, n + 1)
            nc.scalar.activation(sm[:, 0:k], ps[:, 6, 0:k], ACT.Sqrt, bias=eps[:, 0:1], scale=1.0 / D)\
                .then_inc(nm_rt, 1)
            act.wait_ge(nm_bc, n + 1)
            full = width - width % P
            ins = nc.scalar.activation(rbc[:, 0:full], psf[:, 0:full], ACT.Copy)
            if width % P:
                ins = nc.scalar.activation(rbc[:, full:width], psf[:, full:width], ACT.Copy)
            ins.then_inc(nm_cp, 1)

        def dve_norm(dve, n, src, dst, width, gain, wait_dst=None):
            link = S["dve"].link
            for c in range(KC):
                dve.wait_ge(nm_sq, 8 * n + c + 1)
                if c == 0:
                    nc.vector.tensor_copy(acc[:, 0:width], sq[:, 0, 0:width]).then_inc(nm_add, 1)
                else:
                    nc.vector.tensor_tensor(acc[:, 0:width], acc[:, 0:width], sq[:, c % 2, 0:width], ALU.add)\
                        .then_inc(nm_add, 1)
                dve.wait_ge(nm_add, 8 * n + c + 1)
            k = len(tiles_of(width))
            dve.wait_ge(nm_rt, n + 1)
            nc.vector.reciprocal(sm[:, 16:16 + k], sm[:, 0:k]).then_inc(nm_rc, 1)
            dve.wait_ge(nm_cp, n + 1)
            for c in range(KC):
                nc.vector.scalar_tensor_tensor(out=dst[:, c, :], in0=src[:, c, :], scalar=v(gain, c), in1=rbc[:, 0:width],
                                               op0=ALU.mult, op1=ALU.mult).then_inc(nm_out, 1)

        def pe_product(pe, name, pairs, src, width, wait_src):
            wait_src(pe)
            p0, g0 = PAIR0[name], GROUP0[name]
            cols = [(n * N3, N3) for n in range(3)] if width == T else [(0, width)]
            with pe.Fori(0, pairs) as i:
                for s in range(2):
                    pe.wait_ge(w_loaded[s], i * 16 + 16 * (p0 + 1))
                    for o in range(2):
                        j = 2 * s + o
                        st = (g0 + j) % 2
                        pe.wait_ge(psum_free, i * 4 + (g0 + j - 1))
                        for k in range(KC):
                            for n, (c0, cn) in enumerate(cols):
                                ins = nc.tensor.matmul(ps[:, 3 * st + n, 0:cn], w[:, s, k, o * P:(o + 1) * P],
                                                       src[:, k, c0:c0 + cn], start=(k == 0), stop=(k == KC - 1))
                        ins.then_inc(psum_ready, 1)

        def epilogue(eng, name, pairs, op):
            g0 = GROUP0[name]
            with eng.Fori(0, pairs) as i:
                for j in range(4):
                    eng.wait_ge(psum_ready, i * 4 + (g0 + j + 1))
                    op(i, j, (g0 + j) % 2).then_inc(psum_free, 1)

        def at_chunk(buf, c):
            return buf[:, ds(c, 1), :].rearrange("p a (b n) -> p (a b) n", b=3)

        def after(*pairs):
            def wait(eng):
                for s, n in pairs:
                    eng.wait_ge(s, n)
            return wait

        def freed(name, pairs):
            return (psum_free, GROUP0[name] + 4 * pairs)

        def store(pool, dst, src):
            n_stored[0] += 1
            pool.dma_start(dst, src).then_inc(stored, 16)

        qf, kf = big[:, 0:4, :], big[:, 4:8, :]
        vf = part(bigf, 8 * T, QT, 512)
        vs = wk[0:NB, 8000:8512]

        def pe_values(pe):
            pe.wait_ge(nm_out, 8)
            for s in range(2):
                pe.wait_ge(w_loaded[s], 16)
                for t in range(QT + 1):
                    g = 9 * s + t
                    m = P if t < QT else NB
                    if g >= 2:
                        pe.wait_ge(psum_free, g - 1)
                    for k in range(KC):
                        ins = nc.tensor.matmul(ps[0:m, 3 * (g % 2), 0:256], hT[:, k, t * P:t * P + m], w[:, s, k, :],
                                               start=(k == 0), stop=(k == KC - 1))
                    ins.then_inc(psum_ready, 1)

        def act_values(act):
            for g in range(18):
                s, t = divmod(g, 9)
                act.wait_ge(psum_ready, g + 1)
                if t < QT:
                    ins = nc.scalar.activation(vf[:, t, s * 256:s * 256 + 256], ps[:, 3 * (g % 2), 0:256], ACT.Copy)
                else:
                    ins = nc.scalar.activation(vs[:, s * 256:s * 256 + 256], ps[0:NB, 3 * (g % 2), 0:256], ACT.Copy)
                ins.then_inc(psum_free, 1)

        gates_ready, gates_u, gates_exp, gates_done, gc_ready = (sem(n) for n in (
            "gates_ready", "gates_u", "gates_exp", "gates_done", "gc_ready"))
        ga = [part(wk, 4200 + 144 * n, 9, 16) for n in range(8)]
        gbank = ps[:, 7, 0:144].rearrange("p (t n) -> p t n", n=16)
        G_G, G_GC, G_RQ, G_RK, G_RQE, G_RKB, G_B, G_BE, G_KD, G_EL, G_E = range(11)
        tile_at = [t * P for t in range(QT)] + [T - P]

        def pe_gates(pe):
            pe.wait_ge(in_loaded, 80)
            for t in range(9):
                for k in range(KC):
                    ins = nc.tensor.matmul(gbank[:, t, :], hT[:, k, tile_at[t]:tile_at[t] + P], wgate[:, k, :],
                                           start=(k == 0), stop=(k == KC - 1))
            ins.then_inc(gates_ready, 1)
            pe.wait_ge(gates_done, 1)
            for t in range(QT):
                nc.tensor.matmul(ps[:, 7, 256 + 4 * t:260 + 4 * t], upper[:], gt[:, t, G_G, :], start=True, stop=True)
            for t in range(QT):
                nc.tensor.matmul(ps[:, 7, 288 + 4 * t:292 + 4 * t], ones[:], gt[:, t, G_G, :], start=True, stop=True)
            for t in range(QT):
                for u in range(t + 1):
                    ins = nc.tensor.matmul(ps[:, 7, 320 + 8 * t:328 + 8 * t], upper[:] if u == t else ones[:],
                                           lf[:, u, :], start=(u == 0), stop=(u == t))
            ins.then_inc(gc_ready, 1)

        def act_gates(act):
            act.wait_ge(in_loaded, 80)
            nc.scalar.activation(gcoef[:], v("gate_alog", 0, 16), ACT.Exp).then_inc(gates_exp, 1)
            act.wait_ge(gates_u, 1)
            nc.scalar.activation(ga[2], ga[2], ACT.Exp).then_inc(gates_exp, 1)
            nc.scalar.activation(ga[4], ga[0], ACT.Exp).then_inc(gates_exp, 1)
            act.wait_ge(gates_u, 2)
            for src, dst in ((G_GC, G_E), (G_KD, G_KD), (G_EL, G_EL)):
                nc.scalar.activation(gt[:, :, dst, :], gt[:, :, src, :], ACT.Exp).then_inc(gates_exp, 1)

        def dve_gates(dve):
            link, vv = S["dve"].link, nc.vector
            dve.wait_ge(gates_ready, 1)
            dve.wait_ge(gates_exp, 1)
            y, ny, m, z, z2, h = ga[0], ga[1], ga[2], ga[3], ga[5], ga[6]
            bias = v("gate_bias", 0, 16).rearrange("p (a n) -> p a n", a=1).to_broadcast([P, 9, 16])
            link(vv.tensor_tensor(y, gbank, bias, ALU.add))
            link(vv.tensor_scalar(y[:, :, 4:16], y[:, :, 4:16], -1.0, None, ALU.mult))
            link(vv.tensor_scalar(ny, y, -1.0, None, ALU.mult))
            vv.tensor_tensor(m, y, ny, ALU.min).then_inc(gates_u, 1)
            dve.wait_ge(gates_exp, 3)
            link(vv.tensor_scalar(z, m, 2.0, None, ALU.add))
            link(vv.reciprocal(z, z))
            link(vv.tensor_tensor(z, z, m, ALU.mult))
            link(vv.tensor_tensor(z2, z, z, ALU.mult))
            link(vv.tensor_scalar(h, z2, 1.0 / 19, None, ALU.mult))
            for d in (17, 15, 13, 11, 9, 7, 5, 3):
                link(vv.scalar_tensor_tensor(out=h, in0=h, scalar=1.0 / d, in1=z2, op0=ALU.add, op1=ALU.mult))
            link(vv.scalar_tensor_tensor(out=h, in0=h, scalar=1.0, in1=z, op0=ALU.add, op1=ALU.mult))
            link(vv.tensor_scalar(ny, y, 0.0, None, ALU.max))
            link(vv.scalar_tensor_tensor(out=h, in0=h, scalar=2.0, in1=ny, op0=ALU.mult, op1=ALU.add))
            link(vv.tensor_scalar(lf[:], h[:, :, 8:16], -1.0, None, ALU.mult))
            link(vv.tensor_scalar(gcoef[:], gcoef[:], -1.0, None, ALU.mult))
            coef = gcoef[:, 0:4].rearrange("p (a n) -> p a n", a=1).to_broadcast([P, 9, 4])
            link(vv.tensor_scalar(ga[4], ga[4], 1.0, None, ALU.add))
            link(vv.reciprocal(gt[:, :, G_B, :], ga[4][:, :, 4:8]))
            vv.tensor_tensor(gt[:, :, G_G, :], h[:, :, 0:4], coef, ALU.mult).then_inc(gates_done, 1)
            dve.wait_ge(gc_ready, 1)
            dve.wait_ge(gates_done, 1)
            gc_ps = ps[:, 7, 256:288].rearrange("p (t n) -> p t n", n=4)
            tot_ps = ps[:, 7, 288:320].rearrange("p (t n) -> p t n", n=4)
            link(vv.tensor_copy(cf[:], ps[:, 7, 320:384].rearrange("p (t n) -> p t n", n=8)))
            link(vv.tensor_copy(gt[:, 0:QT, G_GC, :], gc_ps))
            link(vv.tensor_copy(gt[:, 0:QT, G_EL, :], tot_ps))
            link(vv.tensor_copy(gt[:, QT, G_GC, :], gt[:, QT, G_G, :]))
            link(vv.tensor_copy(gt[:, QT, G_EL, :], gt[:, QT, G_G, :]))
            vv.tensor_tensor(gt[:, :, G_KD, :], gt[:, :, G_EL, :], gt[:, :, G_GC, :], ALU.subtract).then_inc(gates_u, 1)
            dve.wait_ge(gates_exp, 6)
            link(vv.tensor_tensor(gt[:, :, G_BE, :], gt[:, :, G_B, :], gt[:, :, G_E, :], ALU.mult))

        fox_cst, fox_qk, fox_cb, fox_cbc, fox_s, fox_m, fox_e, fox_pt, fox_ptc, fox_o, fox_on, fox_ot, fox_otc = (
            sem("fox_" + n) for n in ("cst", "qk", "cb", "cbc", "s", "m", "e", "pt", "ptc", "o", "on", "ot", "otc"))
        f_neg = part(aTf, 0, 2, SEQ)
        f_pt = part(aTf, 2 * SEQ, 2, SEQ)
        f_q = part(wk, 0, SEQ)
        f_k = part(wk, SEQ, SEQ)
        f_s = part(wk, 2 * SEQ, 2, SEQ)
        f_o = part(wk, 4 * SEQ, QT, P)
        f_c = part(wk, 5 * SEQ, QT, 2)
        f_st = part(wk, 5 * SEQ + 16, 4, 16)
        NT = 2 * QT

        def blk(n):
            return n // QT, n % QT, (n % QT + 1) * P

        def pe_fox(pe):
            with pe.Fori(0, 4) as i:
                pe.wait_ge(fox_cst, i + 1)
                for h in range(2):
                    if h == 0:
                        pe.wait_ge(fox_otc, i + 1)
                    else:
                        pe.wait_ge(fox_cbc, i * 2 + 1)
                    for t in range(QT):
                        ins = nc.tensor.matmul(psf[:, t * P:t * P + P], f_c[:, t, h:h + 1].to_broadcast([P, P]),
                                               ident[:], start=True, stop=True)
                    ins.then_inc(fox_cb, 1)
                pe.wait_ge(fox_qk, i * 2 + 2)
                pe.wait_ge(fox_cbc, i * 2 + 2)

                def scores(n):
                    h, t, wd = blk(n)
                    if n >= 2:
                        pe.wait_ge(fox_m, i * NT + (n - 1))
                    for c0 in range(0, wd, 512):
                        cn = min(512, wd - c0)
                        ins = nc.tensor.matmul(psf[:, (n % 2) * 1024 + c0:(n % 2) * 1024 + c0 + cn],
                                               f_q[64 * h:64 * h + 64, t * P:t * P + P],
                                               f_k[64 * h:64 * h + 64, c0:c0 + cn], start=True, stop=True)
                    ins.then_inc(fox_s, 1)

                def turn(n):
                    h, t, wd = blk(n)
                    pe.wait_ge(fox_e, i * NT + (n + 1))
                    if n:
                        pe.wait_ge(fox_ptc, i * NT + n)
                    for c0 in range(0, wd, P):
                        ins = nc.tensor.transpose(psf[:, 2048 + c0:2048 + c0 + P], f_s[:, n % 2, c0:c0 + P], ident[:])
                    ins.then_inc(fox_pt, 1)

                def values(n):
                    h, t, wd = blk(n)
                    pe.wait_ge(fox_ptc, i * NT + (n + 1))
                    if n >= 2:
                        pe.wait_ge(fox_on, i * NT + (n - 1))
                    for kt in range(t + 1):
                        ins = nc.tensor.matmul(ps[:, 6 + n % 2, 0:64], f_pt[:, n % 2, kt * P:kt * P + P],
                                               vf[:, kt, ds(i * P + h * 64, 64)], start=(kt == 0), stop=(kt == t))
                    ins.then_inc(fox_o, 1)

                scores(0)
                for n in range(NT):
                    if n + 1 < NT:
                        scores(n + 1)
                    turn(n)
                    values(n)
                pe.wait_ge(fox_on, i * NT + NT)
                for t in range(QT):
                    ins = nc.tensor.transpose(psf[:, t * P:t * P + P], f_o[:, t, :], ident[:])
                ins.then_inc(fox_ot, 1)

        def act_fox(act):
            act.sem_inc(fox_otc, 1)
            with act.Fori(0, 4) as i:
                for h in range(2):
                    act.wait_ge(fox_cb, i * 2 + (h + 1))
                    nc.scalar.activation(f_neg[:, h, :], psf[:, 0:SEQ], ACT.Copy, scale=-1.0).then_inc(fox_cbc, 1)
                for n in range(NT):
                    h, t, wd = blk(n)
                    act.wait_ge(fox_m, i * NT + (n + 1))
                    nc.scalar.activation(f_s[:, n % 2, 0:wd], f_s[:, n % 2, 0:wd], ACT.Exp, bias=f_st[:, 1, n:n + 1],
                                         accum_out=f_st[:, 2, n:n + 1]).then_inc(fox_e, 1)
                    act.wait_ge(fox_pt, i * NT + (n + 1))
                    if n >= 2:
                        act.wait_ge(fox_o, i * NT + (n - 1))
                    nc.scalar.activation(f_pt[:, n % 2, 0:wd], psf[:, 2048:2048 + wd], ACT.Copy).then_inc(fox_ptc, 1)
                act.wait_ge(fox_ot, i + 1)
                nc.scalar.activation(aT[:, ds(i + 4, 1), 0:SEQ].rearrange("p a n -> p (a n)"), psf[:, 0:SEQ], ACT.Copy)\
                    .then_inc(fox_otc, 1)

        def pool_fox(pool):
            pool.wait_ge(*freed("q_fox", 1))
            pool.wait_ge(gates_exp, 6)
            with pool.Fori(0, 4) as i:
                pool.wait_ge(fox_otc, i + 1)
                nc.gpsimd.tensor_copy(f_c, cf[:, :, ds(i * 2, 2)]).then_inc(fox_cst, 1)
                nc.gpsimd.tensor_copy(f_q, qf[:, ds(i, 1), 0:SEQ].rearrange("p a n -> p (a n)")).then_inc(fox_qk, 1)
                nc.gpsimd.tensor_copy(f_k, kf[:, ds(i, 1), 0:SEQ].rearrange("p a n -> p (a n)")).then_inc(fox_qk, 1)

        def dve_fox(dve):
            PER = NT * 3
            with S["dve"].loop(4, PER) as i:
                link, vv = S["dve"].link, nc.vector

                def soft(n):
                    h, t, wd = blk(n)
                    dve.wait_ge(fox_s, i * NT + (n + 1))
                    dve.wait_ge(fox_cbc, i * 2 + 2)
                    if n >= 2:
                        dve.wait_ge(fox_pt, i * NT + (n - 1))
                    link(vv.tensor_tensor(f_s[:, n % 2, 0:wd], psf[:, (n % 2) * 1024:(n % 2) * 1024 + wd],
                                          f_neg[:, h, 0:wd], ALU.add))
                    link(vv.tensor_tensor(f_s[:, n % 2, t * P:wd], f_s[:, n % 2, t * P:wd], neg_qk[:], ALU.add))
                    vv.tensor_reduce(f_st[:, 1, n:n + 1], f_s[:, n % 2, 0:wd], AX.X, ALU.max, negate=True)\
                        .then_inc(fox_m, 1)

                def out(n):
                    h, t, wd = blk(n)
                    dve.wait_ge(fox_o, i * NT + (n + 1))
                    link(vv.reciprocal(f_st[:, 3, n:n + 1], f_st[:, 2, n:n + 1]))
                    if n == 0:
                        dve.wait_ge(fox_otc, i + 1)
                    vv.tensor_scalar(f_o[:, t, h * 64:h * 64 + 64], ps[:, 6 + n % 2, 0:64],
                                     f_st[:, 3, n:n + 1], None, ALU.mult).then_inc(fox_on, 1)

                soft(0)
                for n in range(NT):
                    if n + 1 < NT:
                        soft(n + 1)
                    out(n)

        fs_names = ("small", "turned", "lf", "lft", "lftot", "lfc", "bias", "col", "qb", "qc", "ring0", "ring1", "free", "sc",
                    "snp", "sn", "mx", "mt", "mc", "mb", "sh", "ex", "sum", "tot", "pr", "vring0", "vring1", "pv", "pvc", "out")
        fs = {n: sem("fs_" + n) for n in fs_names}
        s_ring = part(aTf, 0, 2, 4, 512)
        s_q, s_k, s_v = (part(wk, 7000 + 32 * n, 4, NB) for n in range(3))
        s_qb = part(wk, 0, 512)
        s_prod = part(wk, 512, 2048)
        s_sc = part(wk, 2560, NB, NPG, HB)
        s_lft = part(wk, 3584, 1024)
        s_lf = part(wk, 4608, HB, P)
        s_tot = part(wk, 5632, HB)
        s_col = part(wk, 5640, 4)
        s_qk = part(wk, 5648, 32)
        s_sn, s_mx, s_mb, s_sum, s_rs, s_cq = (part(wk, 5700 + 64 * n, NB, HB) for n in range(6))
        s_mc = part(wk, 6100, 1)
        s_o = part(wk, 6104, NB, 8)
        s_pv = part(wk, 6200, 4, NB)

        def heads_even_odd(ap, odd):
            return ap.rearrange("p b (c t) -> p t c b", t=2)[:, odd]

        def pool_fox_rows(pool):
            pool.wait_ge(fox_otc, 5)
            for n, src in ((0, qf), (1, kf)):
                dst = (s_q, s_k)[n]
                nc.gpsimd.tensor_copy(dst, src[:, :, SEQ:T]).then_inc(fs["small"], 1)
            pool.wait_ge(in_loaded, 80)
            pool.indirect_dma_start(out=s_lft, out_offset=None, in_=fpool.rearrange("g t h -> g (t h)"),
                                    in_offset=bass.IndirectOffsetOnAxis(ap=pagec[:, 0:1].bitcast(mybir.dt.uint32), axis=0))\
                .then_inc(fs["lf"], 16)

            def page_loop(src, done, used):
                with pool.Fori(0, 16) as r:
                    for s in range(2):
                        pool.wait_ge(fs["free"], r * 2 + (s + 1 + used))
                        for g in range(4):
                            pg = pool.value_load(pages[0:1, ds(r * 8 + (4 * s + g), 1)], min_val=0,
                                                 max_val=src.shape[0] - 1)
                            pool.dma_start(s_ring[:, s, g, :], src[ds(pg, 1)].rearrange("a p n -> p (a n)"))\
                                .then_inc(fs[f"{done}{s}"], 16)

            page_loop(kpool, "ring", 0)
            page_loop(vpool, "vring", 32)

        def pe_fox_rows(pe):
            pe.wait_ge(fox_otc, 5)
            for c in range(4):
                ins = nc.tensor.transpose(ps[:, 7, c * NB:(c + 1) * NB], vs[:, c * P:(c + 1) * P], ident[0:NB, 0:NB])
            ins.then_inc(fs["turned"], 1)
            pe.wait_ge(fs["lf"], 16)
            for h in range(HB):
                ins = nc.tensor.transpose(psf[:, 2048 + h * P:2048 + (h + 1) * P],
                                          s_lft.rearrange("p (t h) -> p h t", h=HB)[:, h, :], ident[:])
            ins.then_inc(fs["lft"], 1)
            pe.wait_ge(fs["lftot"], 1)
            pe.wait_ge(fs["lfc"], 1)
            for h in range(HB):
                to = psf[:, 2048 + h * P:2048 + (h + 1) * P]
                nc.tensor.matmul(to, later[:], s_lf[:, h, :], start=True, stop=False)
                nc.tensor.matmul(to, s_tot[:, h:h + 1].to_broadcast([P, P]), page_later[:], start=False, stop=True)
            for h in range(HB):
                ins = nc.tensor.matmul(ps[:, 6, h * NB:(h + 1) * NB], lf[:, QT, h:h + 1].to_broadcast([P, P]),
                                       ident[:, P - NB:P], start=True, stop=True)
            ins.then_inc(fs["bias"], 1)
            with pe.Fori(0, NB) as b:
                pe.wait_ge(fs["col"], b + 1)
                for c in range(4):
                    ins = nc.tensor.matmul(ps[:, 0, c * P:(c + 1) * P], s_col[:, c:c + 1].to_broadcast([P, P]), ident[:],
                                           start=True, stop=True)
                ins.then_inc(fs["qb"], 1)
            pe.wait_ge(fs["snp"], 1)
            for t in range(2):
                ins = nc.tensor.matmul(ps[:, 1 + 2 * t, 0:32], ones[64 * t:64 * t + 64, :], s_qk[64 * t:64 * t + 64, :],
                                       start=True, stop=True)
            ins.then_inc(fs["sn"], 1)
            pe.wait_ge(fs["mx"], 1)
            nc.tensor.transpose(ps[0:64, 2, 0:P], s_mx.rearrange("p b h -> p (b h)"), ident[:]).then_inc(fs["mt"], 1)
            pe.wait_ge(fs["mc"], 1)
            nc.tensor.matmul(ps[:, 3, 0:64], s_mc[0:64, :].to_broadcast([64, P]), ident[0:64, 0:64], start=True, stop=True)\
                .then_inc(fs["mb"], 1)
            pe.wait_ge(fs["sum"], 1)
            nc.tensor.matmul(ps[:, 2, 128:192], ones[:], s_sum.rearrange("p b h -> p (b h)"), start=True, stop=True)\
                .then_inc(fs["tot"], 1)
            pe.wait_ge(fs["pr"], 1)
            with pe.Fori(0, 4) as r:
                for e in range(2):
                    pe.wait_ge(fs["pvc"], r * 2 + (e + 1))
                    for q in range(4):
                        pe.wait_ge(fs[f"vring{q % 2}"], r * 256 + 64 * (2 * e + q // 2 + 1))
                        for g in range(4):
                            pg = 4 * q + g
                            for c in range(4):
                                ins = nc.tensor.matmul(
                                    ps[:, e, 2 * c:2 * c + 2], s_ring[:, q % 2, g, c * P:(c + 1) * P],
                                    s_sc[:, ds(r * 2 + e, 1), pg, 2 * c:2 * c + 2].rearrange("p a h -> p (a h)"),
                                    start=(pg == 0 and c == 0), stop=(pg == NPG - 1), skip_group_check=True)
                        ins.then_inc(fs["pv"], 1)

        def act_fox_rows(act):
            act.wait_ge(fs["lft"], 1)
            nc.scalar.activation(s_lf.rearrange("p h t -> p (h t)"), psf[:, 2048:3072], ACT.Copy).then_inc(fs["lfc"], 1)
            act.wait_ge(fs["small"], 2)
            link = S["act"].link
            with act.Fori(0, NB) as b:
                act.wait_ge(fs["qc"], b + 1)
                nc.scalar.activation(s_col, s_q[:, :, ds(b, 1)].rearrange("p c a -> p (c a)"), ACT.Copy)\
                    .then_inc(fs["col"], 1)
                act.wait_ge(fs["qb"], b + 1)
                nc.scalar.activation(s_qb, ps[:, 0, :], ACT.Copy).then_inc(fs["sc"], 1)
            act.wait_ge(fs["sh"], 1)
            nc.scalar.activation(s_sc, s_sc, ACT.Exp).then_inc(fs["ex"], 1)
            nc.scalar.activation(s_sn, s_sn, ACT.Exp).then_inc(fs["ex"], 1)
            act.sem_inc(fs["pvc"], 2)
            with act.Fori(0, 4) as r:
                for e in range(2):
                    act.wait_ge(fs["pv"], r * 8 + (4 * (e + 1)))
                    nc.scalar.activation(s_o[:, ds(r * 2 + e, 1), :].rearrange("p a n -> p (a n)"), ps[:, e, 0:8], ACT.Copy)\
                        .then_inc(fs["pvc"], 1)

        def dve_fox_rows(dve):
            link, vv = S["dve"].link, nc.vector
            dve.wait_ge(fs["turned"], 1)
            link(vv.tensor_copy(s_v, ps[:, 7, 0:32].rearrange("p (c b) -> p c b", b=NB)))
            dve.wait_ge(fs["lf"], 16)
            vv.tensor_reduce(s_tot, s_lft.rearrange("p (t h) -> p h t", h=HB), AX.X, ALU.add).then_inc(fs["lftot"], 1)
            dve.wait_ge(fs["small"], 2)
            vv.tensor_tensor(s_qk, s_q.rearrange("p c b -> p (c b)"), s_k.rearrange("p c b -> p (c b)"), ALU.mult)\
                .then_inc(fs["snp"], 1)
            dve.sem_inc(fs["qc"], 1)
            dve.sem_inc(fs["free"], 2)
            with S["dve"].loop(NB, 4) as b:
                link = S["dve"].link
                dve.wait_ge(fs["sc"], b + 1)
                for q in range(4):
                    dve.wait_ge(fs[f"ring{q % 2}"], b * 128 + 64 * (q // 2 + 1))
                    dve.wait_ge(fs["free"], b * 4 + (q + 2))
                    link(vv.tensor_tensor(s_prod.rearrange("p (g n) -> p g n", g=4), s_ring[:, q % 2, :, :],
                                          s_qb.rearrange("p (a n) -> p a n", a=1).to_broadcast([P, 4, 512]), ALU.mult))
                    vv.tensor_reduce(s_sc[:, ds(b, 1), 4 * q:4 * q + 4, :].rearrange("p a g h -> p (a g h)"),
                                     s_prod.rearrange("p (x n) -> p x n", n=DHB), AX.X, ALU.add).then_inc(fs["free"], 1)
                dve.sem_inc(fs["qc"], 1)
            link = S["dve"].link
            dve.wait_ge(fs["bias"], 1)
            dve.wait_ge(fs["free"], 34)
            link(vv.tensor_copy(s_cq, ps[:, 6, 0:64].rearrange("p (h b) -> p b h", b=NB)))
            link(vv.tensor_tensor(s_sc, s_sc, psf[:, 2048:3072].rearrange("p (h b g) -> p b g h", h=HB, b=NB), ALU.add))
            cq = s_cq.rearrange("p b (a h) -> p b a h", a=1).to_broadcast([P, NB, NPG, HB])
            link(vv.tensor_tensor(s_sc, s_sc, cq, ALU.add))
            vv.tensor_reduce(s_mx, s_sc.rearrange("p b g h -> p b h g"), AX.X, ALU.max).then_inc(fs["mx"], 1)
            dve.wait_ge(fs["sn"], 1)
            for t in range(2):
                link(vv.tensor_copy(heads_even_odd(s_sn, t), ps[:, 1 + 2 * t, 0:32].rearrange("p (c b) -> p c b", b=NB)))
            dve.wait_ge(fs["mt"], 1)
            vv.tensor_reduce(s_mc[0:64, :], ps[0:64, 2, 0:P], AX.X, ALU.max).then_inc(fs["mc"], 1)
            dve.wait_ge(fs["mb"], 1)
            link(vv.tensor_tensor(s_mb, ps[:, 3, 0:64].rearrange("p (b h) -> p b h", h=HB), s_sn, ALU.max))
            mb = s_mb.rearrange("p b (a h) -> p b a h", a=1).to_broadcast([P, NB, NPG, HB])
            link(vv.tensor_tensor(s_sn, s_sn, s_mb, ALU.subtract))
            vv.tensor_tensor(s_sc, s_sc, mb, ALU.subtract).then_inc(fs["sh"], 1)
            dve.wait_ge(fs["ex"], 1)
            vv.tensor_reduce(s_sum, s_sc.rearrange("p b g h -> p b h g"), AX.X, ALU.add).then_inc(fs["sum"], 1)
            dve.wait_ge(fs["ex"], 2)
            dve.wait_ge(fs["tot"], 1)
            link(vv.tensor_tensor(s_rs, ps[:, 2, 128:192].rearrange("p (b h) -> p b h", h=HB), s_sn, ALU.add))
            link(vv.reciprocal(s_rs, s_rs))
            link(vv.tensor_tensor(s_sn, s_sn, s_rs, ALU.mult))
            rs = s_rs.rearrange("p b (a h) -> p b a h", a=1).to_broadcast([P, NB, NPG, HB])
            vv.tensor_tensor(s_sc, s_sc, rs, ALU.mult).then_inc(fs["pr"], 1)
            with dve.Fori(0, 32) as r:
                dve.wait_ge(fs["pv"], r + 1)
                dve.sem_inc(fs["free"], 1)
            dve.wait_ge(fs["pvc"], 2 + NB)
            for t in range(2):
                half = slice(64 * t, 64 * t + 64)
                link(vv.tensor_tensor(s_pv[half], s_v[half], heads_even_odd(s_sn, t)[half], ALU.mult))
                vv.tensor_tensor(aT[half, 4:8, SEQ:T], s_pv[half], s_o.rearrange("p b (c t) -> p t c b", t=2)[half, t],
                                 ALU.add).then_inc(fs["out"], 1)

        conv_done, conv_st, conv_pad, conv_silu = (sem("conv_" + n) for n in ("done", "st", "pad", "silu"))
        c_raw = part(wk, 0, T + 3)
        c_tail = part(wk, 7800, 12, 3 + NB)
        c_st = part(wk, 7932, 12, 3, NB)

        def pool_conv(pool):
            pool.wait_ge(fs["out"], 2)
            nc.gpsimd.memset(c_raw[:, 0:3], 0.0).then_inc(conv_pad, 1)
            pool.dma_start(c_st, st_gconv_in).then_inc(conv_st, 16)

        def act_conv(act):
            g0 = GROUP0["conv"]
            act.wait_ge(conv_pad, 1)
            with act.Fori(0, 3) as i:
                for j in range(4):
                    st = (g0 + j) % 2
                    act.wait_ge(psum_ready, i * 4 + (g0 + j + 1))
                    nc.scalar.activation(c_tail[:, ds(i * 4 + j, 1), :].rearrange("p a n -> p (a n)"),
                                         ps[:, 3 * st + 2, N3 - NB - 3:N3], ACT.Copy)
                    nc.scalar.activation(thirds(c_raw[:, 3:T + 3]), psum_set(st), ACT.Copy).then_inc(psum_free, 1)
                    act.wait_ge(conv_done, i * 4 + (j + 1))
                    chunk = big[:, ds(i * 4 + j, 1), :].rearrange("p a n -> p (a n)")
                    nc.scalar.activation(chunk, chunk, ACT.Silu).then_inc(conv_silu, 1)

        def dve_conv(dve):
            vv, g0, w0 = nc.vector, GROUP0["conv"], VOFF["conv_a"][0]
            dve.wait_ge(stored, 16 * 5)
            dve.wait_ge(conv_st, 16)
            with S["dve"].loop(3, 4 * 7) as i:
                link = S["dve"].link
                for j in range(4):
                    dve.wait_ge(psum_free, i * 4 + (g0 + j + 1))
                    chunk = big[:, ds(i * 4 + j, 1), :].rearrange("p a n -> p (a n)")
                    for t in range(CA):
                        tap = vec[:, ds(i * 16 + (w0 + 4 * j + t), 1)]
                        row = c_st[:, ds(i * 4 + j, 1), t, :].rearrange("p a n -> p (a n)") if t < 3 else c_raw[:, SEQ + 3:]
                        if t == 0:
                            link(vv.tensor_scalar(chunk[:, SEQ:T], row, tap, None, ALU.mult))
                            link(vv.tensor_scalar(chunk[:, 0:SEQ], c_raw[:, 0:SEQ], tap, None, ALU.mult))
                            continue
                        link(vv.scalar_tensor_tensor(out=chunk[:, SEQ:T], in0=row, scalar=tap, in1=chunk[:, SEQ:T],
                                                     op0=ALU.mult, op1=ALU.add))
                        ins = vv.scalar_tensor_tensor(out=chunk[:, 0:SEQ], in0=c_raw[:, t:t + SEQ], scalar=tap,
                                                      in1=chunk[:, 0:SEQ], op0=ALU.mult, op1=ALU.add)
                        if t < 3:
                            link(ins)
                    ins.then_inc(conv_done, 1)

        l2_sq, l2_ps, l2_rt = sem("l2_sq"), sem("l2_ps"), sem("l2_rt")
        l2_n = [0]
        l_st, l_rc = part(wk, 2100, 72), part(wk, 2180, 72)

        def act_squares(act, src, heads, scale):
            n0 = l2_n[0]
            for h in range(heads):
                if h >= 2:
                    act.wait_ge(l2_ps, n0 + h - 1)
                nc.scalar.activation(sq[:, h % 2, :], src[:, h, :], ACT.Square).then_inc(l2_sq, 1)
            act.wait_ge(l2_ps, n0 + heads)
            nc.scalar.activation(l_st[:, 0:9 * heads], ps[:, 6, 0:9 * heads], ACT.Sqrt, bias=eps[:, 0:1], scale=scale)\
                .then_inc(l2_rt, 1)

        def pe_squares(pe, n0, heads):
            for h in range(heads):
                pe.wait_ge(l2_sq, n0 + h + 1)
                for t in range(9):
                    ins = nc.tensor.matmul(ps[:, 6, h * 9 + t:h * 9 + t + 1], sq[:, h % 2, tile_at[t]:tile_at[t] + P],
                                           ones[:, 0:1], start=True, stop=True)
                ins.then_inc(l2_ps, 1)

        def dve_norm_gates(dve):
            link, vv = S["dve"].link, nc.vector
            dve.wait_ge(l2_rt, 1)
            link(vv.reciprocal(l_rc, l_st))
            rc = l_rc.rearrange("p (k h t) -> p k t h", k=2, t=9)
            link(vv.tensor_scalar(gt[:, :, G_RQ, :], rc[:, 0], float(P) ** -0.5, None, ALU.mult))
            link(vv.tensor_copy(gt[:, :, G_RK, :], rc[:, 1]))
            link(vv.tensor_tensor(gt[:, :, G_RQE, :], gt[:, :, G_RQ, :], gt[:, :, G_E, :], ALU.mult))
            vv.tensor_tensor(gt[:, :, G_RKB, :], gt[:, :, G_RK, :], gt[:, :, G_B, :], ALU.mult).then_inc(l2_rt, 1)

        gd = {n: sem("gd_" + n) for n in ("st", "bc", "n", "p", "dt", "ex", "kt", "vt", "kb", "lt", "l", "lc", "ed",
                                          "b", "x", "xc", "e", "u", "uc", "ws", "vn", "o", "oc", "s", "zt")}
        Q8 = 2 * HA * P

        def quad(buf, n):
            return part(buf, n * Q8, 2 * HA, P)

        kn, kb, qn, qg, vS, ktok, vb, kbg = (quad(hTf, n) for n in range(8))
        kd, DT, AT, LT, L_, E_, D_ = (quad(wk, n) for n in range(7))
        X_, B_, u_, wT, vn = DT, (LT, kn), kb, L_, D_
        S_ = part(wk, 7168, HA, P)
        cst = part(wk, 7680, 2, 11, 4)
        P01, P23, P45, P67 = (psf[:, 1024 * n:1024 * n + 1024].rearrange("p (x n) -> p x n", n=P) for n in range(4))

        def cc(kind, x):
            return cst[:, x // HA, kind, x % HA:x % HA + 1]

        def per_token(kind):
            return cst[:, :, kind, :].rearrange("p a (h n) -> p a h n", n=1).to_broadcast([P, 2, HA, P])

        def split(ap):
            return ap.rearrange("p (a h) n -> p a h n", a=2)

        def over8(m):
            return m.rearrange("p (a n) -> p a n", a=1).to_broadcast([P, 2 * HA, P])

        def pool_gdn(pool):
            pool.wait_ge(*freed("z", 1))
            pool.wait_ge(l2_rt, 2)
            with pool.Fori(0, QT // 2) as i:
                pool.wait_ge(gd["s"], i * 2 + 1)
                nc.gpsimd.tensor_copy(cst, gt[:, ds(i * 2, 2), :, :]).then_inc(gd["st"], 1)
                nc.gpsimd.tensor_copy(split(vS), big[:, 8:12, ds(i * 256, 256)].rearrange("p h (a n) -> p a h n", a=2))\
                    .then_inc(gd["st"], 1)
                pool.wait_ge(gd["kt"], i + 1)
                pool.wait_ge(gd["st"], i * 2 + 2)
                nc.gpsimd.tensor_tensor(split(kbg), split(ktok), per_token(G_BE), ALU.mult).then_inc(gd["kb"], 1)
                nc.gpsimd.tensor_tensor(split(kd), split(ktok), per_token(G_KD), ALU.mult).then_inc(gd["kb"], 1)
                for s in range(1, 7):
                    if s == 1:
                        pool.wait_ge(gd["ed"], i * 7 + 1)
                    elif s >= 3:
                        pool.wait_ge(gd["x"], i * 6 + (s - 2))
                    nc.gpsimd.tensor_tensor(B_[s % 2], L_, over8(lev[:, s, :]), ALU.mult).then_inc(gd["b"], 1)

        def pe_gdn(pe):
            mm = nc.tensor.matmul

            def each(op, done, xs=range(2 * HA)):
                for x in xs:
                    ins = op(x)
                ins.then_inc(gd[done], 1)

            with pe.Fori(0, QT // 2) as i:
                pe.wait_ge(gd["st"], i * 2 + 2)
                pe.wait_ge(gd["oc"], i * 2 + 1)
                for to, kind in ((P01, G_RQ), (P23, G_RK), (P45, G_RQE), (P67, G_RKB)):
                    each(lambda x: mm(to[:, x, :], cc(kind, x).to_broadcast([P, P]), ident[:], start=True, stop=True), "bc")
                pe.wait_ge(gd["n"], i * 4 + 4)
                each(lambda x: mm(P45[:, x, :], cc(G_G, x).to_broadcast([P, P]), upper[:], start=True, stop=True), "p")
                each(lambda x: nc.tensor.transpose(P67[:, x, :], kn[:, x, :], ident[:]), "p")
                each(lambda x: mm(P23[:, x, :], kn[:, x, :], qn[:, x, :], start=True, stop=True), "p")
                each(lambda x: mm(P01[:, x, :], kn[:, x, :], kb[:, x, :], start=True, stop=True), "p")
                pe.wait_ge(gd["kt"], i + 1)
                each(lambda x: nc.tensor.transpose(P67[:, x, :], vS[:, x, :], ident[:]), "vt")
                pe.wait_ge(gd["lt"], i + 1)
                each(lambda x: nc.tensor.transpose(P01[:, x, :], LT[:, x, :], ident[:]), "l")
                for s in range(1, 7):
                    pe.wait_ge(gd["b"], i * 6 + s)
                    pe.wait_ge(gd["ed"], i * 7 + s)
                    each(lambda x: mm(P01[:, x, :], B_[s % 2][:, x, :], E_[:, x, :], start=True, stop=True), "x")
                    pe.wait_ge(gd["xc"], i * 6 + s)
                    if s < 6:
                        for x in range(2 * HA):
                            mm(P45[:, x, :], X_[:, x, :], D_[:, x, :], start=True, stop=True)
                    each(lambda x: mm(P23[:, x, :], D_[:, x, :], X_[:, x, :], start=True, stop=True), "e")
                pe.wait_ge(gd["ed"], i * 7 + 7)
                pe.wait_ge(gd["kb"], i * 2 + 2)
                for x in range(2 * HA):
                    mm(P01[:, x, :], E_[:, x, :], vb[:, x, :], start=True, stop=True)
                each(lambda x: mm(P23[:, x, :], kbg[:, x, :], E_[:, x, :], start=True, stop=True), "u")
                pe.wait_ge(gd["uc"], i * 2 + 2)
                for a in range(2):
                    hs = range(4 * a, 4 * a + 4)
                    pe.wait_ge(gd["s"], i * 2 + (a + 1))
                    each(lambda x: mm(P45[:, x % 4, :], wT[:, x, :], S_[:, x % 4, :], start=True, stop=True), "ws", hs)
                    pe.wait_ge(gd["vn"], i * 2 + (a + 1))
                    pe.wait_ge(gd["oc"], i * 2 + (a + 1))
                    for x in hs:
                        mm(P67[:, x % 4, :], kd[:, x, :], vn[:, x, :], start=True, stop=True)
                        mm(P45[:, 4 + x % 4, :], S_[:, x % 4, :], qg[:, x, :], start=True, stop=False)
                        ins = mm(P45[:, 4 + x % 4, :], vn[:, x, :], AT[:, x, :], start=False, stop=True)
                    ins.then_inc(gd["o"], 1)

        def act_gdn(act):
            act.sem_inc(gd["oc"], 1)
            with act.Fori(0, QT // 2) as i:
                act.wait_ge(gd["p"], i * 4 + 2)
                nc.scalar.activation(ktok, P67, ACT.Copy).then_inc(gd["kt"], 1)
                act.wait_ge(gd["dt"], i + 1)
                nc.scalar.activation(DT, DT, ACT.Exp).then_inc(gd["ex"], 1)
                act.wait_ge(gd["l"], i + 1)
                nc.scalar.activation(L_, P01, ACT.Copy).then_inc(gd["lc"], 1)
                for s in range(1, 7):
                    act.wait_ge(gd["x"], i * 6 + s)
                    nc.scalar.activation(X_, P01, ACT.Copy).then_inc(gd["xc"], 1)
                act.wait_ge(gd["u"], i + 1)
                nc.scalar.activation(u_, P01, ACT.Copy).then_inc(gd["uc"], 1)
                nc.scalar.activation(wT, P23, ACT.Copy).then_inc(gd["uc"], 1)
                for a in range(2):
                    act.wait_ge(gd["o"], i * 2 + (a + 1))
                    nc.scalar.activation(big[:, 8:12, ds(i * 256 + a * P, P)], P45[:, 4:8, :], ACT.Copy)\
                        .then_inc(gd["oc"], 1)

        def dve_gdn(dve):
            vv = nc.vector
            link = S["dve"].link
            dve.wait_ge(l2_rt, 2)
            vv.memset(S_, 0.0).then_inc(gd["s"], 1)
            with S["dve"].loop(QT // 2, 16) as i:
                link = S["dve"].link
                dve.wait_ge(gd["s"], i * 2 + 1)
                for n, (to, src, lo, bc) in enumerate(((qn, big, 0, P01), (kn, big, 4, P23), (qg, big, 0, P45),
                                                      (kb, big, 4, P67))):
                    dve.wait_ge(gd["bc"], i * 4 + (n + 1))
                    x = src[:, lo:lo + 4, ds(i * 256, 256)].rearrange("p h (a n) -> p a h n", a=2)
                    vv.tensor_tensor(split(to), x, split(bc), ALU.mult).then_inc(gd["n"], 1)
                dve.wait_ge(gd["p"], i * 4 + 1)
                for x in range(2 * HA):
                    ins = vv.scalar_tensor_tensor(out=DT[:, x, :], in0=P45[:, x, :], scalar=cc(G_GC, x), in1=neg_ji[:],
                                                  op0=ALU.subtract, op1=ALU.add)
                    if x < 2 * HA - 1:
                        link(ins)
                ins.then_inc(gd["dt"], 1)
                dve.wait_ge(gd["p"], i * 4 + 4)
                dve.wait_ge(gd["ex"], i + 1)
                link(vv.tensor_tensor(AT, P23, DT, ALU.mult))
                link(vv.tensor_tensor(DT, DT, over8(strict[:, :]), ALU.mult))
                vv.tensor_tensor(LT, P01, DT, ALU.mult).then_inc(gd["lt"], 1)
                dve.wait_ge(gd["vt"], i + 1)
                link(vv.tensor_tensor(split(vb), split(P67), per_token(G_B), ALU.mult))
                dve.wait_ge(gd["lt"], i + 1)
                link(vv.tensor_tensor(E_, LT, over8(lev0T[:, :]), ALU.mult))
                link(vv.tensor_tensor(E_, over8(ident[:, :]), E_, ALU.subtract))
                dve.wait_ge(gd["lc"], i + 1)
                link(vv.tensor_tensor(D_, L_, over8(lev[:, 0, :]), ALU.mult))
                vv.tensor_tensor(D_, over8(ident[:, :]), D_, ALU.subtract).then_inc(gd["ed"], 1)
                for s in range(1, 7):
                    dve.wait_ge(gd["e"], i * 6 + s)
                    dve.wait_ge(gd["ed"], i * 7 + s)
                    if s < 6:
                        vv.tensor_tensor(D_, D_, P45, ALU.subtract)
                    vv.tensor_tensor(E_, E_, P23, ALU.subtract).then_inc(gd["ed"], 1)
                for a in range(2):
                    dve.wait_ge(gd["ws"], i * 2 + (a + 1))
                    dve.wait_ge(gd["uc"], i * 2 + 2)
                    vv.tensor_tensor(vn[:, 4 * a:4 * a + 4, :], u_[:, 4 * a:4 * a + 4, :], P45[:, 0:4, :], ALU.subtract)\
                        .then_inc(gd["vn"], 1)
                    dve.wait_ge(gd["o"], i * 2 + (a + 1))
                    for h in range(HA):
                        ins = vv.scalar_tensor_tensor(out=S_[:, h, :], in0=S_[:, h, :], scalar=cc(G_EL, 4 * a + h),
                                                      in1=P67[:, h, :], op0=ALU.mult, op1=ALU.add)
                        if h < HA - 1 and a == 0:
                            link(ins)
                    ins.then_inc(gd["s"], 1)

        gs = {n: sem("gs_" + n) for n in ("st", "cb", "n", "ps", "vn", "vr", "out")}
        NS = HA * NB
        st = part(hTf, 0, NB, HA, P)
        g_cb = part(wk, 4400, 6, HA, NB)
        g_q, g_k, g_vb, g_qk, g_vn = (part(wk, 4600 + 32 * n, HA, NB) for n in range(5))
        g_pair = part(wk, 4800, HA, NB, 2)
        KINDS = (G_RQ, G_RK, G_RQE, G_BE, G_B, G_EL)

        def pool_gdn_rows(pool):
            pool.wait_ge(gd["s"], QT + 1)
            store(pool, gdn_p, S_)
            pool.dma_start(st.rearrange("p b h n -> p (b h) n"), st_gdn.rearrange("b h p n -> p (b h) n"))\
                .then_inc(gs["st"], 16)

        def pe_gdn_rows(pe):
            pe.wait_ge(gd["oc"], QT + 1)
            for n, kind in enumerate(KINDS):
                for h in range(HA):
                    ins = nc.tensor.matmul(ps[:, 7, (n * HA + h) * NB:(n * HA + h + 1) * NB],
                                           gt[:, QT, kind, h:h + 1].to_broadcast([P, P]), ident[:, P - NB:P],
                                           start=True, stop=True)
            ins.then_inc(gs["cb"], 1)
            pe.wait_ge(gs["st"], 16)
            pe.wait_ge(gs["n"], 1)
            for h in range(HA):
                for b in range(NB):
                    nc.tensor.matmul(ps[:, 6, 2 * (h * NB + b):2 * (h * NB + b) + 2], st[:, b, h, :], g_pair[:, h, b, :],
                                     start=True, stop=True)
            nc.tensor.matmul(ps[:, 7, 256:288], ones[:], g_qk.rearrange("p h b -> p (h b)"), start=True, stop=True)\
                .then_inc(gs["ps"], 1)
            pe.wait_ge(gs["vn"], 1)
            for h in range(HA):
                for b in range(NB):
                    x = b * HA + h
                    ins = nc.tensor.matmul(psf[:, x * P:x * P + P], g_vn[:, h, b:b + 1].to_broadcast([P, P]), ident[:],
                                           start=True, stop=True)
            ins.then_inc(gs["vr"], 1)

        def dve_gdn_rows(dve):
            link, vv = S["dve"].link, nc.vector
            dve.wait_ge(gs["cb"], 1)
            link(vv.tensor_copy(g_cb, ps[:, 7, 0:192].rearrange("p (n h b) -> p n h b", n=6, b=NB)))
            cols = big[:, :, SEQ:T]
            link(vv.tensor_tensor(g_q, cols[:, 0:4], g_cb[:, 0], ALU.mult))
            link(vv.tensor_tensor(g_k, cols[:, 4:8], g_cb[:, 1], ALU.mult))
            link(vv.tensor_tensor(g_pair[:, :, :, 1], cols[:, 0:4], g_cb[:, 2], ALU.mult))
            link(vv.tensor_tensor(g_pair[:, :, :, 0], g_k, g_cb[:, 3], ALU.mult))
            link(vv.tensor_tensor(g_vb, cols[:, 8:12], g_cb[:, 4], ALU.mult))
            vv.tensor_tensor(g_qk, g_q, g_k, ALU.mult).then_inc(gs["n"], 1)
            dve.wait_ge(gs["ps"], 1)
            pr = ps[:, 6, 0:2 * NS].rearrange("p (h b t) -> p h b t", b=NB, t=2)
            qk = ps[:, 7, 256:288].rearrange("p (h b) -> p h b", b=NB)
            link(vv.tensor_tensor(g_vn, g_vb, pr[:, :, :, 0], ALU.subtract))
            link(vv.tensor_tensor(g_qk, qk, g_vn, ALU.mult))
            vv.tensor_tensor(cols[:, 8:12], g_qk, pr[:, :, :, 1], ALU.add).then_inc(gs["vn"], 1)
            dve.wait_ge(gs["vr"], 1)
            for h in range(HA):
                for b in range(NB):
                    link(vv.tensor_scalar(st[:, b, h, :], st[:, b, h, :], g_cb[:, 5, h, b:b + 1], None, ALU.mult))
                    x = b * HA + h
                    ins = vv.scalar_tensor_tensor(out=st[:, b, h, :], in0=psf[:, x * P:x * P + P],
                                                  scalar=g_k[:, h, b:b + 1], in1=st[:, b, h, :], op0=ALU.mult, op1=ALU.add)
                    if x < NS - 1:
                        link(ins)
            ins.then_inc(gs["out"], 1)

        gn = {n: sem("gn_" + n) for n in ("rc", "bc", "u", "oa")}
        n_t = part(wk, 2300, 2, T)

        def pe_head_norm(pe):
            pe.wait_ge(gs["out"], 1)
            pe_squares(pe, 8, HA)
            pe.wait_ge(gn["rc"], 1)
            for h in range(HA):
                if h >= 2:
                    pe.wait_ge(gn["u"], h - 1)
                base = 1536 * (h % 2)
                for t in range(9):
                    cnt = P if t < QT else NB
                    ins = nc.tensor.matmul(psf[:, base + t * P:base + t * P + cnt],
                                           l_rc[:, h * 9 + t:h * 9 + t + 1].to_broadcast([P, P]), ident[:, P - cnt:P],
                                           start=True, stop=True)
                ins.then_inc(gn["bc"], 1)

        def dve_head_norm(dve):
            link, vv = S["dve"].link, nc.vector
            dve.wait_ge(l2_rt, 3)
            vv.reciprocal(l_rc[:, 0:36], l_st[:, 0:36]).then_inc(gn["rc"], 1)
            for h in range(HA):
                dve.wait_ge(gn["bc"], h + 1)
                if h >= 2:
                    dve.wait_ge(gn["u"], h - 1)
                link(vv.scalar_tensor_tensor(out=n_t[:, h % 2], in0=big[:, 8 + h, :], scalar=v("gnorm"),
                                             in1=psf[:, 1536 * (h % 2):1536 * (h % 2) + T], op0=ALU.mult, op1=ALU.mult))
                vv.tensor_tensor(aT[:, h, :], aT[:, h, :], n_t[:, h % 2], ALU.mult).then_inc(gn["u"], 1)

        def residual(dve, name, pairs):
            dve.wait_ge(psum_free, GROUP0[name])
            epilogue(dve, name, pairs, lambda i, j, st: nc.vector.tensor_tensor(
                at_chunk(xT, i * 4 + j), at_chunk(xT, i * 4 + j), psum_set(st), ALU.add))

        m_raw, m_n, m_k = (part(bigf, 2048 * n, KC, NMEM) for n in range(3))
        m_v = part(bigf, 6144, 2, D)
        x_ring = part(bigf, 8192, 2, 2, D)
        xa = {n: sem("xa_" + n) for n in ("mem", "kd", "vd", "q", "qs", "s", "m", "e", "p", "t", "tc", "o", "oc", "col",
                                          "qb", "qbc", "free", "mx", "mt", "mc", "mb", "sh", "ex", "sum", "tot", "pr", "pv",
                                          "pvc", "ring0", "ring1", "vr0", "vr1")}
        x_q = part(wk, 0, 2, KC, P)
        x_p = part(wk, 2048, 2, HX, NMEM)
        x_t = part(wk, 4096, 2, KC, P)
        x_st = part(wk, 6144, 2, 3, HX)
        r_qb, r_prod = part(wk, 0, D), part(wk, 1024, 2, D)
        r_sc = part(wk, 3200, NB, 2, HX)
        r_mx, r_mb, r_sum, r_rs = (part(wk, 3300 + 32 * n, NB, HX) for n in range(4))
        r_mc, r_col = part(wk, 3440, 1), part(wk, 3450, KC)

        def pe_mem_values(pe, l):
            name = f"mv{l}"
            p0, g0 = PAIR0[name], GROUP0[name]
            with pe.Fori(0, 2) as i:
                for s in range(2):
                    pe.wait_ge(w_loaded[s], i * 16 + 16 * (p0 + 1))
                    for m in range(2):
                        j = 2 * s + m
                        pe.wait_ge(psum_free, i * 4 + (g0 + j - 1))
                        for k in range(KC):
                            ins = nc.tensor.matmul(ps[:, 3 * ((g0 + j) % 2), 0:256], m_n[:, k, m * P:(m + 1) * P],
                                                   w[:, s, k, :], start=(k == 0), stop=(k == KC - 1))
                        ins.then_inc(psum_ready, 1)

        def pool_cross(pool, l, norm_mem):
            pool.dma_start(m_raw, memT_in).then_inc(xa["mem"], 16)
            pool.wait_ge(*freed(f"mk{l}", 2))
            store(pool, mkT[l].rearrange("(c p) m -> p c m", p=P), m_k)
            pool.wait_ge(*freed(f"mv{l}", 2))
            store(pool, mv[l].rearrange("(t p) n -> p t n", p=P), m_v)
            pool.wait_ge(*freed(f"xq{l}", 2))
            with pool.Fori(0, 4) as r:
                for e in range(2):
                    pool.wait_ge(xa["oc"], r * 2 + (8 * l + e + 1))
                    nc.gpsimd.tensor_copy(x_q[:, e], aT[:, :, ds(r * 256 + e * P, P)]).then_inc(xa["qs"], 1)

            def ring_loop(src, done, used):
                with pool.Fori(0, NB // 2) as r:
                    for s in range(2):
                        pool.wait_ge(xa["free"], r * 2 + (16 * l + used + s + 1))
                        pool.dma_start(x_ring[:, s], src[l, ds(r * 2 + s, 1)].rearrange("a (t p) n -> p (a t) n", p=P))\
                            .then_inc(xa[f"{done}{s}"], 16)

            ring_loop(cmk, "ring", 0)
            ring_loop(cmv, "vr", NB)

        def pe_cross(pe, l):
            mm = nc.tensor.matmul

            def scores(r, e):
                pe.wait_ge(xa["qs"], r * 2 + (8 * l + e + 1))
                pe.wait_ge(xa["e"], r * 2 + (8 * l + e + 1))
                for h in range(HX):
                    for c in range(2):
                        ins = mm(psf[:, e * 1024 + h * 256:e * 1024 + h * 256 + 256], x_q[:, e, 2 * h + c, :],
                                 m_k[:, 2 * h + c, :], start=(c == 0), stop=(c == 1))
                ins.then_inc(xa["s"], 1)

            def rest(r, e):
                pe.wait_ge(xa["p"], r * 2 + (8 * l + e + 1))
                pe.wait_ge(xa["tc"], r * 2 + (8 * l + e + 1))
                for h in range(HX):
                    for m in range(2):
                        ins = nc.tensor.transpose(psf[:, 2048 + (2 * h + m) * P:2048 + (2 * h + m + 1) * P],
                                                  x_p[:, e, h, m * P:(m + 1) * P], ident[:])
                ins.then_inc(xa["t"], 1)
                pe.wait_ge(xa["tc"], r * 2 + (8 * l + e + 2))
                pe.wait_ge(xa["oc"], r * 2 + (8 * l + e + 2))
                for c in range(KC):
                    for m in range(2):
                        ins = mm(psf[:, 3072 + c * P:3072 + (c + 1) * P], m_v[:, m, c * P:(c + 1) * P],
                                 x_t[:, e, 2 * (c // 2) + m, :], start=(m == 0), stop=(m == 1))
                ins.then_inc(xa["o"], 1)

            pe.wait_ge(*freed(f"xq{l}", 2))
            with pe.Fori(0, 4) as r:
                scores(r, 0)
                scores(r, 1)
                rest(r, 0)
                rest(r, 1)
            pe.wait_ge(xa["oc"], 8 * l + 10)
            with pe.Fori(0, NB) as b:
                pe.wait_ge(xa["col"], b + (8 * l + 1))
                for c in range(KC):
                    ins = mm(psf[:, c * P:(c + 1) * P], r_col[:, c:c + 1].to_broadcast([P, P]), ident[:], start=True, stop=True)
                ins.then_inc(xa["qb"], 1)
            pe.wait_ge(xa["mx"], l + 1)
            nc.tensor.transpose(ps[0:32, 2, 0:P], r_mx.rearrange("p b h -> p (b h)"), ident[:]).then_inc(xa["mt"], 1)
            pe.wait_ge(xa["mc"], l + 1)
            mm(ps[:, 3, 0:32], r_mc[0:32, :].to_broadcast([32, P]), ident[0:32, 0:32], start=True, stop=True)\
                .then_inc(xa["mb"], 1)
            pe.wait_ge(xa["sum"], l + 1)
            mm(ps[:, 2, 128:160], ones[:], r_sum.rearrange("p b h -> p (b h)"), start=True, stop=True).then_inc(xa["tot"], 1)
            pe.wait_ge(xa["pr"], l + 1)
            with pe.Fori(0, NB // 2) as r:
                for s in range(2):
                    pe.wait_ge(xa[f"vr{s}"], r * 16 + 16 * (4 * l + 1))
                    pe.wait_ge(xa["pvc"], r * 2 + (8 * l + s + 1))
                    for c in range(KC):
                        for m in range(2):
                            ins = mm(ps[:, 4 + s, c:c + 1], x_ring[:, s, m, c * P:(c + 1) * P],
                                     r_sc[:, ds(r * 2 + s, 1), m, c // 2:c // 2 + 1].rearrange("p a h -> p (a h)"),
                                     start=(m == 0), stop=(m == 1))
                    ins.then_inc(xa["pv"], 1)
            pe.wait_ge(xa["pvc"], 8 * l + 2 + NB)

        def act_cross(act, l):
            if l == 0:
                for k, n in (("e", 2), ("tc", 1), ("oc", 2), ("pvc", 2)):
                    act.sem_inc(xa[k], n)
            with act.Fori(0, 4) as r:
                for e in range(2):
                    act.wait_ge(xa["m"], r * 2 + (8 * l + e + 1))
                    for h in range(HX):
                        ins = nc.scalar.activation(x_p[:, e, h, :], psf[:, e * 1024 + h * 256:e * 1024 + h * 256 + 256],
                                                   ACT.Exp, bias=x_st[:, e, 0, h:h + 1], accum_out=x_st[:, e, 1, h:h + 1])
                    ins.then_inc(xa["e"], 1)
                for e in range(2):
                    act.wait_ge(xa["t"], r * 2 + (8 * l + e + 1))
                    nc.scalar.activation(x_t[:, e], psf[:, 2048:3072].rearrange("p (a n) -> p a n", n=P), ACT.Copy)\
                        .then_inc(xa["tc"], 1)
                    act.wait_ge(xa["o"], r * 2 + (8 * l + e + 1))
                    nc.scalar.activation(hT[:, :, ds(r * 256 + e * P, P)], psf[:, 3072:4096].rearrange("p (c n) -> p c n", n=P),
                                         ACT.Copy).then_inc(xa["oc"], 1)
            with act.Fori(0, NB) as b:
                act.wait_ge(xa["qbc"], b + (8 * l + 1))
                nc.scalar.activation(r_col, aT[:, :, ds(b + SEQ, 1)].rearrange("p c a -> p (c a)"), ACT.Copy)\
                    .then_inc(xa["col"], 1)
                act.wait_ge(xa["qb"], b + (8 * l + 1))
                nc.scalar.activation(r_qb, psf[:, 0:D], ACT.Copy).then_inc(xa["q"], 1)
            act.wait_ge(xa["sh"], l + 1)
            nc.scalar.activation(r_sc, r_sc, ACT.Exp).then_inc(xa["ex"], 1)
            with act.Fori(0, NB // 2) as r:
                for s in range(2):
                    act.wait_ge(xa["pv"], r * 2 + (8 * l + s + 1))
                    nc.scalar.activation(hT[:, :, ds(r * 2 + (SEQ + s), 1)].rearrange("p c a -> p (c a)"),
                                         ps[:, 4 + s, 0:KC], ACT.Copy).then_inc(xa["pvc"], 1)

        def dve_cross(dve, l):
            vv = nc.vector
            with S["dve"].loop(4, 2) as r:
                link = S["dve"].link
                for e in range(2):
                    dve.wait_ge(xa["s"], r * 2 + (8 * l + e + 1))
                    vv.tensor_reduce(x_st[:, e, 0, :], psf[:, e * 1024:e * 1024 + 1024].rearrange("p (h n) -> p h n", h=HX),
                                     AX.X, ALU.max, negate=True).then_inc(xa["m"], 1)
                for e in range(2):
                    dve.wait_ge(xa["e"], r * 2 + (8 * l + e + 3))
                    link(vv.reciprocal(x_st[:, e, 2, :], x_st[:, e, 1, :]))
                    rs = x_st[:, e, 2, :].rearrange("p (h n) -> p h n", n=1).to_broadcast([P, HX, NMEM])
                    vv.tensor_tensor(x_p[:, e], x_p[:, e], rs, ALU.mult).then_inc(xa["p"], 1)
            link = S["dve"].link
            dve.wait_ge(xa["oc"], 8 * l + 10)
            if l == 0:
                dve.sem_inc(xa["qbc"], 1)
                dve.sem_inc(xa["free"], 2)
            with S["dve"].loop(NB // 2, 2) as r:
                link = S["dve"].link
                for s in range(2):
                    dve.wait_ge(xa["q"], r * 2 + (8 * l + s + 1))
                    dve.wait_ge(xa[f"ring{s}"], r * 16 + 16 * (4 * l + 1))
                    dve.wait_ge(xa["qbc"], r * 2 + (8 * l + s + 1))
                    link(vv.tensor_tensor(r_prod, x_ring[:, s], r_qb.rearrange("p (a n) -> p a n", a=1).to_broadcast([P, 2, D]),
                                          ALU.mult))
                    dve.sem_inc(xa["free"], 1)
                    vv.tensor_reduce(r_sc[:, ds(r * 2 + s, 1), :, :].rearrange("p a m h -> p (a m h)"),
                                     r_prod.rearrange("p m (h n) -> p (m h) n", n=DHX), AX.X, ALU.add).then_inc(xa["qbc"], 1)
            link = S["dve"].link
            dve.wait_ge(xa["qbc"], 8 * l + 9)
            vv.tensor_reduce(r_mx, r_sc.rearrange("p b m h -> p b h m"), AX.X, ALU.max).then_inc(xa["mx"], 1)
            dve.wait_ge(xa["mt"], l + 1)
            vv.tensor_reduce(r_mc[0:32, :], ps[0:32, 2, 0:P], AX.X, ALU.max).then_inc(xa["mc"], 1)
            dve.wait_ge(xa["mb"], l + 1)
            link(vv.tensor_copy(r_mb, ps[:, 3, 0:32].rearrange("p (b h) -> p b h", h=HX)))

            def over_mem(x):
                return x.rearrange("p b (a h) -> p b a h", a=1).to_broadcast([P, NB, 2, HX])

            vv.tensor_tensor(r_sc, r_sc, over_mem(r_mb), ALU.subtract).then_inc(xa["sh"], 1)
            dve.wait_ge(xa["ex"], l + 1)
            vv.tensor_reduce(r_sum, r_sc.rearrange("p b m h -> p b h m"), AX.X, ALU.add).then_inc(xa["sum"], 1)
            dve.wait_ge(xa["tot"], l + 1)
            link(vv.reciprocal(r_rs, ps[:, 2, 128:160].rearrange("p (b h) -> p b h", h=HX)))
            vv.tensor_tensor(r_sc, r_sc, over_mem(r_rs), ALU.mult).then_inc(xa["pr"], 1)
            with dve.Fori(0, NB) as b:
                dve.wait_ge(xa["pv"], b + (8 * l + 1))
                dve.sem_inc(xa["free"], 1)

        ff_sq = sem("ff_sq")

        def act_up(act, l, g):
            name = f"up{l}{g}"
            g0 = GROUP0[name]
            n0 = 8 * (FF_GROUPS * l + g)
            act.wait_ge(psum_free, g0)
            with act.Fori(0, 2) as i:
                for j in range(4):
                    act.wait_ge(psum_ready, i * 4 + (g0 + j + 1))
                    nc.scalar.activation(at_chunk(aT, i * 4 + j), psum_set((g0 + j) % 2), ACT.Relu).then_inc(psum_free, 1)

        def dve_up(dve, l, g):
            g0 = GROUP0[f"up{l}{g}"]
            with dve.Fori(0, 2) as i:
                for j in range(4):
                    dve.wait_ge(psum_free, i * 4 + (g0 + j + 1))
                    nc.vector.tensor_tensor(at_chunk(aT, i * 4 + j), at_chunk(aT, i * 4 + j), at_chunk(aT, i * 4 + j),
                                            ALU.mult).then_inc(ff_sq, 1)

        def pe_mlp(pe, l):
            for g in range(FF_GROUPS):
                pe_product(pe, f"up{l}{g}", 2, hT, T, after((nm_out, 8 * (F_NORM[l] + 1))))
                pe_product(pe, f"down{l}{g}", 2, aT, T, after((ff_sq, 8 * (FF_GROUPS * l + g + 1))))

        F_NORM = (3, 8)

        cm = {n: sem("cm_" + n) for n in ("pad", "st", "glu", "sg", "out", "sum", "ps", "mean", "bc", "cp", "xc", "silu")}
        GW = CC - 1 + T
        glu = part(bigf, 0, KC, GW)
        d_sg = part(wk, 0, 2, T)
        d_st = part(wk, 2 * T, KC, NB, CC - 1)
        d_tmp = part(wk, 4100, NB, CC - 1)
        d_s8 = part(wk, 4400, NB)

        def pool_conformer(pool):
            pool.wait_ge(*freed("xo0", 2))
            nc.gpsimd.memset(glu[:, :, 0:CC - 1], 0.0).then_inc(cm["pad"], 1)
            pool.wait_ge(nm_out, 40)
            pool.dma_start(d_st, st_cconv_in).then_inc(cm["st"], 16)

        def act_pw1(act):
            g0 = GROUP0["pw1"]
            b0 = VOFF["b_pw1"][0]
            act.wait_ge(psum_free, g0)
            act.wait_ge(cm["pad"], 1)
            act.wait_ge(nm_out, 40)
            with act.Fori(0, 4) as i:
                for j in range(4):
                    act.wait_ge(psum_ready, i * 4 + (g0 + j + 1))
                    if j < 2:
                        nc.scalar.activation(thirds(glu[:, ds(i * 2 + j, 1), CC - 1:].rearrange("p a n -> p (a n)")),
                                             psum_set((g0 + j) % 2), ACT.Identity, bias=vec[:, ds(i * 2 + (b0 + j), 1)])\
                            .then_inc(psum_free, 1)
                    else:
                        act.wait_ge(cm["glu"], i * 2 + (j - 1))
                        nc.scalar.activation(thirds(d_sg[:, j - 2, :]), psum_set((g0 + j) % 2), ACT.Sigmoid,
                                             bias=vec[:, ds(i * 2 + (b0 + 8 + j - 2), 1)]).then_inc(psum_free, 1)

        def dve_conformer(dve):
            vv, g0 = nc.vector, GROUP0["pw1"]
            w0, bd = VOFF["w_dw"][0], VOFF["b_dw"][0]
            dve.sem_inc(cm["glu"], 2)
            dve.wait_ge(cm["st"], 16)
            with S["dve"].loop(4, 2 * 34) as i:
                link = S["dve"].link
                for j in range(2):
                    c = i * 2 + j
                    dve.wait_ge(psum_free, i * 4 + (g0 + j + 3))
                    x = glu[:, ds(c, 1), :].rearrange("p a n -> p (a n)")
                    vv.tensor_tensor(x[:, CC - 1:], x[:, CC - 1:], d_sg[:, j, :], ALU.mult).then_inc(cm["glu"], 1)
                    dve.wait_ge(cm["glu"], i * 2 + (j + 3))
                    y = aT[:, ds(c, 1), :].rearrange("p a n -> p (a n)")

                    def tap(t):
                        return vec[:, ds(c * CC + (w0 + t), 1)]

                    bias = vec[:, ds(c + bd, 1)]
                    wrow = vec[:, ds(c * CC + w0, CC - 1)].rearrange("p (a n) -> p a n", a=1).to_broadcast([P, NB, CC - 1])
                    link(vv.tensor_tensor(d_tmp, d_st[:, ds(c, 1)].rearrange("p a b n -> p (a b) n"), wrow, ALU.mult))
                    link(vv.tensor_reduce(d_s8, d_tmp, AX.X, ALU.add))
                    link(vv.scalar_tensor_tensor(out=d_s8, in0=x[:, CC - 1 + SEQ:], scalar=tap(CC - 1), in1=d_s8,
                                                 op0=ALU.mult, op1=ALU.add))
                    link(vv.tensor_scalar(y[:, SEQ:T], d_s8, bias, None, ALU.add))
                    link(vv.tensor_scalar(y[:, 0:SEQ], x[:, 0:SEQ], tap(0), bias, ALU.mult, ALU.add))
                    for t in range(1, CC):
                        ins = vv.scalar_tensor_tensor(out=y[:, 0:SEQ], in0=x[:, t:t + SEQ], scalar=tap(t), in1=y[:, 0:SEQ],
                                                      op0=ALU.mult, op1=ALU.add)
                        if t < CC - 1:
                            link(ins)
                    ins.then_inc(cm["out"], 1)
            link = S["dve"].link
            dve.wait_ge(cm["out"], 8)
            link(vv.tensor_tensor(acc, aT[:, 0, :], aT[:, 1, :], ALU.add))
            for c in range(2, KC):
                ins = vv.tensor_tensor(acc, acc, aT[:, c, :], ALU.add)
                if c < KC - 1:
                    link(ins)
            ins.then_inc(cm["sum"], 1)
            dve.wait_ge(cm["cp"], 1)
            for c in range(KC):
                vv.tensor_tensor(aT[:, c, :], aT[:, c, :], rbc, ALU.subtract).then_inc(cm["xc"], 1)

        def pe_mean(pe):
            pe.wait_ge(cm["sum"], 1)
            tl = tiles_of(T)
            for j, (at, cnt, skip, _) in enumerate(tl):
                ins = nc.tensor.matmul(ps[:, 6, j:j + 1], acc[:, at:at + P], ones[:, 0:1], start=True, stop=True)
            ins.then_inc(cm["ps"], 1)
            pe.wait_ge(cm["mean"], 1)
            for j, (at, cnt, skip, to) in enumerate(tl):
                ins = nc.tensor.matmul(psf[:, to:to + cnt], sm[:, j:j + 1].to_broadcast([P, P]), ident[:, skip:skip + cnt],
                                       start=True, stop=True)
            ins.then_inc(cm["bc"], 1)

        def act_mean(act):
            act.wait_ge(cm["ps"], 1)
            nc.scalar.activation(sm[:, 0:9], ps[:, 6, 0:9], ACT.Copy, scale=1.0 / D).then_inc(cm["mean"], 1)
            act.wait_ge(cm["bc"], 1)
            nc.scalar.activation(rbc, psf[:, 0:T], ACT.Copy).then_inc(cm["cp"], 1)

        def act_swish(act):
            for c in range(KC):
                act.wait_ge(nm_out, 40 + c + 1)
                nc.scalar.activation(hT[:, c, :], hT[:, c, :], ACT.Silu, bias=v("ln_b", c)).then_inc(cm["silu"], 1)

        copy_to = lambda dst, scale=1.0: (lambda i, j, st: nc.scalar.activation(at_chunk(dst, i * 4 + j), psum_set(st),
                                                                             ACT.Copy, scale=scale))

        def act_memory(act, l):
            act.wait_ge(psum_free, GROUP0[f"mk{l}"])
            epilogue(act, f"mk{l}", 2, lambda i, j, st: nc.scalar.activation(
                m_k[:, ds(i * 4 + j, 1), :].rearrange("p a n -> p (a n)"), ps[:, 3 * st, 0:NMEM], ACT.Copy))
            epilogue(act, f"mv{l}", 2, lambda i, j, st: nc.scalar.activation(
                m_v[:, j % 2, ds(i * 512 + (j // 2) * 256, 256)], ps[:, 3 * st, 0:256], ACT.Copy))

        M_NORM, X_NORM = (1, 6), (2, 7)
        block = ctx.enter_context(nc.Block())

        @block.sync
        def _(sp):
            sp_loads(sp)

        @block.gpsimd
        def _(pool):
            S["pool"] = Steps(pool, pool_steps)
            pool_consts(pool)
            pool_fox(pool)
            store(pool, fkT.rearrange("(c p) t -> p c t", p=P), kf)
            store(pool, fv[0:SEQ, :].rearrange("(t p) n -> p t n", p=P), vf)
            store(pool, fv[SEQ:T, :], vs)
            store(pool, flf[0:SEQ, :].rearrange("(t p) n -> p t n", p=P), lf[:, 0:QT, :])
            store(pool, flf[SEQ:T, :], lf[P - NB:P, QT, :])
            pool_fox_rows(pool)
            store(pool, gkeep, st_gconv_in.rearrange("p c j b -> p c (j b)")[:, :, NB:])
            store(pool, ckeep.rearrange("p c (b j) -> p c b j", b=NB), st_cconv_in[:, :, :, 1:])
            pool_conv(pool)
            pool.wait_ge(conv_silu, 12)
            store(pool, gconv, c_tail)
            pool_gdn(pool)
            pool_gdn_rows(pool)
            pool.wait_ge(gs["out"], 1)
            store(pool, gdn_s, st.rearrange("p b h n -> p (b h) n"))
            pool.wait_ge(gn["u"], 4)
            pool_cross(pool, 0, 1)
            pool_conformer(pool)
            pool.wait_ge(cm["out"], 8)
            store(pool, cconv, glu[:, :, GW - (CC - 1) - NB:GW])
            pool.wait_ge(stored, 16 * n_stored[0])
            pool_cross(pool, 1, 6)
            pool.wait_ge(nm_out, 80)
            store(pool, yT.rearrange("p (c t) -> p c t", c=KC), hT[:])
            pool.wait_ge(stored, 16 * n_stored[0])

        @block.scalar
        def _(act):
            S["act"] = Steps(act, act_steps)
            act.wait_ge(consts_ready, 1)
            act_norm(act, 0, xT, T, after((in_loaded, 80)))
            act_values(act)
            epilogue(act, "k_fox", 1, copy_to(kf))
            epilogue(act, "q_fox", 1, copy_to(qf, float(DHB) ** -0.5))
            act_gates(act)
            act_fox(act)
            act_fox_rows(act)
            act_conv(act)
            epilogue(act, "z", 1, lambda i, j, st: nc.scalar.activation(at_chunk(aT, i * 4 + j), psum_set(st), ACT.Silu))
            act_squares(act, big, 8, 1.0)
            act_gdn(act)
            l2_n[0] = 8
            act.wait_ge(gs["vn"], 1)
            act_squares(act, big[:, 8:12, :], HA, 1.0 / P)

            def cross(l):
                act_norm(act, M_NORM[l], m_raw, NMEM, after((xa["mem"], 16 * (l + 1))))
                act_memory(act, l)
                act_norm(act, X_NORM[l], xT, T, after())
                epilogue(act, f"xq{l}", 2, copy_to(aT, float(DHX) ** -0.5))
                act_cross(act, l)

            def mlp(l):
                act_norm(act, F_NORM[l], xT, T, after(freed(f"xo{l}", 2)))
                for g in range(FF_GROUPS):
                    act_up(act, l, g)

            cross(0)
            mlp(0)
            act_norm(act, 4, xT, T, after(freed("down03", 2)))
            act_pw1(act)
            act_mean(act)
            act_norm(act, 5, aT, T, after((cm["xc"], 8)))
            act_swish(act)
            cross(1)
            mlp(1)
            act_norm(act, 9, xT, T, after(freed("down13", 2)))

        @block.vector
        def _(dve):
            S["dve"] = Steps(dve, dve_steps)
            dve.wait_ge(consts_ready, 1)
            dve_norm(dve, 0, xT, hT, T, "norm_mix0")
            dve_gates(dve)
            dve_fox(dve)
            dve_fox_rows(dve)
            dve_conv(dve)
            dve_norm_gates(dve)
            dve_gdn(dve)
            dve_gdn_rows(dve)
            dve_head_norm(dve)

            def cross(l):
                residual(dve, ("out", "pw2")[l], 2)
                dve_norm(dve, M_NORM[l], m_raw, m_n, NMEM, f"norm_mem{l}")
                dve_norm(dve, X_NORM[l], xT, hT, T, f"norm_x{l}")
                dve_cross(dve, l)
                residual(dve, f"xo{l}", 2)

            def mlp(l):
                dve_norm(dve, F_NORM[l], xT, hT, T, f"norm_f{l}")
                for g in range(FF_GROUPS):
                    dve_up(dve, l, g)
                    residual(dve, f"down{l}{g}", 2)

            cross(0)
            mlp(0)
            dve_norm(dve, 4, xT, hT, T, "norm_mix1")
            dve_conformer(dve)
            dve_norm(dve, 5, aT, hT, T, "ln_g")
            cross(1)
            mlp(1)
            dve_norm(dve, 9, xT, hT, T, "norm_out")

        @block.tensor
        def _(pe):
            pe.wait_ge(consts_ready, 1)
            pe_norm(pe, 0, T)
            pe_values(pe)
            pe_product(pe, "k_fox", 1, hT, T, after())
            pe_product(pe, "q_fox", 1, hT, T, after())
            pe_gates(pe)
            pe_fox(pe)
            pe_fox_rows(pe)
            pe_product(pe, "conv", 3, hT, T, after((fs["pvc"], 2 + NB)))
            pe_product(pe, "z", 1, hT, T, after())
            pe_squares(pe, 0, 8)
            pe_gdn(pe)
            pe_gdn_rows(pe)
            pe_head_norm(pe)
            pe_product(pe, "out", 2, aT, T, after((gn["u"], HA), (fs["out"], 2)))

            def cross(l):
                pe_norm(pe, M_NORM[l], NMEM)
                pe_product(pe, f"mk{l}", 2, m_n, NMEM, after((nm_out, 8 * (M_NORM[l] + 1))))
                pe_mem_values(pe, l)
                pe.wait_ge(*freed(f"mv{l}", 2))
                pe_norm(pe, X_NORM[l], T)
                pe_product(pe, f"xq{l}", 2, hT, T, after((nm_out, 8 * (X_NORM[l] + 1))))
                pe_cross(pe, l)
                pe_product(pe, f"xo{l}", 2, hT, T, after())
                pe_norm(pe, F_NORM[l], T)

            cross(0)
            pe_mlp(pe, 0)
            pe_norm(pe, 4, T)
            pe_product(pe, "pw1", 4, hT, T, after((nm_out, 40)))
            pe_mean(pe)
            pe_norm(pe, 5, T)
            pe_product(pe, "pw2", 2, hT, T, after((cm["silu"], 8)))
            cross(1)
            pe_mlp(pe, 1)
            pe_norm(pe, 9, T)


def kernel(**inputs):
    import numpy as np
    import concourse.bacc as bacc
    from concourse.bass_utils import run_bass_kernel_spmd

    a = {k: np.asarray(x) for k, x in inputs.items()}

    def cols(x, c):
        return x.reshape(c, P).T

    def featmajor(x):
        return x.T.reshape(-1, P, x.shape[0]).transpose(1, 0, 2)

    def tiles(wm):
        n = wm.shape[1] // 256
        return wm.reshape(KC, P, n, 256).transpose(2, 1, 0, 3).reshape(n, P, KC * 256)

    def rows(x):
        return np.broadcast_to(x[None, :], (P, x.shape[0]))

    w_in = a["w_in_e"][0]
    o_z, o_a, o_b, o_q, o_k, o_v, o_f = 1536, 2048, 2052, 2056, 2568, 3080, 3592
    gates = w_in[:, list(range(o_a, o_q)) + list(range(o_f, o_f + HB))]
    z4, z8 = np.zeros(4, np.float32), np.zeros(8, np.float32)
    vecs = np.concatenate(
        [cols(a[n][l], 8) for n in ("norm_mix", "norm_x", "norm_f", "norm_mem") for l in range(2)]
        + [cols(a["norm_out"], 8), cols(a["b_pw1"][0], 16)] + [cols(a[n][0], 8) for n in ("b_dw", "ln_g", "ln_b")]
        + [a["gnorm_a"][0][:, None], a["conv_a"][0].reshape(CA, 12, P).transpose(2, 1, 0).reshape(P, 48),
           a["w_dw"][0].reshape(CC, KC, P).transpose(2, 1, 0).reshape(P, KC * CC),
           rows(np.concatenate([a["dt_bias"][0], z4, a["b_f"][0]])), rows(np.concatenate([a["a_log"][0], z4, z8]))], axis=1)
    pw1 = tiles(a["w_pw1"][0])
    stream = [tiles(w_in[:, o_v:o_v + 512]), tiles(w_in[:, o_k:o_k + 512]), tiles(w_in[:, o_q:o_q + 512]),
              tiles(w_in[:, :1536]), tiles(w_in[:, o_z:o_z + 512]), tiles(a["w_out_e"][0])]
    for l in range(2):
        if l:
            stream += [np.stack([pw1[:4], pw1[4:]], 1).reshape(pw1.shape), tiles(a["w_pw2"][0])]
        stream += [tiles(a["w_xkv"][l]), tiles(a["w_xq"][l]), tiles(a["w_xo"][l])]
        for g in range(FF_GROUPS):
            stream += [tiles(a["w_up"][l][:, g * D:g * D + D]), tiles(a["w_down"][l][g * D:g * D + D])]
    arrays = {
        "xT_in": np.concatenate([featmajor(a["x_prompt"][0]), featmajor(a["x_sample"][:, 0])], axis=2),
        "memT_in": featmajor(a["mem_prompt"][0]),
        "vecs_in": vecs,
        "wall": np.concatenate(stream, axis=0),
        "wgate_in": gates.reshape(KC, P, 16).transpose(1, 0, 2),
        "st_gconv_in": a["state_gdn_conv"][0].transpose(2, 1, 0).reshape(12, P, 3, NB).transpose(1, 0, 2, 3),
        "st_cconv_in": a["state_cfm_conv"][0].transpose(2, 0, 1).reshape(KC, P, NB, CC - 1).transpose(1, 0, 2, 3),
        "pages_in": a["page_table"].reshape(1, NB * NPG),
        "kpool": a["cache_fox_k"][0].reshape(-1, PAGE, 512),
        "vpool": a["cache_fox_v"][0].reshape(-1, PAGE, 512),
        "fpool": a["cache_fox_logf"][0],
        "st_gdn": a["state_gdn"][0],
        "cmk": a["cache_mem_k"].reshape(2, NB, NMEM, D),
        "cmv": a["cache_mem_v"].reshape(2, NB, NMEM, D),
    }
    outs = {"yT": (P, KC * T), "fkT": (512, T), "fv": (T, 512), "flf": (T, HB), "gdn_p": (P, HA, P),
            "gconv": (P, 12, 3 + NB), "gkeep": (P, 12, 2 * NB), "gdn_s": (P, NB * HA, P), "cconv": (P, KC, 30 + NB), "ckeep": (P, KC, NB * 29),
            "mkT": (2, D, NMEM), "mv": (2, NMEM, D)}
    nc = bacc.Bacc("TRN2", target_bir_lowering=False, num_devices=1)
    arrays = {k: np.ascontiguousarray(x) for k, x in arrays.items()}
    args = {k: nc.dram_tensor(k, x.shape, mybir.dt.from_np(x.dtype), kind="ExternalInput").ap() for k, x in arrays.items()}
    args.update({k: nc.dram_tensor(k, s, F32, kind="ExternalOutput").ap() for k, s in outs.items()})
    build(nc, **args)
    r = run_bass_kernel_spmd(nc, [arrays], core_ids=[0]).results[0]

    y = r["yT"].reshape(P, KC, T).transpose(2, 1, 0).reshape(T, D)
    fk = r["fkT"].T.reshape(T, HB, DHB)
    fv_ = r["fv"].reshape(T, HB, DHB)
    gconv = r["gconv"].transpose(2, 1, 0).reshape(3 + NB, 12 * P)
    cconv = r["cconv"].transpose(2, 1, 0).reshape(30 + NB, D)
    gkeep = r["gkeep"].reshape(P, 12, 2, NB).transpose(3, 2, 1, 0).reshape(NB, 2, 12 * P)
    ckeep = r["ckeep"].reshape(P, KC, NB, 29).transpose(2, 3, 1, 0).reshape(NB, 29, D)
    return (y[:SEQ][None], y[SEQ:][:, None], fk[:SEQ][None, None], fv_[:SEQ][None, None], r["flf"][:SEQ][None, None],
            fk[SEQ:][None, :, None], fv_[SEQ:][None, :, None], r["flf"][SEQ:][None, :, None],
            r["gdn_p"].transpose(1, 0, 2)[None, None], gconv[None, None, :3],
            r["gdn_s"].reshape(P, NB, HA, P).transpose(1, 2, 0, 3)[None], np.concatenate([gkeep, gconv[3:][:, None]], axis=1)[None],
            cconv[None, None, :30], np.concatenate([ckeep, cconv[30:][:, None]], axis=1)[None],
            r["mkT"].transpose(0, 2, 1).reshape(2, 1, NMEM, HX, DHX), r["mv"].reshape(2, 1, NMEM, HX, DHX))
```

```python
from contextlib import ExitStack, contextmanager

import concourse.bass as bass
from concourse import mybir

P = 128
D = 1024
KC = D // P
SEQ, NB = 1024, 8
T = SEQ + NB
N3 = T // 3
QT = SEQ // P
PAST, PAGE = 2048, 128
NPG = PAST // PAGE
HA, HB, DHB = 4, 8, 64
HX, DHX, NMEM = 4, 256, 256
CA, CC = 4, 31
EPS = 1e-6
NEG = -1e30
FF_GROUPS = 4
ARENA = 5 * KC * T + 2688 + 6144
ARENA_BYTE = 16512

F32 = mybir.dt.float32
F32R = mybir.dt.float32r
I32 = mybir.dt.int32
ACT = mybir.ActivationFunctionType
ALU = mybir.AluOpType
AX = mybir.AxisListType
ds = bass.ds

VECS = [("norm_mix0", 8), ("norm_mix1", 8), ("norm_x0", 8), ("norm_x1", 8), ("norm_f0", 8), ("norm_f1", 8),
        ("norm_mem0", 8), ("norm_mem1", 8), ("norm_out", 8), ("b_pw1", 16), ("b_dw", 8), ("ln_g", 8), ("ln_b", 8),
        ("gnorm", 1), ("conv_a", 48), ("w_dw", 248), ("gate_bias", 16), ("gate_alog", 16)]
VOFF, _o = {}, 0
for _n, _w in VECS:
    VOFF[_n] = (_o, _w)
    _o += _w
NVEC = _o

STREAM = [("v_fox", 1), ("k_fox", 1), ("q_fox", 1), ("conv", 3), ("z", 1)]
PAIR0, GROUP0, _p, _g = {}, {}, 0, 0
for _n, _w in STREAM:
    PAIR0[_n], GROUP0[_n] = _p, _g
    _p += _w
    _g += 18 if _n == "v_fox" else 4 * _w
NPAIRS = _p
G_V = 18
STREAM_B = [("out", 8)]
for _l in range(2):
    if _l == 1:
        STREAM_B += [("pw1", 16), ("pw2", 8)]
    STREAM_B += [(f"mk{_l}", 8), (f"mv{_l}", 8), (f"xq{_l}", 8), (f"xo{_l}", 8)]
    for _g2 in range(FF_GROUPS):
        STREAM_B += [(f"up{_l}{_g2}", 8), (f"down{_l}{_g2}", 8)]
GROUPS_A, TILE0, _t = _g, {}, 0
for _n, _w in STREAM_B:
    TILE0[_n], GROUP0[_n] = _t, GROUPS_A + _t
    _t += _w
NTILES = _t


class Steps:

    def __init__(self, eng, sem):
        self.eng, self.sem, self.n, self.at = eng, sem, 0, None

    def link(self, ins):
        self.n += 1
        ins.then_inc(self.sem, 1)
        self.eng.wait_ge(self.sem, self.n if self.at is None else self.at + self.n)

    @contextmanager
    def loop(self, trips, per):
        entry = self.n
        with self.eng.Fori(0, trips) as i:
            self.at, self.n = i * per + entry, 0
            yield i
            assert self.n == per, f"{self.n} linked steps in a round, not {per}"
        self.at, self.n = None, entry + trips * per


def build(nc, xT_in, memT_in, vecs_in, wall, wallb, wgate_in, st_gconv_in, st_cconv_in, pages_in, kpool, vpool, fpool, st_gdn,
          cmk, cmv, yT, fkT, fv, flf, gdn_p, gconv, gkeep, gdn_s, cconv, ckeep, mkT, mv):
    ctx = ExitStack()
    with ctx:
        def sb(name, shape, dt=F32):
            return ctx.enter_context(nc.sbuf_tensor(name, shape, dt))

        def sem(name):
            return ctx.enter_context(nc.semaphore(name))

        sb("arena", [P, ARENA + 8])

        def at(name, offset, shape, dt=F32):
            return nc.alloc_sbuf_tensor_at(name, shape, dt, offset=ARENA_BYTE + 4 * offset)

        XW = KC * T
        xT = at("xT", 0, [P, KC, T])
        aT = at("aT", XW, [P, KC, T])
        big = at("big", 2 * XW, [P, 12, T])
        hT = at("hT", 2 * XW + 12 * T, [P, KC, T])
        wk = at("wk", 3 * XW + 12 * T, [P, 8850])
        w = at("w", ARENA - 4096, [P, 2, KC, 256])
        a_hi = at("a_hi", XW, [P, KC, T], F32R)
        a_lo = at("a_lo", 2 * XW, [P, KC, T], F32R)
        h_hi = at("h_hi", ARENA - 6144 - 2 * XW, [P, KC, T], F32R)
        h_lo = at("h_lo", ARENA - 6144 - XW, [P, KC, T], F32R)
        y_out = at("y_out", ARENA - 6144 - 2 * XW, [P, KC, T])
        w_hi = at("w_hi", ARENA - 6144, [P, 2, KC, P], F32R)
        w_lo = at("w_lo", ARENA - 4096, [P, 2, KC, P], F32R)
        w_raw = at("w_raw", ARENA - 2048, [P, 2, KC, P])
        la = at("la", XW, [P, 2 * XW + 2688])
        vec = sb("vec", [P, NVEC])
        ident = sb("ident", [P, P])
        ones = sb("ones", [P, P])
        upper = sb("upper", [P, P])
        later = sb("later", [P, P])
        strict = sb("strict", [P, P])
        neg_qk = sb("neg_qk", [P, P])
        neg_ji = sb("neg_ji", [P, P])
        lev = sb("lev", [P, 7, P])
        page_later = sb("page_later", [P, P])
        lev0T = sb("lev0T", [P, P])
        gt = sb("gt", [P, 9, 11, 4])
        lf = sb("lf", [P, 9, 8])
        cf = wk[:, 5400:5464].rearrange("p (t h) -> p t h", h=8)
        small = sb("small", [P, 56])
        sm = small[:, 0:32]
        gcoef = small[:, 32:48]
        eps = small[:, 48:49]
        pages = wk[0:1, 8550:8550 + NB * NPG].bitcast(I32)
        pagec = small[:, 49:50].bitcast(I32)
        ps = ctx.enter_context(nc.psum_tensor("ps", [P, 8, 512], F32))

        def v(name, c=0, n=1):
            return vec[:, VOFF[name][0] + c:VOFF[name][0] + c + n]

        def part(buf, off, *shape):
            n = 1
            for s in shape:
                n *= s
            flat = buf[:, off:off + n]
            if len(shape) == 1:
                return flat
            names = "abcd"[:len(shape)]
            return flat.rearrange(f"p ({' '.join(names)}) -> p {' '.join(names)}",
                                  **{a: s for a, s in zip(names[1:], shape[1:])})

        bigf = big[:, :, :].rearrange("p a b -> p (a b)")
        hTf = hT[:, :, :].rearrange("p a b -> p (a b)")
        aTf = aT[:, :, :].rearrange("p a b -> p (a b)")
        psf = ps[:, :, :].rearrange("p a b -> p (a b)")

        def thirds(ap):
            return ap.rearrange("p (a n) -> p a n", a=3)

        def psum_set(s):
            return ps[:, 3 * s:3 * s + 3, 0:N3]

        in_loaded = sem("in_loaded")
        w_loaded = [sem("w_loaded0"), sem("w_loaded1")]
        consts_ready = sem("consts_ready")
        psum_ready = sem("psum_ready")
        psum_free = sem("psum_free")
        stored = sem("stored")
        act_steps, dve_steps, pool_steps = sem("act_steps"), sem("dve_steps"), sem("pool_steps")
        nm_sq, nm_add, nm_sum, nm_rt, nm_rc, nm_bc, nm_cp, nm_out, nm_t, nm_hi = (sem("nm_" + n) for n in (
            "sq", "add", "sum", "rt", "rc", "bc", "cp", "out", "t", "hi"))
        w_split = sem("w_split")
        n_stored = [0]

        S = {}

        def pool_consts(pool):
            link = S["pool"].link
            g = nc.gpsimd
            link(g.memset(ident[:], 0.0))
            link(g.affine_select(out=ident[:], in_=ident[:], compare_op=ALU.not_equal, fill=1.0, base=0,
                                 pattern=[[-1, P]], channel_multiplier=1))
            for m, start, op, fill, step in ((upper, 1.0, ALU.is_ge, 0.0, 1), (later, 1.0, ALU.is_gt, 0.0, -1),
                                             (strict, 1.0, ALU.is_gt, 0.0, 1), (neg_qk, 0.0, ALU.is_ge, NEG, -1),
                                             (neg_ji, 0.0, ALU.is_ge, NEG, 1)):
                link(g.memset(m[:], start))
                link(g.affine_select(out=m[:], in_=m[:], compare_op=op, fill=fill, base=0, pattern=[[step, P]],
                                     channel_multiplier=-step))
            link(g.memset(lev[:], 0.0))
            link(g.memset(lev0T[:], 0.0))
            for s in range(7):
                b = 1 << s
                half = lev[:, s, :].rearrange("p (k t r) -> p k t r", t=2, r=b)[:, :, 0, :]
                link(g.memset(half, 1.0))
                link(g.affine_select(out=half, in_=half, compare_op=ALU.is_ge, fill=0.0, base=-b,
                                     pattern=[[-2 * b, P // (2 * b)], [0, b]], channel_multiplier=1))
                link(g.affine_select(out=half, in_=half, compare_op=ALU.is_ge, fill=0.0, base=2 * b - 1,
                                     pattern=[[2 * b, P // (2 * b)], [0, b]], channel_multiplier=-1))
            odd = lev0T[:, :].rearrange("p (k t) -> p k t", t=2)[:, :, 1]
            link(g.memset(odd, 1.0))
            link(g.affine_select(out=odd, in_=odd, compare_op=ALU.is_equal, fill=0.0, base=0,
                                 pattern=[[-2, P // 2]], channel_multiplier=1))
            link(g.memset(page_later[:], 1.0))
            pl = page_later[:, :].rearrange("p (b g) -> p b g", g=NPG)
            link(g.affine_select(out=pl, in_=pl, compare_op=ALU.is_gt, fill=0.0, base=0,
                                 pattern=[[-NPG, NB], [-1, NPG]], channel_multiplier=1))
            link(g.affine_select(out=pl, in_=pl, compare_op=ALU.is_ge, fill=0.0, base=NPG - 1,
                                 pattern=[[NPG, NB], [0, NPG]], channel_multiplier=-1))
            link(g.memset(eps[:], EPS))
            link(g.memset(gt[:], 0.0))
            pool.sem_inc(w_split, 2)
            g.memset(ones[:], 1.0).then_inc(consts_ready, 1)

        wgate = part(wk, 8700, KC, 16)

        def sp_loads(sp):
            for dst, src in ((xT[:], xT_in), (vec[:], vecs_in), (wgate, wgate_in),
                             (pages, pages_in), (pagec[:], pages_in.rearrange("a (p b) -> (a p) b", b=1))):
                sp.dma_start(dst, src).then_inc(in_loaded, 16)

            def load(i, s):
                sp.dma_start(w[:, s, :, :], wall[ds(2 * i + s, 1)].rearrange("a p (k n) -> p (a k) n", k=KC))\
                    .then_inc(w_loaded[s], 16)

            for s in range(2):
                load(0, s)
            for s in range(2):
                sp.wait_ge(psum_ready, 9 * (s + 1))
                load(1, s)
            with sp.Fori(2, NPAIRS) as i:
                for s in range(2):
                    sp.wait_ge(psum_ready, i * 4 + (G_V - 8 + 2 * (s + 1)))
                    load(i, s)
            sp.wait_ge(in_loaded, 80)
            with sp.Fori(0, 16) as r:
                for s in range(2):
                    sp.wait_ge(fs["free"], r * 2 + (s + 33))
                    load_pages(sp, vpool, r, s, "vring")
            with sp.Fori(0, NTILES // 2) as i:
                for s in range(2):
                    if s == 0:
                        sp.wait_ge(psum_ready, GROUPS_A)
                    sp.wait_ge(w_split, i * 2 + (s + 1))
                    sp.dma_start(w_raw[:, s, :, :], wallb[ds(i * 2 + s, 1)].rearrange("a p (k n) -> p (a k) n", k=KC))\
                        .then_inc(w_loaded[s], 16)

        def pool_split(pool, t0, t1):
            one = ones[:, :].rearrange("p (a n) -> p a n", a=1).to_broadcast([P, KC, P])
            with S["pool"].loop((t1 - t0) // 2, 2) as i:
                for s in range(2):
                    pool.wait_ge(w_loaded[s], i * 16 + 16 * (NPAIRS + t0 // 2 + 1))
                    pool.wait_ge(psum_ready, i * 2 + (GROUPS_A + t0 + s - 1))
                    S["pool"].link(nc.gpsimd.tensor_tensor(w_hi[:, s], w_raw[:, s], one, ALU.mult))
                    nc.gpsimd.tensor_tensor(w_lo[:, s], w_raw[:, s], w_hi[:, s].bitcast(F32), ALU.subtract)\
                        .then_inc(w_split, 1)

        def split_tiles(pool, *names):
            pool_split(pool, TILE0[names[0]], TILE0[names[-1]] + dict(STREAM_B)[names[-1]])

        def pool_hand_back(pool, name):
            with pool.Fori(0, 8) as i:
                pool.wait_ge(psum_ready, i + (GROUP0[name] + 1))
                pool.sem_inc(w_split, 1)

        sq, acc0, rbc0 = part(wk, 0, 2, T), part(wk, 2 * T, T), part(wk, 3 * T, T)
        sq1, acc1, rbc1 = part(la, 12352, 2, T), part(la, 12352 + 2 * T, T), part(la, 12352 + 3 * T, T)
        nmf = at("nmf", ARENA - 6144 - 4 * T, [P, 4 * T])
        sqm, accm, rbcm = part(la, 4096, 2, NMEM), part(la, 4608, NMEM), part(la, 4864, NMEM)
        tt = part(la, 2 * XW, 2, T)

        X_NORM, M_NORM, F_NORM = (1, 6), (2, 7), (3, 8)
        OUT0 = {n: 8 * n for n in range(10)} | {1: 16, 2: 8, 6: 56, 7: 48}
        SPLIT = {1: 0, 3: 1, 4: 2, 5: 3, 6: 4, 8: 5}

        def bufs(n):
            if n in M_NORM:
                return sqm, accm, rbcm
            if n in (4, 9):
                return part(nmf, 0, 2, T), part(nmf, 2 * T, T), part(nmf, 3 * T, T)
            return (sq1, acc1, rbc1) if n else (sq, acc0, rbc0)

        def tiles_of(width):
            out = [(t * P, P, 0, (t // 4) * 512 + (t % 4) * P) for t in range(width // P)]
            if width % P:
                out.append((width - P, width % P, P - width % P, (width // P // 4) * 512))
            return out

        def pe_norm(pe, n, width):
            acc = bufs(n)[1]
            pe.wait_ge(nm_add, 8 * (n + 1))
            if n:
                pe.wait_ge(nm_cp, n)
            tl = tiles_of(width)
            for j, (at_, cnt, skip, _) in enumerate(tl):
                ins = nc.tensor.matmul(ps[:, 6, j:j + 1], acc[:, at_:at_ + P], ones[:, 0:1], start=True, stop=True)
            ins.then_inc(nm_sum, 1)
            pe.wait_ge(nm_rc, n + 1)
            for j, (_, cnt, skip, to) in enumerate(tl):
                ins = nc.tensor.matmul(psf[:, to:to + cnt], sm[:, 16 + j:17 + j].to_broadcast([P, P]),
                                       ident[:, skip:skip + cnt], start=True, stop=True)
            ins.then_inc(nm_bc, 1)

        def act_norm(act, n, src, width, wait):
            sq, _, rbc = bufs(n)
            for c in range(KC):
                wait(act, c)
                if c >= 2:
                    act.wait_ge(nm_add, 8 * n + c - 1)
                nc.scalar.activation(sq[:, c % 2, 0:width], src[:, c, :], ACT.Square).then_inc(nm_sq, 1)
            k = len(tiles_of(width))
            act.wait_ge(nm_sum, n + 1)
            nc.scalar.activation(sm[:, 0:k], ps[:, 6, 0:k], ACT.Sqrt, bias=eps[:, 0:1], scale=1.0 / D)\
                .then_inc(nm_rt, 1)
            act.wait_ge(nm_bc, n + 1)
            full = width - width % P
            ins = nc.scalar.activation(rbc[:, 0:full], psf[:, 0:full], ACT.Copy)
            if width % P:
                ins = nc.scalar.activation(rbc[:, full:width], psf[:, full:width], ACT.Copy)
            ins.then_inc(nm_cp, 1)

        def act_scale(act, n):
            for c in range(KC):
                act.wait_ge(nm_t, 8 * SPLIT[n] + c + 1)
                if n == 5:
                    S["act"].link(nc.scalar.activation(tt[:, c % 2], tt[:, c % 2], ACT.Silu, bias=v("ln_b", c)))
                nc.scalar.activation(h_hi[:, c, :], tt[:, c % 2], ACT.Copy).then_inc(nm_hi, 1)

        def dve_norm(dve, n, width, residual_of=None):
            sq, acc, rbc = bufs(n)
            if residual_of is None:
                for c in range(KC):
                    dve.wait_ge(nm_sq, 8 * n + c + 1)
                    if c == 0:
                        nc.vector.tensor_copy(acc[:, 0:width], sq[:, 0, 0:width]).then_inc(nm_add, 1)
                    else:
                        nc.vector.tensor_tensor(acc[:, 0:width], acc[:, 0:width], sq[:, c % 2, 0:width], ALU.add)\
                            .then_inc(nm_add, 1)
                    dve.wait_ge(nm_add, 8 * n + c + 1)
            else:
                g0 = GROUP0[residual_of]
                S["dve"].link(nc.vector.memset(acc, 0.0))
                dve.wait_ge(psum_free, g0)
                with dve.Fori(0, 2) as i:
                    for j in range(4):
                        dve.wait_ge(psum_ready, i * 4 + (g0 + j + 1))
                        nc.vector.tensor_tensor(at_chunk(xT, i * 4 + j), at_chunk(xT, i * 4 + j), psum_set(j % 2), ALU.add)\
                            .then_inc(psum_free, 1)
                        dve.wait_ge(nm_sq, i * 4 + (8 * n + j + 1))
                        dve.wait_ge(nm_add, i * 4 + (8 * n + j))
                        nc.vector.tensor_tensor(acc, acc, sq[:, j % 2], ALU.add).then_inc(nm_add, 1)
            k = len(tiles_of(width))
            dve.wait_ge(nm_rt, n + 1)
            nc.vector.reciprocal(sm[:, 16:16 + k], sm[:, 0:k]).then_inc(nm_rc, 1)

        def dve_scale(dve, n, src, dst, width, gain):
            rbc = bufs(n)[2]
            dve.wait_ge(nm_cp, n + 1)
            if n not in SPLIT:
                for c in range(KC):
                    nc.vector.scalar_tensor_tensor(out=dst[:, c, :], in0=src[:, c, :], scalar=v(gain, c), in1=rbc[:, 0:width],
                                                   op0=ALU.mult, op1=ALU.mult).then_inc(nm_out, 1)
                return

            def rest(c):
                dve.wait_ge(nm_hi, 8 * SPLIT[n] + c + 1)
                nc.vector.tensor_tensor(h_lo[:, c, :], tt[:, c % 2], h_hi[:, c, :].bitcast(F32), ALU.subtract)\
                    .then_inc(nm_out, 1)

            for c in range(KC):
                if c >= 2:
                    dve.wait_ge(nm_out, OUT0[n] + c - 1)
                nc.vector.scalar_tensor_tensor(out=tt[:, c % 2], in0=src[:, c, :], scalar=v(gain, c), in1=rbc[:, 0:width],
                                               op0=ALU.mult, op1=ALU.mult).then_inc(nm_t, 1)
                if c:
                    rest(c - 1)
            rest(KC - 1)

        def pe_product(pe, name, pairs, src, width, wait_src):
            wait_src(pe)
            p0, g0 = PAIR0[name], GROUP0[name]
            cols = [(n * N3, N3) for n in range(3)] if width == T else [(0, width)]
            with pe.Fori(0, pairs) as i:
                for s in range(2):
                    pe.wait_ge(w_loaded[s], i * 16 + 16 * (p0 + 1))
                    for o in range(2):
                        j = 2 * s + o
                        st = (g0 + j) % 2
                        pe.wait_ge(psum_free, i * 4 + (g0 + j - 1))
                        for k in range(KC):
                            for n, (c0, cn) in enumerate(cols):
                                ins = nc.tensor.matmul(ps[:, 3 * st + n, 0:cn], w[:, s, k, o * P:(o + 1) * P],
                                                       src[:, k, c0:c0 + cn], start=(k == 0), stop=(k == KC - 1))
                        ins.then_inc(psum_ready, 1)

        def pe_product3(pe, name, rounds, hi, lo, wait_src):
            t0, g0 = TILE0[name], GROUP0[name]
            with pe.Fori(0, rounds) as i:
                for j in range(4):
                    pe.wait_ge(w_split, i * 4 + (t0 + j + 3))
                    pe.wait_ge(psum_free, i * 4 + (g0 + j - 1))
                    for k in range(KC):
                        if j == 0:
                            wait_src(pe, k)
                        for n_pass, (wt, src) in enumerate(((w_hi, hi), (w_hi, lo), (w_lo, hi))):
                            for n in range(3):
                                ins = nc.tensor.matmul(ps[:, 3 * (j % 2) + n, 0:N3], wt[:, j % 2, k, :],
                                                       src[:, k, n * N3:(n + 1) * N3], start=(k == 0 and n_pass == 0),
                                                       stop=(k == KC - 1 and n_pass == 2))
                    ins.then_inc(psum_ready, 1)

        def epilogue(eng, name, pairs, op):
            g0 = GROUP0[name]
            with eng.Fori(0, pairs) as i:
                for j in range(4):
                    eng.wait_ge(psum_ready, i * 4 + (g0 + j + 1))
                    op(i, j, (g0 + j) % 2).then_inc(psum_free, 1)

        def at_chunk(buf, c):
            return buf[:, ds(c, 1), :].rearrange("p a (b n) -> p (a b) n", b=3)

        def after(*pairs):
            def wait(eng):
                for s, n in pairs:
                    eng.wait_ge(s, n)
            return wait

        def freed(name, pairs):
            return (psum_free, GROUP0[name] + 4 * pairs)

        def store(pool, dst, src):
            n_stored[0] += 1
            pool.dma_start(dst, src).then_inc(stored, 16)

        qf, kf = big[:, 0:4, :], big[:, 4:8, :]
        vf = part(bigf, 8 * T, QT, 512)
        vs = wk[0:NB, 8000:8512]

        def pe_values(pe):
            pe.wait_ge(nm_out, 8)
            for s in range(2):
                pe.wait_ge(w_loaded[s], 16)
                for t in range(QT + 1):
                    g = 9 * s + t
                    m = P if t < QT else NB
                    if g >= 2:
                        pe.wait_ge(psum_free, g - 1)
                    for k in range(KC):
                        ins = nc.tensor.matmul(ps[0:m, 3 * (g % 2), 0:256], hT[:, k, t * P:t * P + m], w[:, s, k, :],
                                               start=(k == 0), stop=(k == KC - 1))
                    ins.then_inc(psum_ready, 1)

        def act_values(act):
            for g in range(18):
                s, t = divmod(g, 9)
                act.wait_ge(psum_ready, g + 1)
                if t < QT:
                    ins = nc.scalar.activation(vf[:, t, s * 256:s * 256 + 256], ps[:, 3 * (g % 2), 0:256], ACT.Copy)
                else:
                    ins = nc.scalar.activation(vs[:, s * 256:s * 256 + 256], ps[0:NB, 3 * (g % 2), 0:256], ACT.Copy)
                ins.then_inc(psum_free, 1)

        gates_ready, gates_u, gates_exp, gates_done, gc_ready = (sem(n) for n in (
            "gates_ready", "gates_u", "gates_exp", "gates_done", "gc_ready"))
        ga = [part(wk, 4200 + 144 * n, 9, 16) for n in range(8)]
        gbank = ps[:, 7, 0:144].rearrange("p (t n) -> p t n", n=16)
        G_G, G_GC, G_RQ, G_RK, G_RQE, G_RKB, G_B, G_BE, G_KD, G_EL, G_E = range(11)
        tile_at = [t * P for t in range(QT)] + [T - P]

        def pe_gate_sums(pe):
            pe.wait_ge(gates_done, 1)
            for t in range(QT):
                nc.tensor.matmul(ps[:, 7, 256 + 4 * t:260 + 4 * t], upper[:], gt[:, t, G_G, :], start=True, stop=True)
            for t in range(QT):
                nc.tensor.matmul(ps[:, 7, 288 + 4 * t:292 + 4 * t], ones[:], gt[:, t, G_G, :], start=True, stop=True)
            for t in range(QT):
                for u in range(t + 1):
                    ins = nc.tensor.matmul(ps[:, 7, 320 + 8 * t:328 + 8 * t], upper[:] if u == t else ones[:],
                                           lf[:, u, :], start=(u == 0), stop=(u == t))
            ins.then_inc(gc_ready, 1)

        def pe_gates(pe):
            pe.wait_ge(in_loaded, 80)
            for t in range(9):
                for k in range(KC):
                    ins = nc.tensor.matmul(gbank[:, t, :], hT[:, k, tile_at[t]:tile_at[t] + P], wgate[:, k, :],
                                           start=(k == 0), stop=(k == KC - 1))
            ins.then_inc(gates_ready, 1)

        def act_gates(act):
            act.wait_ge(in_loaded, 80)
            nc.scalar.activation(gcoef[:], v("gate_alog", 0, 16), ACT.Exp).then_inc(gates_exp, 1)
            act.wait_ge(gates_u, 1)
            nc.scalar.activation(ga[2], ga[2], ACT.Exp).then_inc(gates_exp, 1)
            nc.scalar.activation(ga[4], ga[0], ACT.Exp).then_inc(gates_exp, 1)

        def act_gate_sums(act):
            act.wait_ge(gates_u, 2)
            for src, dst in ((G_GC, G_E), (G_KD, G_KD), (G_EL, G_EL)):
                nc.scalar.activation(gt[:, :, dst, :], gt[:, :, src, :], ACT.Exp).then_inc(gates_exp, 1)

        def dve_gates(dve):
            link, vv = S["dve"].link, nc.vector
            dve.wait_ge(gates_ready, 1)
            dve.wait_ge(gates_exp, 1)
            y, ny, m, z, z2, h = ga[0], ga[1], ga[2], ga[3], ga[5], ga[6]
            bias = v("gate_bias", 0, 16).rearrange("p (a n) -> p a n", a=1).to_broadcast([P, 9, 16])
            link(vv.tensor_tensor(y, gbank, bias, ALU.add))
            link(vv.tensor_scalar(y[:, :, 4:16], y[:, :, 4:16], -1.0, None, ALU.mult))
            link(vv.tensor_scalar(ny, y, -1.0, None, ALU.mult))
            vv.tensor_tensor(m, y, ny, ALU.min).then_inc(gates_u, 1)
            dve.wait_ge(gates_exp, 3)
            link(vv.tensor_scalar(z, m, 2.0, None, ALU.add))
            link(vv.reciprocal(z, z))
            link(vv.tensor_tensor(z, z, m, ALU.mult))
            link(vv.tensor_tensor(z2, z, z, ALU.mult))
            link(vv.tensor_scalar(h, z2, 1.0 / 19, None, ALU.mult))
            for d in (17, 15, 13, 11, 9, 7, 5, 3):
                link(vv.scalar_tensor_tensor(out=h, in0=h, scalar=1.0 / d, in1=z2, op0=ALU.add, op1=ALU.mult))
            link(vv.scalar_tensor_tensor(out=h, in0=h, scalar=1.0, in1=z, op0=ALU.add, op1=ALU.mult))
            link(vv.tensor_scalar(ny, y, 0.0, None, ALU.max))
            link(vv.scalar_tensor_tensor(out=h, in0=h, scalar=2.0, in1=ny, op0=ALU.mult, op1=ALU.add))
            link(vv.tensor_scalar(lf[:], h[:, :, 8:16], -1.0, None, ALU.mult))
            link(vv.tensor_scalar(gcoef[:], gcoef[:], -1.0, None, ALU.mult))
            coef = gcoef[:, 0:4].rearrange("p (a n) -> p a n", a=1).to_broadcast([P, 9, 4])
            link(vv.tensor_scalar(ga[4], ga[4], 1.0, None, ALU.add))
            link(vv.reciprocal(gt[:, :, G_B, :], ga[4][:, :, 4:8]))
            vv.tensor_tensor(gt[:, :, G_G, :], h[:, :, 0:4], coef, ALU.mult).then_inc(gates_done, 1)
            dve.wait_ge(gc_ready, 1)
            dve.wait_ge(gates_done, 1)
            gc_ps = ps[:, 7, 256:288].rearrange("p (t n) -> p t n", n=4)
            tot_ps = ps[:, 7, 288:320].rearrange("p (t n) -> p t n", n=4)
            link(vv.tensor_copy(cf[:], ps[:, 7, 320:384].rearrange("p (t n) -> p t n", n=8)))
            link(vv.tensor_copy(gt[:, 0:QT, G_GC, :], gc_ps))
            link(vv.tensor_copy(gt[:, 0:QT, G_EL, :], tot_ps))
            link(vv.tensor_copy(gt[:, QT, G_GC, :], gt[:, QT, G_G, :]))
            link(vv.tensor_copy(gt[:, QT, G_EL, :], gt[:, QT, G_G, :]))
            vv.tensor_tensor(gt[:, :, G_KD, :], gt[:, :, G_EL, :], gt[:, :, G_GC, :], ALU.subtract).then_inc(gates_u, 1)
            dve.wait_ge(gates_exp, 6)
            link(vv.tensor_tensor(gt[:, :, G_BE, :], gt[:, :, G_B, :], gt[:, :, G_E, :], ALU.mult))

        fox_cst, fox_qk, fox_cb, fox_cbc, fox_s, fox_m, fox_e, fox_pt, fox_ptc, fox_o, fox_on, fox_ot, fox_otc = (
            sem("fox_" + n) for n in ("cst", "qk", "cb", "cbc", "s", "m", "e", "pt", "ptc", "o", "on", "ot", "otc"))
        f_neg = part(aTf, 0, 2, SEQ)
        f_pt = part(aTf, 2 * SEQ, 2, SEQ)
        f_q = part(wk, 0, SEQ)
        f_k = part(wk, SEQ, SEQ)
        f_s = part(wk, 2 * SEQ, 2, SEQ)
        f_o = part(wk, 4 * SEQ, QT, P)
        f_c = part(wk, 5 * SEQ, QT, 2)
        f_st = part(wk, 5 * SEQ + 16, 4, 16)
        NT = 2 * QT

        def blk(n):
            return n // QT, n % QT, (n % QT + 1) * P

        def pe_fox(pe):
            with pe.Fori(0, 4) as i:
                pe.wait_ge(fox_cst, i + 1)
                for h in range(2):
                    if h == 0:
                        pe.wait_ge(fox_otc, i + 1)
                    else:
                        pe.wait_ge(fox_cbc, i * 2 + 1)
                    for t in range(QT):
                        ins = nc.tensor.matmul(psf[:, t * P:t * P + P], f_c[:, t, h:h + 1].to_broadcast([P, P]),
                                               ident[:], start=True, stop=True)
                    ins.then_inc(fox_cb, 1)
                pe.wait_ge(fox_qk, i * 2 + 2)
                pe.wait_ge(fox_cbc, i * 2 + 2)

                def scores(n):
                    h, t, wd = blk(n)
                    if n >= 2:
                        pe.wait_ge(fox_m, i * NT + (n - 1))
                    for c0 in range(0, wd, 512):
                        cn = min(512, wd - c0)
                        ins = nc.tensor.matmul(psf[:, (n % 2) * 1024 + c0:(n % 2) * 1024 + c0 + cn],
                                               f_q[64 * h:64 * h + 64, t * P:t * P + P],
                                               f_k[64 * h:64 * h + 64, c0:c0 + cn], start=True, stop=True)
                    ins.then_inc(fox_s, 1)

                def turn(n):
                    h, t, wd = blk(n)
                    pe.wait_ge(fox_e, i * NT + (n + 1))
                    if n:
                        pe.wait_ge(fox_ptc, i * NT + n)
                    for c0 in range(0, wd, P):
                        ins = nc.tensor.transpose(psf[:, 2048 + c0:2048 + c0 + P], f_s[:, n % 2, c0:c0 + P], ident[:])
                    ins.then_inc(fox_pt, 1)

                def values(n):
                    h, t, wd = blk(n)
                    pe.wait_ge(fox_ptc, i * NT + (n + 1))
                    if n >= 2:
                        pe.wait_ge(fox_on, i * NT + (n - 1))
                    for kt in range(t + 1):
                        ins = nc.tensor.matmul(ps[:, 6 + n % 2, 0:64], f_pt[:, n % 2, kt * P:kt * P + P],
                                               vf[:, kt, ds(i * P + h * 64, 64)], start=(kt == 0), stop=(kt == t))
                    ins.then_inc(fox_o, 1)

                scores(0)
                scores(1)
                for n in range(NT):
                    turn(n)
                    if n + 2 < NT:
                        scores(n + 2)
                    if n:
                        values(n - 1)
                values(NT - 1)
                pe.wait_ge(fox_on, i * NT + NT)
                for t in range(QT):
                    ins = nc.tensor.transpose(psf[:, t * P:t * P + P], f_o[:, t, :], ident[:])
                ins.then_inc(fox_ot, 1)

        def act_fox(act):
            act.sem_inc(fox_otc, 1)
            with act.Fori(0, 4) as i:
                for h in range(2):
                    act.wait_ge(fox_cb, i * 2 + (h + 1))
                    nc.scalar.activation(f_neg[:, h, :], psf[:, 0:SEQ], ACT.Copy, scale=-1.0).then_inc(fox_cbc, 1)

                def exps(n):
                    h, t, wd = blk(n)
                    act.wait_ge(fox_m, i * NT + (n + 1))
                    nc.scalar.activation(f_s[:, n % 2, 0:wd], f_s[:, n % 2, 0:wd], ACT.Exp, bias=f_st[:, 1, n:n + 1],
                                         accum_out=f_st[:, 2, n:n + 1]).then_inc(fox_e, 1)

                exps(0)
                for n in range(NT):
                    if n + 1 < NT:
                        exps(n + 1)
                    h, t, wd = blk(n)
                    act.wait_ge(fox_pt, i * NT + (n + 1))
                    if n >= 2:
                        act.wait_ge(fox_o, i * NT + (n - 1))
                    nc.scalar.activation(f_pt[:, n % 2, 0:wd], psf[:, 2048:2048 + wd], ACT.Copy).then_inc(fox_ptc, 1)
                act.wait_ge(fox_ot, i + 1)
                nc.scalar.activation(aT[:, ds(i + 4, 1), 0:SEQ].rearrange("p a n -> p (a n)"), psf[:, 0:SEQ], ACT.Copy)\
                    .then_inc(fox_otc, 1)

        def pool_fox(pool):
            pool.wait_ge(*freed("q_fox", 1))
            pool.wait_ge(gates_exp, 6)
            with pool.Fori(0, 4) as i:
                pool.wait_ge(fox_otc, i + 1)
                nc.gpsimd.tensor_copy(f_c, cf[:, :, ds(i * 2, 2)]).then_inc(fox_cst, 1)
                nc.gpsimd.tensor_copy(f_q, qf[:, ds(i, 1), 0:SEQ].rearrange("p a n -> p (a n)")).then_inc(fox_qk, 1)
                nc.gpsimd.tensor_copy(f_k, kf[:, ds(i, 1), 0:SEQ].rearrange("p a n -> p (a n)")).then_inc(fox_qk, 1)

        def dve_fox(dve):
            PER = NT * 3
            with S["dve"].loop(4, PER) as i:
                link, vv = S["dve"].link, nc.vector

                def soft(n):
                    h, t, wd = blk(n)
                    dve.wait_ge(fox_s, i * NT + (n + 1))
                    dve.wait_ge(fox_cbc, i * 2 + 2)
                    if n >= 2:
                        dve.wait_ge(fox_pt, i * NT + (n - 1))
                    link(vv.tensor_tensor(f_s[:, n % 2, 0:wd], psf[:, (n % 2) * 1024:(n % 2) * 1024 + wd],
                                          f_neg[:, h, 0:wd], ALU.add))
                    link(vv.tensor_tensor(f_s[:, n % 2, t * P:wd], f_s[:, n % 2, t * P:wd], neg_qk[:], ALU.add))
                    vv.tensor_reduce(f_st[:, 1, n:n + 1], f_s[:, n % 2, 0:wd], AX.X, ALU.max, negate=True)\
                        .then_inc(fox_m, 1)

                def out(n):
                    h, t, wd = blk(n)
                    dve.wait_ge(fox_o, i * NT + (n + 1))
                    link(vv.reciprocal(f_st[:, 3, n:n + 1], f_st[:, 2, n:n + 1]))
                    if n == 0:
                        dve.wait_ge(fox_otc, i + 1)
                    vv.tensor_scalar(f_o[:, t, h * 64:h * 64 + 64], ps[:, 6 + n % 2, 0:64],
                                     f_st[:, 3, n:n + 1], None, ALU.mult).then_inc(fox_on, 1)

                soft(0)
                soft(1)
                for n in range(NT):
                    if n + 2 < NT:
                        soft(n + 2)
                    if n:
                        out(n - 1)
                out(NT - 1)

        fs_names = ("small", "turned", "lf", "lft", "lftot", "lfc", "bias", "biasc", "qb", "qbc", "ring0", "ring1", "free",
                    "snp", "snc", "back", "sn", "mx", "mt", "mc", "mb", "sh", "ex", "sum", "tot", "pr", "vring0", "vring1", "pvc", "out")
        fs = {n: sem("fs_" + n) for n in fs_names}
        xTf = xT[:, :, :].rearrange("p a b -> p (a b)")
        s_ring = part(xTf, 0, 2, 4, 512)
        s_qb = part(xTf, 4096, NB, 512)
        s_pr = part(xTf, 4096, NB, NPG, HB)
        s_o = part(xTf, 5120, NB, 8)
        s_pv = part(xTf, 5184, 4, NB)
        s_sn = part(xTf, 8192, NB, HB)
        s_q, s_k, s_v = (part(wk, o, 4, NB) for o in (6240, 6272, 7768))
        s_prod = part(wk, 512, 2048)
        s_sc = part(wk, 2560, NB, NPG, HB)
        s_lft = part(wk, 3584, 1024)
        s_lf = part(wk, 4608, HB, P)
        s_tot = part(wk, 5632, HB)
        s_qk = part(wk, 5648, 32)
        s_mx, s_mb, s_sum, s_rs, s_cq = (part(wk, 5764 + 64 * n, NB, HB) for n in range(5))
        s_mc = part(wk, 6100, 1)

        def heads_even_odd(ap, odd):
            return ap.rearrange("p b (c t) -> p t c b", t=2)[:, odd]

        def pool_fox_rows(pool):
            pool.wait_ge(fox_otc, 5)
            for n, src in ((0, qf), (1, kf)):
                dst = (s_q, s_k)[n]
                nc.gpsimd.tensor_copy(dst, src[:, :, SEQ:T]).then_inc(fs["small"], 1)
            pool.wait_ge(in_loaded, 80)
            pool.indirect_dma_start(out=s_lft, out_offset=None, in_=fpool.rearrange("g t h -> g (t h)"),
                                    in_offset=bass.IndirectOffsetOnAxis(ap=pagec[:, 0:1].bitcast(mybir.dt.uint32), axis=0))\
                .then_inc(fs["lf"], 16)

        def load_pages(eng, src, r, s, done):
            for g in range(4):
                pg = eng.value_load(pages[0:1, ds(r * 8 + (4 * s + g), 1)], min_val=0, max_val=src.shape[0] - 1)
                eng.dma_start(s_ring[:, s, g, :], src[ds(pg, 1)].rearrange("a p n -> p (a n)"))\
                    .then_inc(fs[f"{done}{s}"], 16)

        def pool_key_pages(pool):
            with pool.Fori(0, 16) as r:
                for s in range(2):
                    pool.wait_ge(fs["free"], r * 2 + (s + 1))
                    load_pages(pool, kpool, r, s, "ring")

        def pe_fox_rows(pe):
            pe.wait_ge(fox_otc, 5)
            pe.wait_ge(fs["small"], 2)

            def queries(half):
                for b in range(4):
                    for c in range(4):
                        ins = nc.tensor.matmul(ps[:, b, c * P:(c + 1) * P],
                                               s_q[:, c, 4 * half + b:4 * half + b + 1].to_broadcast([P, P]), ident[:],
                                               start=True, stop=True)
                ins.then_inc(fs["qb"], 1)

            queries(0)
            for c in range(4):
                ins = nc.tensor.transpose(ps[:, 7, c * NB:(c + 1) * NB], vs[:, c * P:(c + 1) * P], ident[0:NB, 0:NB])
            ins.then_inc(fs["turned"], 1)
            pe.wait_ge(fs["qbc"], 1)
            queries(1)
            pe.wait_ge(fs["lf"], 16)
            for h in range(HB):
                ins = nc.tensor.transpose(psf[:, 2048 + h * P:2048 + (h + 1) * P],
                                          s_lft.rearrange("p (t h) -> p h t", h=HB)[:, h, :], ident[:])
            ins.then_inc(fs["lft"], 1)
            pe.wait_ge(fs["lftot"], 1)
            pe.wait_ge(fs["lfc"], 1)
            for h in range(HB):
                to = psf[:, 2048 + h * P:2048 + (h + 1) * P]
                nc.tensor.matmul(to, later[:], s_lf[:, h, :], start=True, stop=False)
                nc.tensor.matmul(to, s_tot[:, h:h + 1].to_broadcast([P, P]), page_later[:], start=False, stop=True)
            for h in range(HB):
                ins = nc.tensor.matmul(ps[:, 6, h * NB:(h + 1) * NB], lf[:, QT, h:h + 1].to_broadcast([P, P]),
                                       ident[:, P - NB:P], start=True, stop=True)
            ins.then_inc(fs["bias"], 1)
            pe.wait_ge(fs["snp"], 1)
            pe.wait_ge(fs["qbc"], 2)
            for t in range(2):
                ins = nc.tensor.matmul(ps[:, 1 + 2 * t, 0:32], ones[64 * t:64 * t + 64, :], s_qk[64 * t:64 * t + 64, :],
                                       start=True, stop=True)
            ins.then_inc(fs["sn"], 1)
            pe.wait_ge(fs["biasc"], 2)
            pe.wait_ge(fs["snc"], 1)

        def pe_fox_soft(pe):
            pe.wait_ge(*freed("z", 1))
            pe.wait_ge(fs["mx"], 1)
            nc.tensor.transpose(ps[0:64, 2, 0:P], s_mx.rearrange("p b h -> p (b h)"), ident[:]).then_inc(fs["mt"], 1)
            pe.wait_ge(fs["mc"], 1)
            nc.tensor.matmul(ps[:, 3, 0:64], s_mc[0:64, :].to_broadcast([64, P]), ident[0:64, 0:64], start=True, stop=True)\
                .then_inc(fs["mb"], 1)
            pe.wait_ge(fs["sum"], 1)
            nc.tensor.matmul(ps[:, 2, 128:192], ones[:], s_sum.rearrange("p b h -> p (b h)"), start=True, stop=True)\
                .then_inc(fs["tot"], 1)

        def pe_fox_values(pe, i, e, q):
            pe.wait_ge(fs[f"vring{q % 2}"], i * 256 + 64 * (2 * e + q // 2 + 1))
            for g in range(4):
                pg = 4 * q + g
                for c in range(4):
                    ins = nc.tensor.matmul(ps[:, 6 + e, 2 * c:2 * c + 2], s_ring[:, q % 2, g, c * P:(c + 1) * P],
                                           s_pr[:, ds(i * 2 + e, 1), pg, 2 * c:2 * c + 2].rearrange("p a h -> p (a h)"),
                                           start=(pg == 0 and c == 0), stop=(pg == NPG - 1), skip_group_check=True)
            ins.then_inc(fs["free"], 1)

        def act_fox_rows(act):
            act.wait_ge(fs["qb"], 1)
            nc.scalar.activation(s_qb[:, 0:4, :], ps[:, 0:4, :], ACT.Copy).then_inc(fs["qbc"], 1)
            act.wait_ge(fs["lft"], 1)
            nc.scalar.activation(s_lf.rearrange("p h t -> p (h t)"), psf[:, 2048:3072], ACT.Copy).then_inc(fs["lfc"], 1)
            act.wait_ge(fs["qb"], 2)
            nc.scalar.activation(s_qb[:, 4:8, :], ps[:, 0:4, :], ACT.Copy).then_inc(fs["qbc"], 1)
            act.wait_ge(fs["bias"], 1)
            act.wait_ge(fs["lftot"], 1)
            nc.scalar.activation(s_lft, psf[:, 2048:3072], ACT.Copy).then_inc(fs["biasc"], 1)
            nc.scalar.activation(s_cq, ps[:, 6, 0:64].rearrange("p (h b) -> p b h", b=NB), ACT.Copy).then_inc(fs["biasc"], 1)

        def act_fox_soft(act):
            act.wait_ge(fs["sh"], 1)
            nc.scalar.activation(s_sc, s_sc, ACT.Exp).then_inc(fs["ex"], 1)
            nc.scalar.activation(s_sn, s_sn, ACT.Exp).then_inc(fs["ex"], 1)

        def act_fox_values(act, i, e):
            act.wait_ge(fs["free"], i * 8 + (4 * e + 38))
            nc.scalar.activation(s_o[:, ds(i * 2 + e, 1), :].rearrange("p a n -> p (a n)"), ps[:, 6 + e, 0:8], ACT.Copy)\
                .then_inc(fs["pvc"], 1)

        def dve_fox_rows(dve):
            link, vv = S["dve"].link, nc.vector
            dve.wait_ge(fs["turned"], 1)
            link(vv.tensor_copy(s_v, ps[:, 7, 0:32].rearrange("p (c b) -> p c b", b=NB)))
            dve.wait_ge(fs["small"], 2)
            vv.tensor_tensor(s_qk, s_q.rearrange("p c b -> p (c b)"), s_k.rearrange("p c b -> p (c b)"), ALU.mult)\
                .then_inc(fs["snp"], 1)
            dve.wait_ge(fs["lf"], 16)
            vv.tensor_reduce(s_tot, s_lft.rearrange("p (t h) -> p h t", h=HB), AX.X, ALU.add).then_inc(fs["lftot"], 1)
            dve.wait_ge(fs["sn"], 1)
            for t in range(2):
                ins = vv.tensor_copy(heads_even_odd(s_sn, t), ps[:, 1 + 2 * t, 0:32].rearrange("p (c b) -> p c b", b=NB))
                if t == 0:
                    link(ins)
            ins.then_inc(fs["snc"], 1)

        def dve_key_scores(dve, i, j, link):
            vv = nc.vector
            for s in range(2):
                q = 2 * (j % 2) + s
                dve.wait_ge(fs[f"ring{s}"], i * 256 + 64 * (j + 1))
                dve.wait_ge(fs["free"], i * 8 + (2 * j + s + 2))
                link(vv.tensor_tensor(s_prod.rearrange("p (g n) -> p g n", g=4), s_ring[:, s, :, :],
                                      s_qb[:, ds(i * 2 + j // 2, 1), :].to_broadcast([P, 4, 512]), ALU.mult))
                vv.tensor_reduce(s_sc[:, ds(i * 2 + j // 2, 1), 4 * q:4 * q + 4, :].rearrange("p a g h -> p (a g h)"),
                                 s_prod.rearrange("p (x n) -> p x n", n=DHB), AX.X, ALU.add).then_inc(fs["free"], 1)

        def dve_fox_soft(dve):
            link, vv = S["dve"].link, nc.vector
            dve.wait_ge(fs["free"], 34)
            dve.wait_ge(fs["biasc"], 2)
            link(vv.tensor_tensor(s_sc, s_sc, s_lft.rearrange("p (h b g) -> p b g h", h=HB, b=NB), ALU.add))
            cq = s_cq.rearrange("p b (a h) -> p b a h", a=1).to_broadcast([P, NB, NPG, HB])
            link(vv.tensor_tensor(s_sc, s_sc, cq, ALU.add))
            vv.tensor_reduce(s_mx, s_sc.rearrange("p b g h -> p b h g"), AX.X, ALU.max).then_inc(fs["mx"], 1)
            dve.wait_ge(fs["mt"], 1)
            vv.tensor_reduce(s_mc[0:64, :], ps[0:64, 2, 0:P], AX.X, ALU.max).then_inc(fs["mc"], 1)
            dve.wait_ge(fs["mb"], 1)
            link(vv.tensor_tensor(s_mb, ps[:, 3, 0:64].rearrange("p (b h) -> p b h", h=HB), s_sn, ALU.max))
            mb = s_mb.rearrange("p b (a h) -> p b a h", a=1).to_broadcast([P, NB, NPG, HB])
            link(vv.tensor_tensor(s_sn, s_sn, s_mb, ALU.subtract))
            vv.tensor_tensor(s_sc, s_sc, mb, ALU.subtract).then_inc(fs["sh"], 1)
            dve.wait_ge(fs["ex"], 1)
            vv.tensor_reduce(s_sum, s_sc.rearrange("p b g h -> p b h g"), AX.X, ALU.add).then_inc(fs["sum"], 1)
            dve.wait_ge(fs["ex"], 2)
            dve.wait_ge(fs["tot"], 1)
            link(vv.tensor_tensor(s_rs, ps[:, 2, 128:192].rearrange("p (b h) -> p b h", h=HB), s_sn, ALU.add))
            link(vv.reciprocal(s_rs, s_rs))
            link(vv.tensor_tensor(s_sn, s_sn, s_rs, ALU.mult))
            rs = s_rs.rearrange("p b (a h) -> p b a h", a=1).to_broadcast([P, NB, NPG, HB])
            vv.tensor_tensor(s_pr, s_sc, rs, ALU.mult).then_inc(fs["pr"], 1)

        def dve_fox_out(dve):
            link, vv = S["dve"].link, nc.vector
            dve.wait_ge(fs["pvc"], NB)
            for t in range(2):
                half = slice(64 * t, 64 * t + 64)
                link(vv.tensor_tensor(s_pv[half], s_v[half], heads_even_odd(s_sn, t)[half], ALU.mult))
                vv.tensor_tensor(aT[half, 4:8, SEQ:T], s_pv[half], s_o.rearrange("p b (c t) -> p t c b", t=2)[half, t],
                                 ALU.add).then_inc(fs["out"], 1)

        conv_done, conv_st, conv_pad, conv_silu = (sem("conv_" + n) for n in ("done", "st", "pad", "silu"))
        c_raw = part(wk, 6400, T + 3)
        c_tail = part(wk, 7800, 12, 3 + NB)
        c_st = part(wk, 7932, 12, 3, NB)

        def pool_conv(pool):
            pool.wait_ge(stored, 16 * 5)
            pool.wait_ge(fs["turned"], 1)
            nc.gpsimd.memset(c_raw[:, 0:3], 0.0).then_inc(conv_pad, 1)
            pool.dma_start(c_st, st_gconv_in).then_inc(conv_st, 16)

        def act_conv(act):
            g0 = GROUP0["conv"]
            act.wait_ge(conv_pad, 1)
            with act.Fori(0, 3) as i:
                for j in range(4):
                    st = (g0 + j) % 2
                    act.wait_ge(psum_ready, i * 4 + (g0 + j + 1))
                    nc.scalar.activation(c_tail[:, ds(i * 4 + j, 1), :].rearrange("p a n -> p (a n)"),
                                         ps[:, 3 * st + 2, N3 - NB - 3:N3], ACT.Copy)
                    nc.scalar.activation(thirds(c_raw[:, 3:T + 3]), psum_set(st), ACT.Copy).then_inc(psum_free, 1)
                    act.wait_ge(conv_done, i * 4 + (j + 1))
                    chunk = big[:, ds(i * 4 + j, 1), :].rearrange("p a n -> p (a n)")
                    nc.scalar.activation(chunk, chunk, ACT.Silu).then_inc(conv_silu, 1)

        def dve_conv(dve):
            vv, g0, w0 = nc.vector, GROUP0["conv"], VOFF["conv_a"][0]
            dve.wait_ge(stored, 16 * 5)
            dve.wait_ge(conv_st, 16)
            dve.wait_ge(fs["qbc"], 2)
            dve.sem_inc(fs["free"], 2)
            with S["dve"].loop(3, 4 * 9) as i:
                link = S["dve"].link
                for j in range(4):
                    dve.wait_ge(psum_free, i * 4 + (g0 + j + 1))
                    chunk = big[:, ds(i * 4 + j, 1), :].rearrange("p a n -> p (a n)")
                    for t in range(CA):
                        tap = vec[:, ds(i * 16 + (w0 + 4 * j + t), 1)]
                        row = c_st[:, ds(i * 4 + j, 1), t, :].rearrange("p a n -> p (a n)") if t < 3 else c_raw[:, SEQ + 3:]
                        if t == 0:
                            link(vv.tensor_scalar(chunk[:, SEQ:T], row, tap, None, ALU.mult))
                            link(vv.tensor_scalar(chunk[:, 0:SEQ], c_raw[:, 0:SEQ], tap, None, ALU.mult))
                            continue
                        link(vv.scalar_tensor_tensor(out=chunk[:, SEQ:T], in0=row, scalar=tap, in1=chunk[:, SEQ:T],
                                                     op0=ALU.mult, op1=ALU.add))
                        ins = vv.scalar_tensor_tensor(out=chunk[:, 0:SEQ], in0=c_raw[:, t:t + SEQ], scalar=tap,
                                                      in1=chunk[:, 0:SEQ], op0=ALU.mult, op1=ALU.add)
                        if t < 3:
                            link(ins)
                    ins.then_inc(conv_done, 1)
                    dve_key_scores(dve, i, j, link)
            for j in range(4):
                dve_key_scores(dve, 3, j, S["dve"].link)

        l2_sq, l2_ps, l2_rt = sem("l2_sq"), sem("l2_ps"), sem("l2_rt")
        l2_n = [0]
        l_st, l_rc = part(wk, 2100, 72), part(wk, 2180, 72)

        def act_squares(act, src, heads, scale):
            n0 = l2_n[0]
            for h in range(heads):
                if h >= 2:
                    act.wait_ge(l2_ps, n0 + h - 1)
                nc.scalar.activation(sq[:, h % 2, :], src[:, h, :], ACT.Square).then_inc(l2_sq, 1)
            act.wait_ge(l2_ps, n0 + heads)
            nc.scalar.activation(l_st[:, 0:9 * heads], ps[:, 6, 0:9 * heads], ACT.Sqrt, bias=eps[:, 0:1], scale=scale)\
                .then_inc(l2_rt, 1)

        def pe_squares(pe, n0, heads):
            for h in range(heads):
                pe.wait_ge(l2_sq, n0 + h + 1)
                for t in range(9):
                    ins = nc.tensor.matmul(ps[:, 6, h * 9 + t:h * 9 + t + 1], sq[:, h % 2, tile_at[t]:tile_at[t] + P],
                                           ones[:, 0:1], start=True, stop=True)
                ins.then_inc(l2_ps, 1)

        def dve_norm_gates(dve):
            link, vv = S["dve"].link, nc.vector
            dve.wait_ge(l2_rt, 1)
            link(vv.reciprocal(l_rc, l_st))
            rc = l_rc.rearrange("p (k h t) -> p k t h", k=2, t=9)
            link(vv.tensor_scalar(gt[:, :, G_RQ, :], rc[:, 0], float(P) ** -0.5, None, ALU.mult))
            link(vv.tensor_copy(gt[:, :, G_RK, :], rc[:, 1]))
            link(vv.tensor_tensor(gt[:, :, G_RQE, :], gt[:, :, G_RQ, :], gt[:, :, G_E, :], ALU.mult))
            vv.tensor_tensor(gt[:, :, G_RKB, :], gt[:, :, G_RK, :], gt[:, :, G_B, :], ALU.mult).then_inc(l2_rt, 1)

        gd = {n: sem("gd_" + n) for n in ("st", "bc", "n", "p", "dt", "ex", "kt", "vt", "kb", "lt", "l", "lc", "ed",
                                          "b", "x", "xc", "e", "u", "uc", "ws", "vn", "o", "oc", "s")}
        Q8 = 2 * HA * P

        def quad(buf, n):
            return part(buf, n * Q8, 2 * HA, P)

        kn, kb, qn, qg, vS, ktok, vb, kbg = (quad(hTf, n) for n in range(8))
        kd, DT, AT, LT, L_, E_, D_ = (quad(wk, n) for n in range(7))
        X_, B_, u_, wT, vn = DT, (LT, kn), kb, L_, D_
        S_ = part(wk, 7168, HA, P)
        cst = part(wk, 7680, 2, 11, 4)
        P01, P23, P45, P67 = (psf[:, 1024 * n:1024 * n + 1024].rearrange("p (x n) -> p x n", n=P) for n in range(4))

        def cc(kind, x):
            return cst[:, x // HA, kind, x % HA:x % HA + 1]

        def per_token(kind):
            return cst[:, :, kind, :].rearrange("p a (h n) -> p a h n", n=1).to_broadcast([P, 2, HA, P])

        def split(ap):
            return ap.rearrange("p (a h) n -> p a h n", a=2)

        def over8(m):
            return m.rearrange("p (a n) -> p a n", a=1).to_broadcast([P, 2 * HA, P])

        def pool_gdn(pool):
            pool.wait_ge(*freed("z", 1))
            pool.wait_ge(l2_rt, 2)
            pool.wait_ge(fs["pr"], 1)
            with pool.Fori(0, QT // 2) as i:
                pool.wait_ge(gd["s"], i * 2 + 1)
                nc.gpsimd.tensor_copy(cst, gt[:, ds(i * 2, 2), :, :]).then_inc(gd["st"], 1)
                nc.gpsimd.tensor_copy(split(vS), big[:, 8:12, ds(i * 256, 256)].rearrange("p h (a n) -> p a h n", a=2))\
                    .then_inc(gd["st"], 1)
                pool.wait_ge(gd["kt"], i + 1)
                pool.wait_ge(gd["st"], i * 2 + 2)
                nc.gpsimd.tensor_tensor(split(kbg), split(ktok), per_token(G_BE), ALU.mult).then_inc(gd["kb"], 1)
                nc.gpsimd.tensor_tensor(split(kd), split(ktok), per_token(G_KD), ALU.mult).then_inc(gd["kb"], 1)
                for s in range(1, 7):
                    if s == 1:
                        pool.wait_ge(gd["ed"], i * 7 + 1)
                    elif s >= 3:
                        pool.wait_ge(gd["x"], i * 6 + (s - 2))
                    nc.gpsimd.tensor_tensor(B_[s % 2], L_, over8(lev[:, s, :]), ALU.mult).then_inc(gd["b"], 1)

        V_AT = {1: ((0, 0), (0, 1)), 2: ((0, 2), (0, 3)), 3: ((1, 0), (1, 1)), 4: ((1, 2), (1, 3))}

        def pe_gdn(pe):
            mm = nc.tensor.matmul

            def each(op, done, xs=range(2 * HA)):
                for x in xs:
                    ins = op(x)
                ins.then_inc(gd[done], 1)

            with pe.Fori(0, QT // 2) as i:
                pe.wait_ge(gd["st"], i * 2 + 2)
                pe.wait_ge(gd["oc"], i * 2 + 1)
                for to, kind in ((P01, G_RQ), (P23, G_RK), (P45, G_RQE), (P67, G_RKB)):
                    each(lambda x: mm(to[:, x, :], cc(kind, x).to_broadcast([P, P]), ident[:], start=True, stop=True), "bc")
                pe.wait_ge(gd["n"], i * 4 + 4)
                each(lambda x: mm(P45[:, x, :], cc(G_G, x).to_broadcast([P, P]), upper[:], start=True, stop=True), "p")
                each(lambda x: nc.tensor.transpose(P67[:, x, :], kn[:, x, :], ident[:]), "p")
                each(lambda x: mm(P23[:, x, :], kn[:, x, :], qn[:, x, :], start=True, stop=True), "p")
                each(lambda x: mm(P01[:, x, :], kn[:, x, :], kb[:, x, :], start=True, stop=True), "p")
                pe.wait_ge(gd["kt"], i + 1)
                each(lambda x: nc.tensor.transpose(P67[:, x, :], vS[:, x, :], ident[:]), "vt")
                pe.wait_ge(gd["lt"], i + 1)
                each(lambda x: nc.tensor.transpose(P01[:, x, :], LT[:, x, :], ident[:]), "l")
                for s in range(1, 7):
                    pe.wait_ge(gd["b"], i * 6 + s)
                    pe.wait_ge(gd["ed"], i * 7 + s)
                    each(lambda x: mm(P01[:, x, :], B_[s % 2][:, x, :], E_[:, x, :], start=True, stop=True), "x")
                    if s in V_AT:
                        pe_fox_values(pe, i, *V_AT[s][0])
                    pe.wait_ge(gd["xc"], i * 6 + s)
                    if s < 6:
                        for x in range(2 * HA):
                            mm(P45[:, x, :], X_[:, x, :], D_[:, x, :], start=True, stop=True)
                    each(lambda x: mm(P23[:, x, :], D_[:, x, :], X_[:, x, :], start=True, stop=True), "e")
                    if s in V_AT:
                        pe_fox_values(pe, i, *V_AT[s][1])
                pe.wait_ge(gd["ed"], i * 7 + 7)
                pe.wait_ge(gd["kb"], i * 2 + 2)
                for x in range(2 * HA):
                    mm(P01[:, x, :], E_[:, x, :], vb[:, x, :], start=True, stop=True)
                each(lambda x: mm(P23[:, x, :], kbg[:, x, :], E_[:, x, :], start=True, stop=True), "u")
                pe.wait_ge(gd["uc"], i * 2 + 2)
                for a in range(2):
                    hs = range(4 * a, 4 * a + 4)
                    pe.wait_ge(gd["s"], i * 2 + (a + 1))
                    each(lambda x: mm(P45[:, x % 4, :], wT[:, x, :], S_[:, x % 4, :], start=True, stop=True), "ws", hs)
                    pe.wait_ge(gd["vn"], i * 2 + (a + 1))
                    pe.wait_ge(gd["oc"], i * 2 + (a + 1))
                    pe.wait_ge(fs["pvc"], i * 2 + 2)
                    for x in hs:
                        mm(P67[:, x % 4, :], kd[:, x, :], vn[:, x, :], start=True, stop=True)
                        mm(P45[:, 4 + x % 4, :], S_[:, x % 4, :], qg[:, x, :], start=True, stop=False)
                        ins = mm(P45[:, 4 + x % 4, :], vn[:, x, :], AT[:, x, :], start=False, stop=True)
                    ins.then_inc(gd["o"], 1)

        def act_gdn(act):
            act.sem_inc(gd["oc"], 1)
            with act.Fori(0, QT // 2) as i:
                act.wait_ge(gd["p"], i * 4 + 2)
                nc.scalar.activation(ktok, P67, ACT.Copy).then_inc(gd["kt"], 1)
                act.wait_ge(gd["dt"], i + 1)
                nc.scalar.activation(DT, DT, ACT.Exp).then_inc(gd["ex"], 1)
                act.wait_ge(gd["l"], i + 1)
                nc.scalar.activation(L_, P01, ACT.Copy).then_inc(gd["lc"], 1)
                for s in range(1, 7):
                    act.wait_ge(gd["x"], i * 6 + s)
                    nc.scalar.activation(X_, P01, ACT.Copy).then_inc(gd["xc"], 1)
                    if s == 3:
                        act_fox_values(act, i, 0)
                    if s == 5:
                        act_fox_values(act, i, 1)
                act.wait_ge(gd["u"], i + 1)
                nc.scalar.activation(u_, P01, ACT.Copy).then_inc(gd["uc"], 1)
                nc.scalar.activation(wT, P23, ACT.Copy).then_inc(gd["uc"], 1)
                for a in range(2):
                    act.wait_ge(gd["o"], i * 2 + (a + 1))
                    nc.scalar.activation(big[:, 8:12, ds(i * 256 + a * P, P)], P45[:, 4:8, :], ACT.Copy)\
                        .then_inc(gd["oc"], 1)

        def dve_gdn(dve):
            vv = nc.vector
            link = S["dve"].link
            dve.wait_ge(l2_rt, 2)
            vv.memset(S_, 0.0).then_inc(gd["s"], 1)
            with S["dve"].loop(QT // 2, 16) as i:
                link = S["dve"].link
                dve.wait_ge(gd["s"], i * 2 + 1)
                for n, (to, src, lo, bc) in enumerate(((qn, big, 0, P01), (kn, big, 4, P23), (qg, big, 0, P45),
                                                      (kb, big, 4, P67))):
                    dve.wait_ge(gd["bc"], i * 4 + (n + 1))
                    x = src[:, lo:lo + 4, ds(i * 256, 256)].rearrange("p h (a n) -> p a h n", a=2)
                    vv.tensor_tensor(split(to), x, split(bc), ALU.mult).then_inc(gd["n"], 1)
                dve.wait_ge(gd["p"], i * 4 + 1)
                for x in range(2 * HA):
                    ins = vv.scalar_tensor_tensor(out=DT[:, x, :], in0=P45[:, x, :], scalar=cc(G_GC, x), in1=neg_ji[:],
                                                  op0=ALU.subtract, op1=ALU.add)
                    if x < 2 * HA - 1:
                        link(ins)
                ins.then_inc(gd["dt"], 1)
                dve.wait_ge(gd["p"], i * 4 + 4)
                dve.wait_ge(gd["ex"], i + 1)
                link(vv.tensor_tensor(AT, P23, DT, ALU.mult))
                link(vv.tensor_tensor(DT, DT, over8(strict[:, :]), ALU.mult))
                vv.tensor_tensor(LT, P01, DT, ALU.mult).then_inc(gd["lt"], 1)
                dve.wait_ge(gd["vt"], i + 1)
                link(vv.tensor_tensor(split(vb), split(P67), per_token(G_B), ALU.mult))
                dve.wait_ge(gd["lt"], i + 1)
                link(vv.tensor_tensor(E_, LT, over8(lev0T[:, :]), ALU.mult))
                link(vv.tensor_tensor(E_, over8(ident[:, :]), E_, ALU.subtract))
                dve.wait_ge(gd["lc"], i + 1)
                link(vv.tensor_tensor(D_, L_, over8(lev[:, 0, :]), ALU.mult))
                vv.tensor_tensor(D_, over8(ident[:, :]), D_, ALU.subtract).then_inc(gd["ed"], 1)
                for s in range(1, 7):
                    dve.wait_ge(gd["e"], i * 6 + s)
                    dve.wait_ge(gd["ed"], i * 7 + s)
                    if s < 6:
                        vv.tensor_tensor(D_, D_, P45, ALU.subtract)
                    vv.tensor_tensor(E_, E_, P23, ALU.subtract).then_inc(gd["ed"], 1)
                for a in range(2):
                    dve.wait_ge(gd["ws"], i * 2 + (a + 1))
                    dve.wait_ge(gd["uc"], i * 2 + 2)
                    vv.tensor_tensor(vn[:, 4 * a:4 * a + 4, :], u_[:, 4 * a:4 * a + 4, :], P45[:, 0:4, :], ALU.subtract)\
                        .then_inc(gd["vn"], 1)
                    dve.wait_ge(gd["o"], i * 2 + (a + 1))
                    for h in range(HA):
                        ins = vv.scalar_tensor_tensor(out=S_[:, h, :], in0=S_[:, h, :], scalar=cc(G_EL, 4 * a + h),
                                                      in1=P67[:, h, :], op0=ALU.mult, op1=ALU.add)
                        if h < HA - 1 and a == 0:
                            link(ins)
                    ins.then_inc(gd["s"], 1)

        gs = {n: sem("gs_" + n) for n in ("st", "cb", "n", "ps", "vn", "vr", "out")}
        NS = HA * NB
        st = part(hTf, 0, NB, HA, P)
        g_cb = part(wk, 4400, 6, HA, NB)
        g_q, g_k, g_vb, g_qk, g_vn = (part(wk, 4600 + 32 * n, HA, NB) for n in range(5))
        g_pair = part(wk, 4800, HA, NB, 2)
        KINDS = (G_RQ, G_RK, G_RQE, G_BE, G_B, G_EL)

        def pool_gdn_rows(pool):
            pool.wait_ge(gd["s"], QT + 1)
            store(pool, gdn_p, S_)
            pool.dma_start(st.rearrange("p b h n -> p (b h) n"), st_gdn.rearrange("b h p n -> p (b h) n"))\
                .then_inc(gs["st"], 16)
            pool.wait_ge(fs["out"], 2)
            pool.dma_start(xT[:], xT_in).then_inc(fs["back"], 16)

        def pe_gdn_rows(pe):
            pe.wait_ge(gd["oc"], QT + 1)
            for n, kind in enumerate(KINDS):
                for h in range(HA):
                    ins = nc.tensor.matmul(ps[:, 7, (n * HA + h) * NB:(n * HA + h + 1) * NB],
                                           gt[:, QT, kind, h:h + 1].to_broadcast([P, P]), ident[:, P - NB:P],
                                           start=True, stop=True)
            ins.then_inc(gs["cb"], 1)
            pe.wait_ge(gs["st"], 16)
            pe.wait_ge(gs["n"], 1)
            for h in range(HA):
                for b in range(NB):
                    nc.tensor.matmul(ps[:, 6, 2 * (h * NB + b):2 * (h * NB + b) + 2], st[:, b, h, :], g_pair[:, h, b, :],
                                     start=True, stop=True)
            nc.tensor.matmul(ps[:, 7, 256:288], ones[:], g_qk.rearrange("p h b -> p (h b)"), start=True, stop=True)\
                .then_inc(gs["ps"], 1)
            pe.wait_ge(gs["vn"], 1)
            for h in range(HA):
                for b in range(NB):
                    x = b * HA + h
                    ins = nc.tensor.matmul(psf[:, x * P:x * P + P], g_vn[:, h, b:b + 1].to_broadcast([P, P]), ident[:],
                                           start=True, stop=True)
            ins.then_inc(gs["vr"], 1)

        def dve_gdn_rows(dve):
            link, vv = S["dve"].link, nc.vector
            dve.wait_ge(gs["cb"], 1)
            link(vv.tensor_copy(g_cb, ps[:, 7, 0:192].rearrange("p (n h b) -> p n h b", n=6, b=NB)))
            cols = big[:, :, SEQ:T]
            link(vv.tensor_tensor(g_q, cols[:, 0:4], g_cb[:, 0], ALU.mult))
            link(vv.tensor_tensor(g_k, cols[:, 4:8], g_cb[:, 1], ALU.mult))
            link(vv.tensor_tensor(g_pair[:, :, :, 1], cols[:, 0:4], g_cb[:, 2], ALU.mult))
            link(vv.tensor_tensor(g_pair[:, :, :, 0], g_k, g_cb[:, 3], ALU.mult))
            link(vv.tensor_tensor(g_vb, cols[:, 8:12], g_cb[:, 4], ALU.mult))
            vv.tensor_tensor(g_qk, g_q, g_k, ALU.mult).then_inc(gs["n"], 1)
            dve.wait_ge(gs["ps"], 1)
            pr = ps[:, 6, 0:2 * NS].rearrange("p (h b t) -> p h b t", b=NB, t=2)
            qk = ps[:, 7, 256:288].rearrange("p (h b) -> p h b", b=NB)
            link(vv.tensor_tensor(g_vn, g_vb, pr[:, :, :, 0], ALU.subtract))
            link(vv.tensor_tensor(g_qk, qk, g_vn, ALU.mult))
            vv.tensor_tensor(cols[:, 8:12], g_qk, pr[:, :, :, 1], ALU.add).then_inc(gs["vn"], 1)
            dve.wait_ge(gs["vr"], 1)
            for h in range(HA):
                for b in range(NB):
                    link(vv.tensor_scalar(st[:, b, h, :], st[:, b, h, :], g_cb[:, 5, h, b:b + 1], None, ALU.mult))
                    x = b * HA + h
                    ins = vv.scalar_tensor_tensor(out=st[:, b, h, :], in0=psf[:, x * P:x * P + P],
                                                  scalar=g_k[:, h, b:b + 1], in1=st[:, b, h, :], op0=ALU.mult, op1=ALU.add)
                    if x < NS - 1:
                        link(ins)
            ins.then_inc(gs["out"], 1)

        gn = {n: sem("gn_" + n) for n in ("rc", "bc", "u")}
        n_t = part(wk, 2300, 2, T)

        def pe_head_norm(pe):
            pe.wait_ge(gs["out"], 1)
            pe_squares(pe, 8, HA)
            pe.wait_ge(gn["rc"], 1)
            for h in range(HA):
                if h >= 2:
                    pe.wait_ge(gn["u"], h - 1)
                base = 1536 * (h % 2)
                for t in range(9):
                    cnt = P if t < QT else NB
                    ins = nc.tensor.matmul(psf[:, base + t * P:base + t * P + cnt],
                                           l_rc[:, h * 9 + t:h * 9 + t + 1].to_broadcast([P, P]), ident[:, P - cnt:P],
                                           start=True, stop=True)
                ins.then_inc(gn["bc"], 1)

        def dve_head_norm(dve):
            link, vv = S["dve"].link, nc.vector
            dve.wait_ge(l2_rt, 3)
            vv.reciprocal(l_rc[:, 0:36], l_st[:, 0:36]).then_inc(gn["rc"], 1)
            for h in range(HA):
                dve.wait_ge(gn["bc"], h + 1)
                if h >= 2:
                    dve.wait_ge(gn["u"], h - 1)
                link(vv.scalar_tensor_tensor(out=n_t[:, h % 2], in0=big[:, 8 + h, :], scalar=v("gnorm"),
                                             in1=psf[:, 1536 * (h % 2):1536 * (h % 2) + T], op0=ALU.mult, op1=ALU.mult))
                vv.tensor_tensor(aT[:, h, :], aT[:, h, :], n_t[:, h % 2], ALU.mult).then_inc(gn["u"], 1)

        def residual(dve, name, pairs):
            dve.wait_ge(psum_free, GROUP0[name])
            epilogue(dve, name, pairs, lambda i, j, st: nc.vector.tensor_tensor(
                at_chunk(xT, i * 4 + j), at_chunk(xT, i * 4 + j), psum_set(st), ALU.add))

        q32 = la[:, 0:XW].rearrange("p (c t) -> p c t", c=KC)
        m_raw, m_n = part(la, 0, KC, NMEM), part(la, 2048, KC, NMEM)
        m_k, m_v = part(la, XW, KC, NMEM), part(la, XW + 2048, 2, D)
        x_ring = part(la, 12352, 2, 2, D)
        xa = {n: sem("xa_" + n) for n in ("mem", "q", "qs", "s", "m", "e", "p", "t", "tc", "o", "oc", "col",
                                          "qb", "qbc", "oh", "free", "mx", "mt", "mc", "mb", "sh", "ex", "sum", "tot", "pr", "pv",
                                          "pvc", "ring0", "ring1", "vr0", "vr1")}
        x_q = part(la, 2 * XW, 2, KC, P)
        x_p = part(la, 12352, 2, HX, NMEM)
        x_t = part(la, 14400, 2, KC, P)
        x_st = part(la, 18576, 2, 3, HX)
        r_qb, r_prod = part(la, 2 * XW, 2, D), part(la, XW, 2, D)
        r_sc = part(la, 18624, NB, 2, HX)
        r_mx, r_mb, r_sum, r_rs = (part(la, 18720 + 32 * n, NB, HX) for n in range(4))
        r_mc, r_col = part(la, 18860, 1), part(la, 18870, 2, KC)

        cat_hi, cat_lo, mix_free = sem("cat_hi"), sem("cat_lo"), sem("mix_free")

        def act_cat(act):
            act.wait_ge(mix_free, 1)
            for c in range(KC):
                nc.scalar.activation(h_hi[:, c, :], aT[:, c, :], ACT.Copy).then_inc(cat_hi, 1)

        def dve_cat(dve):
            for c in range(KC):
                dve.wait_ge(cat_hi, c + 1)
                nc.vector.tensor_tensor(h_lo[:, c, :], aT[:, c, :], h_hi[:, c, :].bitcast(F32), ALU.subtract)\
                    .then_inc(cat_lo, 1)

        def pe_memory(pe, l):
            for name in (f"mk{l}", f"mv{l}"):
                t0, g0 = TILE0[name], GROUP0[name]
                with pe.Fori(0, 2) as i:
                    for j in range(4):
                        pe.wait_ge(w_loaded[j % 2], i * 32 + 16 * (NPAIRS + (t0 + j) // 2 + 1))
                        pe.wait_ge(psum_free, i * 4 + (g0 + j - 1))
                        if name[1] == "k":
                            for k in range(KC):
                                ins = nc.tensor.matmul(ps[:, 3 * (j % 2), 0:NMEM], w_raw[:, j % 2, k, :], m_n[:, k, :],
                                                       start=(k == 0), stop=(k == KC - 1))
                        else:
                            for m in range(2):
                                for k in range(KC):
                                    ins = nc.tensor.matmul(ps[:, 3 * (j % 2), m * P:(m + 1) * P],
                                                           m_n[:, k, m * P:(m + 1) * P], w_raw[:, j % 2, k, :],
                                                           start=(k == 0), stop=(k == KC - 1))
                        ins.then_inc(psum_ready, 1)

        def pool_cross(pool, l):
            pool.dma_start(m_raw, memT_in).then_inc(xa["mem"], 16)
            if l == 0:
                pool_split(pool, 2, TILE0["out"] + 8)
            pool_hand_back(pool, f"mk{l}")
            pool_hand_back(pool, f"mv{l}")
            pool.wait_ge(*freed(f"mv{l}", 2))
            store(pool, mkT[l].rearrange("(c p) m -> p c m", p=P), m_k)
            store(pool, mv[l].rearrange("(t p) n -> p t n", p=P), m_v)
            split_tiles(pool, f"xq{l}")
            xo = TILE0[f"xo{l}"]
            pool_split(pool, xo, xo + 2)
            pool.wait_ge(*freed(f"xq{l}", 2))
            for e in range(2):
                nc.gpsimd.tensor_copy(x_q[:, e], q32[:, :, e * P:(e + 1) * P]).then_inc(xa["qs"], 1)
            with pool.Fori(0, 3) as r:
                for e in range(2):
                    pool.wait_ge(xa["s"], r * 2 + (8 * l + e + 1))
                    nc.gpsimd.tensor_copy(x_q[:, e], q32[:, :, ds(r * 256 + (2 + e) * P, P)]).then_inc(xa["qs"], 1)
            pool.wait_ge(stored, 16 * n_stored[0])
            pool.wait_ge(xa["oc"], 8 * l + 10)

            def ring_loop(src, done, used):
                with pool.Fori(0, NB // 2) as r:
                    for s in range(2):
                        pool.wait_ge(xa["free"], r * 2 + (16 * l + used + s + 1))
                        pool.dma_start(x_ring[:, s], src[l, ds(r * 2 + s, 1)].rearrange("a (t p) n -> p (a t) n", p=P))\
                            .then_inc(xa[f"{done}{s}"], 16)

            ring_loop(cmk, "ring", 0)
            ring_loop(cmv, "vr", NB)
            pool_split(pool, xo + 2, xo + 8)
            split_tiles(pool, f"up{l}0", f"down{l}{FF_GROUPS - 1}")

        def pe_cross(pe, l):
            mm = nc.tensor.matmul

            def scores(r, e, ahead=0):
                n = 8 * l + e + ahead
                pe.wait_ge(xa["qs"], r * 2 + (n + 1))
                pe.wait_ge(xa["e"], r * 2 + (n + 1))
                for h in range(HX):
                    for c in range(2):
                        ins = mm(psf[:, e * 1024 + h * 256:e * 1024 + h * 256 + 256], x_q[:, e, 2 * h + c, :],
                                 m_k[:, 2 * h + c, :], start=(c == 0), stop=(c == 1))
                ins.then_inc(xa["s"], 1)

            def turn(r, e):
                pe.wait_ge(xa["p"], r * 2 + (8 * l + e + 1))
                pe.wait_ge(xa["tc"], r * 2 + (8 * l + e + 1))
                for h in range(HX):
                    for m in range(2):
                        ins = nc.tensor.transpose(psf[:, 2048 + (2 * h + m) * P:2048 + (2 * h + m + 1) * P],
                                                  x_p[:, e, h, m * P:(m + 1) * P], ident[:])
                ins.then_inc(xa["t"], 1)

            def values(r, e):
                pe.wait_ge(xa["tc"], r * 2 + (8 * l + e + 2))
                pe.wait_ge(xa["oc"], r * 2 + (8 * l + e + 2))
                for c in range(KC):
                    for m in range(2):
                        ins = mm(psf[:, 3072 + c * P:3072 + (c + 1) * P], m_v[:, m, c * P:(c + 1) * P],
                                 x_t[:, e, 2 * (c // 2) + m, :], start=(m == 0), stop=(m == 1))
                ins.then_inc(xa["o"], 1)

            pe.wait_ge(*freed(f"xq{l}", 2))
            scores(0, 0)
            with pe.Fori(0, 3) as r:
                turn(r, 0)
                scores(r, 1)
                values(r, 0)
                turn(r, 1)
                scores(r, 0, 2)
                values(r, 1)
            turn(3, 0)
            scores(3, 1)
            values(3, 0)
            turn(3, 1)
            values(3, 1)
            pe.wait_ge(xa["oc"], 8 * l + 10)
            with pe.Fori(0, NB // 2) as r:
                for s in range(2):
                    pe.wait_ge(xa["col"], r * 2 + (8 * l + s + 1))
                    for c in range(KC):
                        ins = mm(psf[:, c * P:(c + 1) * P], r_col[:, s, c:c + 1].to_broadcast([P, P]), ident[:],
                                 start=True, stop=True)
                    ins.then_inc(xa["qb"], 1)
            pe.wait_ge(xa["mx"], l + 1)
            nc.tensor.transpose(ps[0:32, 2, 0:P], r_mx.rearrange("p b h -> p (b h)"), ident[:]).then_inc(xa["mt"], 1)
            pe.wait_ge(xa["mc"], l + 1)
            mm(ps[:, 3, 0:32], r_mc[0:32, :].to_broadcast([32, P]), ident[0:32, 0:32], start=True, stop=True)\
                .then_inc(xa["mb"], 1)
            pe.wait_ge(xa["sum"], l + 1)
            mm(ps[:, 2, 128:160], ones[:], r_sum.rearrange("p b h -> p (b h)"), start=True, stop=True).then_inc(xa["tot"], 1)
            pe.wait_ge(xa["pr"], l + 1)
            with pe.Fori(0, NB // 2) as r:
                for s in range(2):
                    pe.wait_ge(xa[f"vr{s}"], r * 16 + 16 * (4 * l + 1))
                    pe.wait_ge(xa["pvc"], r * 2 + (8 * l + s + 1))
                    for c in range(KC):
                        for m in range(2):
                            ins = mm(ps[:, 4 + s, c:c + 1], x_ring[:, s, m, c * P:(c + 1) * P],
                                     r_sc[:, ds(r * 2 + s, 1), m, c // 2:c // 2 + 1].rearrange("p a h -> p (a h)"),
                                     start=(m == 0), stop=(m == 1))
                    ins.then_inc(xa["pv"], 1)
            pe.wait_ge(xa["pvc"], 8 * l + 2 + NB)

        def act_cross(act, l):
            if l == 0:
                for k, n in (("e", 2), ("tc", 1), ("oc", 2), ("pvc", 2)):
                    act.sem_inc(xa[k], n)
            def exps(r, e, ahead=0):
                act.wait_ge(xa["m"], r * 2 + (8 * l + e + ahead + 1))
                for h in range(HX):
                    ins = nc.scalar.activation(x_p[:, e, h, :], psf[:, e * 1024 + h * 256:e * 1024 + h * 256 + 256],
                                               ACT.Exp, bias=x_st[:, e, 0, h:h + 1], accum_out=x_st[:, e, 1, h:h + 1])
                ins.then_inc(xa["e"], 1)

            def turned(r, e):
                act.wait_ge(xa["t"], r * 2 + (8 * l + e + 1))
                nc.scalar.activation(x_t[:, e], psf[:, 2048:3072].rearrange("p (a n) -> p a n", n=P), ACT.Copy)\
                    .then_inc(xa["tc"], 1)

            def out(r, e):
                act.wait_ge(xa["o"], r * 2 + (8 * l + e + 1))
                nc.scalar.activation(h_hi[:, :, ds(r * 256 + e * P, P)],
                                     psf[:, 3072:4096].rearrange("p (c n) -> p c n", n=P), ACT.Copy).then_inc(xa["oh"], 1)

            exps(0, 0)
            with act.Fori(0, 3) as r:
                turned(r, 0)
                exps(r, 1)
                out(r, 0)
                turned(r, 1)
                exps(r, 0, 2)
                out(r, 1)
            turned(3, 0)
            exps(3, 1)
            out(3, 0)
            turned(3, 1)
            out(3, 1)
            with act.Fori(0, NB // 2) as r:
                for s in range(2):
                    act.wait_ge(xa["qbc"], r * 2 + (8 * l + s + 1))
                    nc.scalar.activation(r_col[:, s], q32[:, :, ds(r * 2 + (SEQ + s), 1)].rearrange("p c a -> p (c a)"),
                                         ACT.Copy).then_inc(xa["col"], 1)
                    act.wait_ge(xa["qb"], r * 2 + (8 * l + s + 1))
                    nc.scalar.activation(r_qb[:, s], psf[:, 0:D], ACT.Copy).then_inc(xa["q"], 1)
            act.wait_ge(xa["sh"], l + 1)
            nc.scalar.activation(r_sc, r_sc, ACT.Exp).then_inc(xa["ex"], 1)
            with act.Fori(0, NB // 2) as r:
                for s in range(2):
                    act.wait_ge(xa["pv"], r * 2 + (8 * l + s + 1))
                    nc.scalar.activation(h_hi[:, :, ds(r * 2 + (SEQ + s), 1)].rearrange("p c a -> p (c a)"),
                                         ps[:, 4 + s, 0:KC], ACT.Copy).then_inc(xa["oh"], 1)

        def dve_cross(dve, l):
            vv = nc.vector
            def soft(r, e, ahead=0):
                n = 8 * l + e + ahead
                dve.wait_ge(xa["s"], r * 2 + (n + 1))
                vv.tensor_reduce(x_st[:, e, 0, :], psf[:, e * 1024:e * 1024 + 1024].rearrange("p (h n) -> p h n", h=HX),
                                 AX.X, ALU.max, negate=True).then_inc(xa["m"], 1)
                dve.wait_ge(xa["e"], r * 2 + (n + 3))
                S["dve"].link(vv.reciprocal(x_st[:, e, 2, :], x_st[:, e, 1, :]))
                rs = x_st[:, e, 2, :].rearrange("p (h n) -> p h n", n=1).to_broadcast([P, HX, NMEM])
                vv.tensor_tensor(x_p[:, e], x_p[:, e], rs, ALU.mult).then_inc(xa["p"], 1)

            def rest(r, e):
                cols = slice(None), slice(None), ds(r * 256 + e * P, P)
                dve.wait_ge(xa["oh"], r * 2 + (16 * l + e + 1))
                vv.tensor_tensor(h_lo[cols], psf[:, 3072:4096].rearrange("p (c n) -> p c n", n=P),
                                 h_hi[cols].bitcast(F32), ALU.subtract).then_inc(xa["oc"], 1)

            soft(0, 0)
            with S["dve"].loop(3, 2) as r:
                soft(r, 1)
                rest(r, 0)
                soft(r, 0, 2)
                rest(r, 1)
            soft(3, 1)
            rest(3, 0)
            rest(3, 1)
            link = S["dve"].link
            dve.wait_ge(xa["oc"], 8 * l + 10)
            if l == 0:
                dve.sem_inc(xa["qbc"], 2)
                dve.sem_inc(xa["free"], 2)
            with S["dve"].loop(NB // 2, 2) as r:
                link = S["dve"].link
                for s in range(2):
                    dve.wait_ge(xa["q"], r * 2 + (8 * l + s + 1))
                    dve.wait_ge(xa[f"ring{s}"], r * 16 + 16 * (4 * l + 1))
                    dve.wait_ge(xa["qbc"], r * 2 + (8 * l + s + 2))
                    link(vv.tensor_tensor(r_prod, x_ring[:, s], r_qb[:, s].rearrange("p (a n) -> p a n", a=1).to_broadcast([P, 2, D]),
                                          ALU.mult))
                    dve.sem_inc(xa["free"], 1)
                    vv.tensor_reduce(r_sc[:, ds(r * 2 + s, 1), :, :].rearrange("p a m h -> p (a m h)"),
                                     r_prod.rearrange("p m (h n) -> p (m h) n", n=DHX), AX.X, ALU.add).then_inc(xa["qbc"], 1)
            link = S["dve"].link
            dve.wait_ge(xa["qbc"], 8 * l + 10)
            vv.tensor_reduce(r_mx, r_sc.rearrange("p b m h -> p b h m"), AX.X, ALU.max).then_inc(xa["mx"], 1)
            dve.wait_ge(xa["mt"], l + 1)
            vv.tensor_reduce(r_mc[0:32, :], ps[0:32, 2, 0:P], AX.X, ALU.max).then_inc(xa["mc"], 1)
            dve.wait_ge(xa["mb"], l + 1)
            link(vv.tensor_copy(r_mb, ps[:, 3, 0:32].rearrange("p (b h) -> p b h", h=HX)))

            def over_mem(x):
                return x.rearrange("p b (a h) -> p b a h", a=1).to_broadcast([P, NB, 2, HX])

            vv.tensor_tensor(r_sc, r_sc, over_mem(r_mb), ALU.subtract).then_inc(xa["sh"], 1)
            dve.wait_ge(xa["ex"], l + 1)
            vv.tensor_reduce(r_sum, r_sc.rearrange("p b m h -> p b h m"), AX.X, ALU.add).then_inc(xa["sum"], 1)
            dve.wait_ge(xa["tot"], l + 1)
            link(vv.reciprocal(r_rs, ps[:, 2, 128:160].rearrange("p (b h) -> p b h", h=HX)))
            vv.tensor_tensor(r_sc, r_sc, over_mem(r_rs), ALU.mult).then_inc(xa["pr"], 1)
            with dve.Fori(0, NB // 2) as r:
                for s in range(2):
                    dve.wait_ge(xa["pv"], r * 2 + (8 * l + s + 1))
                    dve.sem_inc(xa["free"], 1)
                    dve.wait_ge(xa["oh"], r * 2 + (16 * l + 8 + s + 1))
                    col = slice(None), slice(None), ds(r * 2 + (SEQ + s), 1)
                    vv.tensor_tensor(h_lo[col].rearrange("p c a -> p (c a)"), ps[:, 4 + s, 0:KC],
                                     h_hi[col].rearrange("p c a -> p (c a)").bitcast(F32), ALU.subtract)\
                        .then_inc(xa["pvc"], 1)

        ff_sq, ff_hi, ff_lo = sem("ff_sq"), sem("ff_hi"), sem("ff_lo")

        def act_up(act, l, g):
            name = f"up{l}{g}"
            g0 = GROUP0[name]
            n0 = 8 * (FF_GROUPS * l + g)
            act.wait_ge(psum_free, g0)
            if n0 == 0:
                act.sem_inc(ff_lo, 2)
            with act.Fori(0, 2) as i:
                for j in range(4):
                    act.wait_ge(ff_lo, i * 4 + (n0 + j + 1))
                    act.wait_ge(psum_ready, i * 4 + (g0 + j + 1))
                    nc.scalar.activation(thirds(tt[:, j % 2]), psum_set(j % 2), ACT.Relu).then_inc(psum_free, 1)
                    act.wait_ge(ff_sq, i * 4 + (n0 + j + 1))
                    nc.scalar.activation(a_hi[:, ds(i * 4 + j, 1), :].rearrange("p a n -> p (a n)"), tt[:, j % 2], ACT.Copy)\
                        .then_inc(ff_hi, 1)

        def dve_up(dve, l, g):
            g0 = GROUP0[f"up{l}{g}"]
            n0 = 8 * (FF_GROUPS * l + g)
            with dve.Fori(0, 2) as i:
                for j in range(4):
                    dve.wait_ge(psum_free, i * 4 + (g0 + j + 1))
                    nc.vector.tensor_tensor(tt[:, j % 2], tt[:, j % 2], tt[:, j % 2], ALU.mult).then_inc(ff_sq, 1)
                    dve.wait_ge(ff_hi, i * 4 + (n0 + j + 1))
                    chunk = slice(None), ds(i * 4 + j, 1), slice(None)
                    nc.vector.tensor_tensor(a_lo[chunk].rearrange("p a n -> p (a n)"), tt[:, j % 2],
                                            a_hi[chunk].rearrange("p a n -> p (a n)").bitcast(F32), ALU.subtract)\
                        .then_inc(ff_lo, 1)

        def by_chunk(sem_, base):
            return lambda pe, k: pe.wait_ge(sem_, base + k + 1)

        def at_once(*pairs):
            return lambda pe, k: after(*pairs)(pe) if k == 0 else None

        def pe_mlp(pe, l):
            for g in range(FF_GROUPS):
                pe_product3(pe, f"up{l}{g}", 2, h_hi, h_lo, by_chunk(nm_out, OUT0[F_NORM[l]]))
                pe_product3(pe, f"down{l}{g}", 2, a_hi, a_lo, by_chunk(ff_lo, 8 * (FF_GROUPS * l + g) + 2))

        cm = {n: sem("cm_" + n) for n in ("pad", "st", "glu", "out", "sum", "ps", "mean", "bc", "cp", "xc")}
        GW = CC - 1 + T
        glu = part(la, 0, KC, GW)
        d_sg = part(la, KC * GW, 2, T)
        d_st = part(la, KC * GW + 2 * T, KC, NB, CC - 1)
        d_y = part(la, 12480, SEQ)
        d_tmp = part(la, 13504, NB, CC - 1)
        d_s8 = part(la, 13744, NB)
        d_tail = part(la, 18600, KC, CC - 1 + NB)
        glu_y = glu[:, :, 0:T]

        def pool_conformer(pool):
            pool.wait_ge(nm_out, 40)
            nc.gpsimd.memset(glu[:, :, 0:CC - 1], 0.0).then_inc(cm["pad"], 1)
            pool.dma_start(d_st, st_cconv_in).then_inc(cm["st"], 16)

        def act_pw1(act):
            g0 = GROUP0["pw1"]
            b0 = VOFF["b_pw1"][0]
            act.wait_ge(psum_free, g0)
            act.wait_ge(cm["pad"], 1)
            act.wait_ge(nm_out, 40)
            with act.Fori(0, 4) as i:
                for j in range(4):
                    act.wait_ge(psum_ready, i * 4 + (g0 + j + 1))
                    h = j // 2
                    if j % 2 == 0:
                        nc.scalar.activation(thirds(glu[:, ds(i * 2 + h, 1), CC - 1:].rearrange("p a n -> p (a n)")),
                                             psum_set(0), ACT.Identity, bias=vec[:, ds(i * 2 + (b0 + h), 1)])\
                            .then_inc(psum_free, 1)
                    else:
                        act.wait_ge(cm["glu"], i * 2 + (h + 1))
                        nc.scalar.activation(thirds(d_sg[:, h, :]), psum_set(1), ACT.Sigmoid,
                                             bias=vec[:, ds(i * 2 + (b0 + 8 + h), 1)]).then_inc(psum_free, 1)

        def dve_conformer(dve):
            vv, g0 = nc.vector, GROUP0["pw1"]
            w0, bd = VOFF["w_dw"][0], VOFF["b_dw"][0]
            dve.sem_inc(cm["glu"], 2)
            dve.wait_ge(cm["st"], 16)
            with S["dve"].loop(4, 2 * 35) as i:
                link = S["dve"].link
                for j in range(2):
                    c = i * 2 + j
                    dve.wait_ge(psum_free, i * 4 + (g0 + 2 * j + 2))
                    x = glu[:, ds(c, 1), :].rearrange("p a n -> p (a n)")
                    vv.tensor_tensor(x[:, CC - 1:], x[:, CC - 1:], d_sg[:, j, :], ALU.mult).then_inc(cm["glu"], 1)
                    dve.wait_ge(cm["glu"], i * 2 + (j + 3))

                    def tap(t):
                        return vec[:, ds(c * CC + (w0 + t), 1)]

                    bias = vec[:, ds(c + bd, 1)]
                    wrow = vec[:, ds(c * CC + w0, CC - 1)].rearrange("p (a n) -> p a n", a=1).to_broadcast([P, NB, CC - 1])
                    link(vv.tensor_tensor(d_tmp, d_st[:, ds(c, 1)].rearrange("p a b n -> p (a b) n"), wrow, ALU.mult))
                    link(vv.tensor_reduce(d_s8, d_tmp, AX.X, ALU.add))
                    link(vv.scalar_tensor_tensor(out=d_s8, in0=x[:, CC - 1 + SEQ:], scalar=tap(CC - 1), in1=d_s8,
                                                 op0=ALU.mult, op1=ALU.add))
                    link(vv.tensor_scalar(d_tail[:, ds(c, 1), :].rearrange("p a n -> p (a n)"), x[:, SEQ:GW], 1.0, None,
                                          ALU.mult))
                    link(vv.tensor_scalar(d_y, x[:, 0:SEQ], tap(0), bias, ALU.mult, ALU.add))
                    for t in range(1, CC):
                        link(vv.scalar_tensor_tensor(out=d_y if t < CC - 1 else x[:, 0:SEQ], in0=x[:, t:t + SEQ],
                                                     scalar=tap(t), in1=d_y, op0=ALU.mult, op1=ALU.add))
                    vv.tensor_scalar(x[:, SEQ:T], d_s8, bias, None, ALU.add).then_inc(cm["out"], 1)
            link = S["dve"].link
            dve.wait_ge(cm["out"], 8)
            link(vv.tensor_tensor(acc1, glu_y[:, 0, :], glu_y[:, 1, :], ALU.add))
            for c in range(2, KC):
                ins = vv.tensor_tensor(acc1, acc1, glu_y[:, c, :], ALU.add)
                if c < KC - 1:
                    link(ins)
            ins.then_inc(cm["sum"], 1)
            dve.wait_ge(cm["cp"], 1)
            for c in range(KC):
                vv.tensor_tensor(glu_y[:, c, :], glu_y[:, c, :], rbc1, ALU.subtract).then_inc(cm["xc"], 1)

        def pe_mean(pe):
            pe.wait_ge(cm["sum"], 1)
            tl = tiles_of(T)
            for j, (at, cnt, skip, _) in enumerate(tl):
                ins = nc.tensor.matmul(ps[:, 6, j:j + 1], acc1[:, at:at + P], ones[:, 0:1], start=True, stop=True)
            ins.then_inc(cm["ps"], 1)
            pe.wait_ge(cm["mean"], 1)
            for j, (at, cnt, skip, to) in enumerate(tl):
                ins = nc.tensor.matmul(psf[:, to:to + cnt], sm[:, j:j + 1].to_broadcast([P, P]), ident[:, skip:skip + cnt],
                                       start=True, stop=True)
            ins.then_inc(cm["bc"], 1)

        def act_mean(act):
            act.wait_ge(cm["ps"], 1)
            nc.scalar.activation(sm[:, 0:9], ps[:, 6, 0:9], ACT.Copy, scale=1.0 / D).then_inc(cm["mean"], 1)
            act.wait_ge(cm["bc"], 1)
            nc.scalar.activation(rbc1, psf[:, 0:T], ACT.Copy).then_inc(cm["cp"], 1)

        copy_to = lambda dst, scale=1.0: (lambda i, j, st: nc.scalar.activation(at_chunk(dst, i * 4 + j), psum_set(st),
                                                                             ACT.Copy, scale=scale))

        def act_memory(act, l):
            act.wait_ge(psum_free, GROUP0[f"mk{l}"])
            epilogue(act, f"mk{l}", 2, lambda i, j, st: nc.scalar.activation(
                m_k[:, ds(i * 4 + j, 1), :].rearrange("p a n -> p (a n)"), ps[:, 3 * st, 0:NMEM], ACT.Copy))
            epilogue(act, f"mv{l}", 2, lambda i, j, st: nc.scalar.activation(
                m_v[:, :, ds(i * 512 + j * P, P)], ps[:, 3 * st, 0:256].rearrange("p (m n) -> p m n", m=2), ACT.Copy))

        block = ctx.enter_context(nc.Block())

        @block.sync
        def _(sp):
            sp_loads(sp)

        @block.gpsimd
        def _(pool):
            S["pool"] = Steps(pool, pool_steps)
            pool_consts(pool)
            pool_fox(pool)
            store(pool, fkT.rearrange("(c p) t -> p c t", p=P), kf)
            store(pool, fv[0:SEQ, :].rearrange("(t p) n -> p t n", p=P), vf)
            store(pool, fv[SEQ:T, :], vs)
            store(pool, flf[0:SEQ, :].rearrange("(t p) n -> p t n", p=P), lf[:, 0:QT, :])
            store(pool, flf[SEQ:T, :], lf[P - NB:P, QT, :])
            pool_fox_rows(pool)
            pool_conv(pool)
            pool_key_pages(pool)
            pool.wait_ge(conv_silu, 12)
            store(pool, gkeep, st_gconv_in.rearrange("p c j b -> p c (j b)")[:, :, NB:])
            store(pool, ckeep.rearrange("p c (b j) -> p c b j", b=NB), st_cconv_in[:, :, :, 1:])
            store(pool, gconv, c_tail)
            pool_gdn(pool)
            pool_gdn_rows(pool)
            pool.wait_ge(gs["out"], 1)
            store(pool, gdn_s, st.rearrange("p b h n -> p (b h) n"))
            pool.wait_ge(gn["u"], 4)
            pool.wait_ge(stored, 16 * n_stored[0])
            pool.sem_inc(mix_free, 1)
            pool_split(pool, 0, 2)
            pool.wait_ge(cat_lo, 8)
            pool_cross(pool, 0)
            pool_split(pool, TILE0["pw1"], TILE0["pw1"] + 2)
            pool_conformer(pool)
            pool_split(pool, TILE0["pw1"] + 2, TILE0["pw2"] + 2)
            pool.wait_ge(cm["out"], 8)
            store(pool, cconv, d_tail)
            pool_split(pool, TILE0["pw2"] + 2, TILE0["pw2"] + 8)
            pool.wait_ge(stored, 16 * n_stored[0])
            pool.wait_ge(nm_out, 48)
            pool_cross(pool, 1)
            pool.wait_ge(nm_out, 80)
            store(pool, yT.rearrange("p (c t) -> p c t", c=KC), y_out[:])
            pool.wait_ge(stored, 16 * n_stored[0])

        @block.scalar
        def _(act):
            S["act"] = Steps(act, act_steps)
            act.wait_ge(consts_ready, 1)

            def once(*pairs):
                return lambda eng, c: after(*pairs)(eng) if c == 0 else None

            def behind(name):
                return lambda eng, c: eng.wait_ge(psum_free, GROUP0[name] + c + 1)

            act_norm(act, 0, xT, T, once((in_loaded, 80)))
            act_values(act)
            act_gates(act)
            epilogue(act, "k_fox", 1, copy_to(kf))
            act_gate_sums(act)
            epilogue(act, "q_fox", 1, copy_to(qf, float(DHB) ** -0.5))
            act_fox(act)
            act_fox_rows(act)
            act_conv(act)
            epilogue(act, "z", 1, lambda i, j, st: nc.scalar.activation(at_chunk(aT, i * 4 + j), psum_set(st), ACT.Silu))
            act_fox_soft(act)
            act_squares(act, big, 8, 1.0)
            act_gdn(act)
            l2_n[0] = 8
            act.wait_ge(gs["vn"], 1)
            act_squares(act, big[:, 8:12, :], HA, 1.0 / P)
            act_cat(act)

            def cross(l):
                act_norm(act, X_NORM[l], xT, T, behind(("out", "pw2")[l]))
                act_norm(act, M_NORM[l], m_raw, NMEM, once((xa["mem"], 16 * (l + 1))))
                act_scale(act, X_NORM[l])
                act_memory(act, l)
                epilogue(act, f"xq{l}", 2, copy_to(q32, float(DHX) ** -0.5))
                act_cross(act, l)

            def mlp(l):
                act_norm(act, F_NORM[l], xT, T, behind(f"xo{l}"))
                act_scale(act, F_NORM[l])
                for g in range(FF_GROUPS):
                    act_up(act, l, g)

            cross(0)
            mlp(0)
            act_norm(act, 4, xT, T, behind("down03"))
            act_scale(act, 4)
            act_pw1(act)
            act_mean(act)
            act_norm(act, 5, glu_y, T, lambda eng, c: eng.wait_ge(cm["xc"], c + 1))
            act_scale(act, 5)
            cross(1)
            mlp(1)
            act_norm(act, 9, xT, T, behind("down13"))

        @block.vector
        def _(dve):
            S["dve"] = Steps(dve, dve_steps)
            dve.wait_ge(consts_ready, 1)
            dve_norm(dve, 0, T)
            dve_scale(dve, 0, xT, hT, T, "norm_mix0")
            dve_gates(dve)
            dve_fox(dve)
            dve_fox_rows(dve)
            dve_conv(dve)
            dve_fox_soft(dve)
            dve_norm_gates(dve)
            dve_gdn(dve)
            dve_fox_out(dve)
            dve_gdn_rows(dve)
            dve_head_norm(dve)
            dve_cat(dve)

            def cross(l):
                if l == 0:
                    dve.wait_ge(fs["back"], 16)
                dve_norm(dve, X_NORM[l], T, ("out", "pw2")[l])
                dve_norm(dve, M_NORM[l], NMEM)
                dve_scale(dve, M_NORM[l], m_raw, m_n, NMEM, f"norm_mem{l}")
                dve_scale(dve, X_NORM[l], xT, None, T, f"norm_x{l}")
                dve_cross(dve, l)

            def mlp(l):
                dve_norm(dve, F_NORM[l], T, f"xo{l}")
                dve_scale(dve, F_NORM[l], xT, None, T, f"norm_f{l}")
                for g in range(FF_GROUPS):
                    dve_up(dve, l, g)
                    if g < FF_GROUPS - 1:
                        residual(dve, f"down{l}{g}", 2)
                dve_norm(dve, (4, 9)[l], T, f"down{l}{FF_GROUPS - 1}")

            cross(0)
            mlp(0)
            dve_scale(dve, 4, xT, None, T, "norm_mix1")
            dve_conformer(dve)
            dve_norm(dve, 5, T)
            dve_scale(dve, 5, glu_y, None, T, "ln_g")
            cross(1)
            mlp(1)
            dve_scale(dve, 9, xT, y_out, T, "norm_out")

        @block.tensor
        def _(pe):
            pe.wait_ge(consts_ready, 1)
            pe_norm(pe, 0, T)
            pe_values(pe)
            pe_gates(pe)
            pe_product(pe, "k_fox", 1, hT, T, after())
            pe_gate_sums(pe)
            pe_product(pe, "q_fox", 1, hT, T, after())
            pe_fox(pe)
            pe_fox_rows(pe)
            pe_product(pe, "conv", 3, hT, T, after())
            pe_product(pe, "z", 1, hT, T, after())
            pe_fox_soft(pe)
            pe_squares(pe, 0, 8)
            pe_gdn(pe)
            pe_gdn_rows(pe)
            pe_head_norm(pe)
            pe_product3(pe, "out", 2, h_hi, h_lo, by_chunk(cat_lo, 0))

            def cross(l):
                pe_norm(pe, X_NORM[l], T)
                pe_norm(pe, M_NORM[l], NMEM)
                pe.wait_ge(nm_out, OUT0[M_NORM[l]] + 8)
                pe.wait_ge(nm_cp, M_NORM[l] + 1)
                pe_memory(pe, l)
                pe_product3(pe, f"xq{l}", 2, h_hi, h_lo, by_chunk(nm_out, OUT0[X_NORM[l]]))
                pe_cross(pe, l)
                pe_product3(pe, f"xo{l}", 2, h_hi, h_lo, at_once((xa["oc"], 8 * l + 10), (xa["pvc"], 8 * l + 2 + NB)))
                pe_norm(pe, F_NORM[l], T)

            cross(0)
            pe_mlp(pe, 0)
            pe_norm(pe, 4, T)
            pe_product3(pe, "pw1", 4, h_hi, h_lo, by_chunk(nm_out, OUT0[4]))
            pe_mean(pe)
            pe_norm(pe, 5, T)
            pe_product3(pe, "pw2", 2, h_hi, h_lo, by_chunk(nm_out, OUT0[5]))
            cross(1)
            pe_mlp(pe, 1)
            pe_norm(pe, 9, T)


def kernel(**inputs):
    import numpy as np
    import concourse.bacc as bacc
    from concourse.bass_utils import run_bass_kernel_spmd

    a = {k: np.asarray(x) for k, x in inputs.items()}

    def cols(x, c):
        return x.reshape(c, P).T

    def featmajor(x):
        return x.T.reshape(-1, P, x.shape[0]).transpose(1, 0, 2)

    def tiles(wm):
        n = wm.shape[1] // 256
        return wm.reshape(KC, P, n, 256).transpose(2, 1, 0, 3).reshape(n, P, KC * 256)

    def tiles_b(wm):
        n = wm.shape[1] // P
        return wm.reshape(KC, P, n, P).transpose(2, 1, 0, 3).reshape(n, P, KC * P)

    def rows(x):
        return np.broadcast_to(x[None, :], (P, x.shape[0]))

    w_in = a["w_in_e"][0]
    o_z, o_a, o_b, o_q, o_k, o_v, o_f = 1536, 2048, 2052, 2056, 2568, 3080, 3592
    gates = w_in[:, list(range(o_a, o_q)) + list(range(o_f, o_f + HB))]
    z4, z8 = np.zeros(4, np.float32), np.zeros(8, np.float32)
    vecs = np.concatenate(
        [cols(a[n][l], 8) for n in ("norm_mix", "norm_x", "norm_f", "norm_mem") for l in range(2)]
        + [cols(a["norm_out"], 8), cols(a["b_pw1"][0], 16)] + [cols(a[n][0], 8) for n in ("b_dw", "ln_g", "ln_b")]
        + [a["gnorm_a"][0][:, None], a["conv_a"][0].reshape(CA, 12, P).transpose(2, 1, 0).reshape(P, 48),
           a["w_dw"][0].reshape(CC, KC, P).transpose(2, 1, 0).reshape(P, KC * CC),
           rows(np.concatenate([a["dt_bias"][0], z4, a["b_f"][0]])), rows(np.concatenate([a["a_log"][0], z4, z8]))], axis=1)
    pw1 = tiles_b(a["w_pw1"][0])
    pw1 = np.stack([pw1[:8], pw1[8:]], 1).reshape(pw1.shape)
    stream = [tiles(w_in[:, o_v:o_v + 512]), tiles(w_in[:, o_k:o_k + 512]), tiles(w_in[:, o_q:o_q + 512]),
              tiles(w_in[:, :1536]), tiles(w_in[:, o_z:o_z + 512])]
    stream_b = [tiles_b(a["w_out_e"][0])]
    for l in range(2):
        if l:
            stream_b += [pw1, tiles_b(a["w_pw2"][0])]
        stream_b += [tiles_b(a["w_xkv"][l]), tiles_b(a["w_xq"][l]), tiles_b(a["w_xo"][l])]
        for g in range(FF_GROUPS):
            stream_b += [tiles_b(a["w_up"][l][:, g * D:g * D + D]), tiles_b(a["w_down"][l][g * D:g * D + D])]
    arrays = {
        "xT_in": np.concatenate([featmajor(a["x_prompt"][0]), featmajor(a["x_sample"][:, 0])], axis=2),
        "memT_in": featmajor(a["mem_prompt"][0]),
        "vecs_in": vecs,
        "wall": np.concatenate(stream, axis=0),
        "wallb": np.concatenate(stream_b, axis=0),
        "wgate_in": gates.reshape(KC, P, 16).transpose(1, 0, 2),
        "st_gconv_in": a["state_gdn_conv"][0].transpose(2, 1, 0).reshape(12, P, 3, NB).transpose(1, 0, 2, 3),
        "st_cconv_in": a["state_cfm_conv"][0].transpose(2, 0, 1).reshape(KC, P, NB, CC - 1).transpose(1, 0, 2, 3),
        "pages_in": a["page_table"].reshape(1, NB * NPG),
        "kpool": a["cache_fox_k"][0].reshape(-1, PAGE, 512),
        "vpool": a["cache_fox_v"][0].reshape(-1, PAGE, 512),
        "fpool": a["cache_fox_logf"][0],
        "st_gdn": a["state_gdn"][0],
        "cmk": a["cache_mem_k"].reshape(2, NB, NMEM, D),
        "cmv": a["cache_mem_v"].reshape(2, NB, NMEM, D),
    }
    outs = {"yT": (P, KC * T), "fkT": (512, T), "fv": (T, 512), "flf": (T, HB), "gdn_p": (P, HA, P),
            "gconv": (P, 12, 3 + NB), "gkeep": (P, 12, 2 * NB), "gdn_s": (P, NB * HA, P), "cconv": (P, KC, 30 + NB), "ckeep": (P, KC, NB * 29),
            "mkT": (2, D, NMEM), "mv": (2, NMEM, D)}
    nc = bacc.Bacc("TRN2", target_bir_lowering=False, num_devices=1)
    arrays = {k: np.ascontiguousarray(x) for k, x in arrays.items()}
    args = {k: nc.dram_tensor(k, x.shape, mybir.dt.from_np(x.dtype), kind="ExternalInput").ap() for k, x in arrays.items()}
    args.update({k: nc.dram_tensor(k, s, F32, kind="ExternalOutput").ap() for k, s in outs.items()})
    build(nc, **args)
    r = run_bass_kernel_spmd(nc, [arrays], core_ids=[0]).results[0]

    y = r["yT"].reshape(P, KC, T).transpose(2, 1, 0).reshape(T, D)
    fk = r["fkT"].T.reshape(T, HB, DHB)
    fv_ = r["fv"].reshape(T, HB, DHB)
    gconv = r["gconv"].transpose(2, 1, 0).reshape(3 + NB, 12 * P)
    cconv = r["cconv"].transpose(2, 1, 0).reshape(30 + NB, D)
    gkeep = r["gkeep"].reshape(P, 12, 2, NB).transpose(3, 2, 1, 0).reshape(NB, 2, 12 * P)
    ckeep = r["ckeep"].reshape(P, KC, NB, 29).transpose(2, 3, 1, 0).reshape(NB, 29, D)
    return (y[:SEQ][None], y[SEQ:][:, None], fk[:SEQ][None, None], fv_[:SEQ][None, None], r["flf"][:SEQ][None, None],
            fk[SEQ:][None, :, None], fv_[SEQ:][None, :, None], r["flf"][SEQ:][None, :, None],
            r["gdn_p"].transpose(1, 0, 2)[None, None], gconv[None, None, :3],
            r["gdn_s"].reshape(P, NB, HA, P).transpose(1, 2, 0, 3)[None], np.concatenate([gkeep, gconv[3:][:, None]], axis=1)[None],
            cconv[None, None, :30], np.concatenate([ckeep, cconv[30:][:, None]], axis=1)[None],
            r["mkT"].transpose(0, 2, 1).reshape(2, 1, NMEM, HX, DHX), r["mv"].reshape(2, 1, NMEM, HX, DHX))
```

```python
from contextlib import ExitStack, contextmanager

import concourse.bass as bass
from concourse import mybir

P = 128
D = 1024
KC = D // P
SEQ, NB = 1024, 8
T = SEQ + NB
N3 = T // 3
QT = SEQ // P
PAST, PAGE = 2048, 128
NPG = PAST // PAGE
HA, HB, DHB = 4, 8, 64
HX, DHX, NMEM = 4, 256, 256
CA, CC = 4, 31
EPS = 1e-6
NEG = -1e30
FF_GROUPS = 4
ARENA = 5 * KC * T + 2688 + 6144
ARENA_BYTE = 16512

F32 = mybir.dt.float32
F32R = mybir.dt.float32r
I32 = mybir.dt.int32
ACT = mybir.ActivationFunctionType
ALU = mybir.AluOpType
AX = mybir.AxisListType
ds = bass.ds

VECS = [("norm_mix0", 8), ("norm_mix1", 8), ("norm_x0", 8), ("norm_x1", 8), ("norm_f0", 8), ("norm_f1", 8),
        ("norm_mem0", 8), ("norm_mem1", 8), ("norm_out", 8), ("b_pw1", 16), ("b_dw", 8), ("ln_g", 8), ("ln_b", 8),
        ("gnorm", 1), ("conv_a", 48), ("w_dw", 248), ("gate_bias", 16), ("gate_alog", 16)]
VOFF, _o = {}, 0
for _n, _w in VECS:
    VOFF[_n] = (_o, _w)
    _o += _w
NVEC = _o

STREAM = [("v_fox", 1), ("k_fox", 1), ("q_fox", 1), ("conv", 3), ("z", 1)]
PAIR0, GROUP0, _p, _g = {}, {}, 0, 0
for _n, _w in STREAM:
    PAIR0[_n], GROUP0[_n] = _p, _g
    _p += _w
    _g += 18 if _n == "v_fox" else 4 * _w
NPAIRS = _p
G_V = 18
STREAM_B = [("out", 8)]
for _l in range(2):
    if _l == 1:
        STREAM_B += [("pw1", 16), ("pw2", 8)]
    STREAM_B += [(f"mk{_l}", 8), (f"mv{_l}", 8), (f"xq{_l}", 8), (f"xo{_l}", 8)]
    for _g2 in range(FF_GROUPS):
        STREAM_B += [(f"up{_l}{_g2}", 8), (f"down{_l}{_g2}", 8)]
GROUPS_A, TILE0, _t = _g, {}, 0
for _n, _w in STREAM_B:
    TILE0[_n], GROUP0[_n] = _t, GROUPS_A + _t
    _t += _w
NTILES = _t


class Steps:

    def __init__(self, eng, sem):
        self.eng, self.sem, self.n, self.at = eng, sem, 0, None

    def link(self, ins):
        self.n += 1
        ins.then_inc(self.sem, 1)
        self.eng.wait_ge(self.sem, self.n if self.at is None else self.at + self.n)

    def lag(self, ins):
        self.n += 1
        ins.then_inc(self.sem, 1)
        self.eng.wait_ge(self.sem, self.n - 1 if self.at is None else self.at + (self.n - 1))

    @contextmanager
    def loop(self, trips, per):
        entry = self.n
        with self.eng.Fori(0, trips) as i:
            self.at, self.n = i * per + entry, 0
            yield i
            assert self.n == per, f"{self.n} linked steps in a round, not {per}"
        self.at, self.n = None, entry + trips * per


def build(nc, xT_in, memT_in, vecs_in, x_spill, wall, wallb, wgate_in, st_gconv_in, st_cconv_in, pages_in, kpool, vpool, fpool, st_gdn,
          cmk, cmv, yT, fkT, fv, flf, gdn_p, gconv, gkeep, gdn_s, cconv, ckeep, mkT, mv):
    ctx = ExitStack()
    with ctx:
        def sb(name, shape, dt=F32):
            return ctx.enter_context(nc.sbuf_tensor(name, shape, dt))

        def sem(name):
            return ctx.enter_context(nc.semaphore(name))

        sb("arena", [P, ARENA + 8])

        def at(name, offset, shape, dt=F32):
            return nc.alloc_sbuf_tensor_at(name, shape, dt, offset=ARENA_BYTE + 4 * offset)

        XW = KC * T
        xT = at("xT", 0, [P, KC, T])
        aT = at("aT", XW, [P, KC, T])
        big = at("big", 2 * XW, [P, 12, T])
        hT = at("hT", 2 * XW + 12 * T, [P, KC, T])
        wk = at("wk", 3 * XW + 12 * T, [P, 8850])
        w = at("w", ARENA - 4096, [P, 2, KC, 256])
        a_hi = at("a_hi", XW, [P, KC, T], F32R)
        a_lo = at("a_lo", 2 * XW, [P, KC, T], F32R)
        h_hi = at("h_hi", ARENA - 6144 - 2 * XW, [P, KC, T], F32R)
        h_lo = at("h_lo", ARENA - 6144 - XW, [P, KC, T], F32R)
        y_out = at("y_out", ARENA - 6144 - 2 * XW, [P, KC, T])
        w_hi = at("w_hi", ARENA - 6144, [P, 2, KC, P], F32R)
        w_lo = at("w_lo", ARENA - 4096, [P, 2, KC, P], F32R)
        w_raw = at("w_raw", ARENA - 2048, [P, 2, KC, P])
        la = at("la", XW, [P, 2 * XW + 2688])
        vec = sb("vec", [P, NVEC])
        ident = sb("ident", [P, P])
        ones = sb("ones", [P, P])
        upper = sb("upper", [P, P])
        later = sb("later", [P, P])
        strict = sb("strict", [P, P])
        neg_qk = sb("neg_qk", [P, P])
        neg_ji = sb("neg_ji", [P, P])
        lev = sb("lev", [P, 7, P])
        page_later = sb("page_later", [P, P])
        lev0T = sb("lev0T", [P, P])
        gt = sb("gt", [P, 9, 11, 4])
        lf = sb("lf", [P, 9, 8])
        cf = wk[:, 5400:5464].rearrange("p (t h) -> p t h", h=8)
        small = sb("small", [P, 56])
        sm = small[:, 0:32]
        gcoef = small[:, 32:48]
        eps = small[:, 48:49]
        pages = wk[0:1, 8550:8550 + NB * NPG].bitcast(I32)
        pagec = small[:, 49:50].bitcast(I32)
        ps = ctx.enter_context(nc.psum_tensor("ps", [P, 8, 512], F32))

        def v(name, c=0, n=1):
            return vec[:, VOFF[name][0] + c:VOFF[name][0] + c + n]

        def part(buf, off, *shape):
            n = 1
            for s in shape:
                n *= s
            flat = buf[:, off:off + n]
            if len(shape) == 1:
                return flat
            names = "abcd"[:len(shape)]
            return flat.rearrange(f"p ({' '.join(names)}) -> p {' '.join(names)}",
                                  **{a: s for a, s in zip(names[1:], shape[1:])})

        bigf = big[:, :, :].rearrange("p a b -> p (a b)")
        hTf = hT[:, :, :].rearrange("p a b -> p (a b)")
        aTf = aT[:, :, :].rearrange("p a b -> p (a b)")
        psf = ps[:, :, :].rearrange("p a b -> p (a b)")

        def thirds(ap):
            return ap.rearrange("p (a n) -> p a n", a=3)

        def psum_set(s):
            return ps[:, 3 * s:3 * s + 3, 0:N3]

        in_loaded = sem("in_loaded")
        w_loaded = [sem("w_loaded0"), sem("w_loaded1")]
        consts_ready = sem("consts_ready")
        psum_ready = sem("psum_ready")
        psum_free = sem("psum_free")
        stored = sem("stored")
        act_steps, dve_steps, pool_steps = sem("act_steps"), sem("dve_steps"), sem("pool_steps")
        nm_sq, nm_add, nm_sum, nm_rt, nm_rc, nm_bc, nm_cp, nm_out, nm_t, nm_hi = (sem("nm_" + n) for n in (
            "sq", "add", "sum", "rt", "rc", "bc", "cp", "out", "t", "hi"))
        w_split = sem("w_split")
        n_stored = [0]

        S = {}

        def pool_consts(pool):
            link = S["pool"].link
            g = nc.gpsimd
            link(g.memset(ident[:], 0.0))
            link(g.affine_select(out=ident[:], in_=ident[:], compare_op=ALU.not_equal, fill=1.0, base=0,
                                 pattern=[[-1, P]], channel_multiplier=1))
            for m, start, op, fill, step in ((upper, 1.0, ALU.is_ge, 0.0, 1), (later, 1.0, ALU.is_gt, 0.0, -1),
                                             (strict, 1.0, ALU.is_gt, 0.0, 1), (neg_qk, 0.0, ALU.is_ge, NEG, -1),
                                             (neg_ji, 0.0, ALU.is_ge, NEG, 1)):
                link(g.memset(m[:], start))
                link(g.affine_select(out=m[:], in_=m[:], compare_op=op, fill=fill, base=0, pattern=[[step, P]],
                                     channel_multiplier=-step))
            link(g.memset(lev[:], 0.0))
            link(g.memset(lev0T[:], 0.0))
            for s in range(7):
                b = 1 << s
                half = lev[:, s, :].rearrange("p (k t r) -> p k t r", t=2, r=b)[:, :, 0, :]
                link(g.memset(half, 1.0))
                link(g.affine_select(out=half, in_=half, compare_op=ALU.is_ge, fill=0.0, base=-b,
                                     pattern=[[-2 * b, P // (2 * b)], [0, b]], channel_multiplier=1))
                link(g.affine_select(out=half, in_=half, compare_op=ALU.is_ge, fill=0.0, base=2 * b - 1,
                                     pattern=[[2 * b, P // (2 * b)], [0, b]], channel_multiplier=-1))
            odd = lev0T[:, :].rearrange("p (k t) -> p k t", t=2)[:, :, 1]
            link(g.memset(odd, 1.0))
            link(g.affine_select(out=odd, in_=odd, compare_op=ALU.is_equal, fill=0.0, base=0,
                                 pattern=[[-2, P // 2]], channel_multiplier=1))
            link(g.memset(page_later[:], 1.0))
            pl = page_later[:, :].rearrange("p (b g) -> p b g", g=NPG)
            link(g.affine_select(out=pl, in_=pl, compare_op=ALU.is_gt, fill=0.0, base=0,
                                 pattern=[[-NPG, NB], [-1, NPG]], channel_multiplier=1))
            link(g.affine_select(out=pl, in_=pl, compare_op=ALU.is_ge, fill=0.0, base=NPG - 1,
                                 pattern=[[NPG, NB], [0, NPG]], channel_multiplier=-1))
            link(g.memset(eps[:], EPS))
            link(g.memset(gt[:], 0.0))
            pool.sem_inc(w_split, 2)
            g.memset(ones[:], 1.0).then_inc(consts_ready, 1)

        wgate = part(wk, 8700, KC, 16)

        def sp_loads(sp):
            for dst, src in ((xT[:], xT_in), (vec[:], vecs_in), (wgate, wgate_in),
                             (pages, pages_in), (pagec[:], pages_in.rearrange("a (p b) -> (a p) b", b=1))):
                sp.dma_start(dst, src).then_inc(in_loaded, 16)

            def load(i, s):
                sp.dma_start(w[:, s, :, :], wall[ds(2 * i + s, 1)].rearrange("a p (k n) -> p (a k) n", k=KC))\
                    .then_inc(w_loaded[s], 16)

            for s in range(2):
                load(0, s)
            for s in range(2):
                sp.wait_ge(psum_ready, 9 * (s + 1))
                load(1, s)
            with sp.Fori(2, NPAIRS) as i:
                for s in range(2):
                    sp.wait_ge(psum_ready, i * 4 + (G_V - 8 + 2 * (s + 1)))
                    load(i, s)
            sp.wait_ge(in_loaded, 80)
            with sp.Fori(0, 16) as r:
                for s in range(2):
                    sp.wait_ge(fs["free"], r * 2 + (s + 33))
                    load_pages(sp, vpool, r, s, "vring")
            with sp.Fori(0, NTILES // 2) as i:
                for s in range(2):
                    if s == 0:
                        sp.wait_ge(psum_ready, GROUPS_A)
                    sp.wait_ge(w_split, i * 2 + (s + 1))
                    sp.dma_start(w_raw[:, s, :, :], wallb[ds(i * 2 + s, 1)].rearrange("a p (k n) -> p (a k) n", k=KC))\
                        .then_inc(w_loaded[s], 16)

        def split_tile(pool, s, i, t0):
            one = ones[:, :].rearrange("p (a n) -> p a n", a=1).to_broadcast([P, KC, P])
            pool.wait_ge(w_loaded[s], i * 16 + 16 * (NPAIRS + t0 // 2 + 1))
            pool.wait_ge(psum_ready, i * 2 + (GROUPS_A + t0 + s - 1))
            S["pool"].link(nc.gpsimd.tensor_tensor(w_hi[:, s], w_raw[:, s], one, ALU.mult))
            nc.gpsimd.tensor_tensor(w_lo[:, s], w_raw[:, s], w_hi[:, s].bitcast(F32), ALU.subtract).then_inc(w_split, 1)

        def pool_split(pool, t0, t1):
            with S["pool"].loop((t1 - t0) // 2, 2) as i:
                for s in range(2):
                    split_tile(pool, s, i, t0)

        def split_tiles(pool, *names):
            pool_split(pool, TILE0[names[0]], TILE0[names[-1]] + dict(STREAM_B)[names[-1]])

        def pool_hand_back(pool, name):
            with pool.Fori(0, 8) as i:
                pool.wait_ge(psum_ready, i + (GROUP0[name] + 1))
                pool.sem_inc(w_split, 1)

        sq, acc0, rbc0 = part(wk, 0, 2, T), part(wk, 2 * T, T), part(wk, 3 * T, T)
        sq1, acc1, rbc1 = part(la, 12352, 2, T), part(la, 12352 + 2 * T, T), part(la, 12352 + 3 * T, T)
        nmf = at("nmf", ARENA - 6144 - 4 * T, [P, 4 * T])
        sqm, accm, rbcm = part(la, 4096, 2, NMEM), part(la, 4608, NMEM), part(la, 4864, NMEM)
        tt = part(la, 2 * XW, 2, T)

        X_NORM, M_NORM, F_NORM = (1, 6), (2, 7), (3, 8)
        OUT0 = {n: 8 * n for n in range(10)} | {1: 16, 2: 8, 6: 56, 7: 48}
        SPLIT = {1: 0, 3: 1, 4: 2, 5: 3, 6: 4, 8: 5}

        def bufs(n):
            if n in M_NORM:
                return sqm, accm, rbcm
            if n in (4, 9):
                return part(nmf, 0, 2, T), part(nmf, 2 * T, T), part(nmf, 3 * T, T)
            return (sq1, acc1, rbc1) if n else (sq, acc0, rbc0)

        def tiles_of(width):
            out = [(t * P, P, 0, (t // 4) * 512 + (t % 4) * P) for t in range(width // P)]
            if width % P:
                out.append((width - P, width % P, P - width % P, (width // P // 4) * 512))
            return out

        def pe_norm(pe, n, width):
            acc = bufs(n)[1]
            pe.wait_ge(nm_add, 8 * (n + 1))
            if n:
                pe.wait_ge(nm_cp, n)
            tl = tiles_of(width)
            for j, (at_, cnt, skip, _) in enumerate(tl):
                ins = nc.tensor.matmul(ps[:, 6, j:j + 1], acc[:, at_:at_ + P], ones[:, 0:1], start=True, stop=True)
            ins.then_inc(nm_sum, 1)
            pe.wait_ge(nm_rc, n + 1)
            for j, (_, cnt, skip, to) in enumerate(tl):
                ins = nc.tensor.matmul(psf[:, to:to + cnt], sm[:, 16 + j:17 + j].to_broadcast([P, P]),
                                       ident[:, skip:skip + cnt], start=True, stop=True)
            ins.then_inc(nm_bc, 1)

        def act_norm(act, n, src, width, wait):
            sq, _, rbc = bufs(n)
            for c in range(KC):
                wait(act, c)
                if c >= 2:
                    act.wait_ge(nm_add, 8 * n + c - 1)
                nc.scalar.activation(sq[:, c % 2, 0:width], src[:, c, :], ACT.Square).then_inc(nm_sq, 1)
            k = len(tiles_of(width))
            act.wait_ge(nm_sum, n + 1)
            nc.scalar.activation(sm[:, 0:k], ps[:, 6, 0:k], ACT.Sqrt, bias=eps[:, 0:1], scale=1.0 / D)\
                .then_inc(nm_rt, 1)
            act.wait_ge(nm_bc, n + 1)
            full = width - width % P
            ins = nc.scalar.activation(rbc[:, 0:full], psf[:, 0:full], ACT.Copy)
            if width % P:
                ins = nc.scalar.activation(rbc[:, full:width], psf[:, full:width], ACT.Copy)
            ins.then_inc(nm_cp, 1)

        def act_scale(act, n):
            for c in range(KC):
                act.wait_ge(nm_t, 8 * SPLIT[n] + c + 1)
                if n == 5:
                    S["act"].link(nc.scalar.activation(tt[:, c % 2], tt[:, c % 2], ACT.Silu, bias=v("ln_b", c)))
                nc.scalar.activation(h_hi[:, c, :], tt[:, c % 2], ACT.Copy).then_inc(nm_hi, 1)

        def dve_norm(dve, n, width, residual_of=None):
            sq, acc, rbc = bufs(n)
            if residual_of is None:
                for c in range(KC):
                    dve.wait_ge(nm_sq, 8 * n + c + 1)
                    if c == 0:
                        nc.vector.tensor_copy(acc[:, 0:width], sq[:, 0, 0:width]).then_inc(nm_add, 1)
                    else:
                        nc.vector.tensor_tensor(acc[:, 0:width], acc[:, 0:width], sq[:, c % 2, 0:width], ALU.add)\
                            .then_inc(nm_add, 1)
                    dve.wait_ge(nm_add, 8 * n + c + 1)
            else:
                g0 = GROUP0[residual_of]
                S["dve"].link(nc.vector.memset(acc, 0.0))
                dve.wait_ge(psum_free, g0)
                with dve.Fori(0, 2) as i:
                    for j in range(4):
                        dve.wait_ge(psum_ready, i * 4 + (g0 + j + 1))
                        nc.vector.tensor_tensor(at_chunk(xT, i * 4 + j), at_chunk(xT, i * 4 + j), psum_set(j % 2), ALU.add)\
                            .then_inc(psum_free, 1)
                        dve.wait_ge(nm_sq, i * 4 + (8 * n + j + 1))
                        dve.wait_ge(nm_add, i * 4 + (8 * n + j))
                        nc.vector.tensor_tensor(acc, acc, sq[:, j % 2], ALU.add).then_inc(nm_add, 1)
            k = len(tiles_of(width))
            dve.wait_ge(nm_rt, n + 1)
            nc.vector.reciprocal(sm[:, 16:16 + k], sm[:, 0:k]).then_inc(nm_rc, 1)

        def dve_scale(dve, n, src, dst, width, gain):
            rbc = bufs(n)[2]
            dve.wait_ge(nm_cp, n + 1)
            if n not in SPLIT:
                for c in range(KC):
                    nc.vector.scalar_tensor_tensor(out=dst[:, c, :], in0=src[:, c, :], scalar=v(gain, c), in1=rbc[:, 0:width],
                                                   op0=ALU.mult, op1=ALU.mult).then_inc(nm_out, 1)
                return

            def rest(c):
                dve.wait_ge(nm_hi, 8 * SPLIT[n] + c + 1)
                nc.vector.tensor_tensor(h_lo[:, c, :], tt[:, c % 2], h_hi[:, c, :].bitcast(F32), ALU.subtract)\
                    .then_inc(nm_out, 1)

            for c in range(KC):
                if c >= 2:
                    dve.wait_ge(nm_out, OUT0[n] + c - 1)
                nc.vector.scalar_tensor_tensor(out=tt[:, c % 2], in0=src[:, c, :], scalar=v(gain, c), in1=rbc[:, 0:width],
                                               op0=ALU.mult, op1=ALU.mult).then_inc(nm_t, 1)
                if c:
                    rest(c - 1)
            rest(KC - 1)

        def pe_product(pe, name, pairs, src, width, wait_src):
            wait_src(pe)
            p0, g0 = PAIR0[name], GROUP0[name]
            cols = [(n * N3, N3) for n in range(3)] if width == T else [(0, width)]
            with pe.Fori(0, pairs) as i:
                for s in range(2):
                    pe.wait_ge(w_loaded[s], i * 16 + 16 * (p0 + 1))
                    for o in range(2):
                        j = 2 * s + o
                        st = (g0 + j) % 2
                        pe.wait_ge(psum_free, i * 4 + (g0 + j - 1))
                        for k in range(KC):
                            for n, (c0, cn) in enumerate(cols):
                                ins = nc.tensor.matmul(ps[:, 3 * st + n, 0:cn], w[:, s, k, o * P:(o + 1) * P],
                                                       src[:, k, c0:c0 + cn], start=(k == 0), stop=(k == KC - 1))
                        ins.then_inc(psum_ready, 1)

        def pe_product3(pe, name, rounds, hi, lo, wait_src):
            t0, g0 = TILE0[name], GROUP0[name]
            with pe.Fori(0, rounds) as i:
                for j in range(4):
                    pe.wait_ge(w_split, i * 4 + (t0 + j + 3))
                    pe.wait_ge(psum_free, i * 4 + (g0 + j - 1))
                    for k in range(KC):
                        if j == 0:
                            wait_src(pe, k)
                        for n_pass, (wt, src) in enumerate(((w_hi, hi), (w_hi, lo), (w_lo, hi))):
                            for n in range(3):
                                ins = nc.tensor.matmul(ps[:, 3 * (j % 2) + n, 0:N3], wt[:, j % 2, k, :],
                                                       src[:, k, n * N3:(n + 1) * N3], start=(k == 0 and n_pass == 0),
                                                       stop=(k == KC - 1 and n_pass == 2))
                    ins.then_inc(psum_ready, 1)

        def epilogue(eng, name, pairs, op):
            g0 = GROUP0[name]
            with eng.Fori(0, pairs) as i:
                for j in range(4):
                    eng.wait_ge(psum_ready, i * 4 + (g0 + j + 1))
                    op(i, j, (g0 + j) % 2).then_inc(psum_free, 1)

        def at_chunk(buf, c):
            return buf[:, ds(c, 1), :].rearrange("p a (b n) -> p (a b) n", b=3)

        def after(*pairs):
            def wait(eng):
                for s, n in pairs:
                    eng.wait_ge(s, n)
            return wait

        def freed(name, pairs):
            return (psum_free, GROUP0[name] + 4 * pairs)

        def store(pool, dst, src):
            n_stored[0] += 1
            pool.dma_start(dst, src).then_inc(stored, 16)

        qf, kf = big[:, 0:4, :], big[:, 4:8, :]
        vf = part(bigf, 8 * T, QT, 512)
        vs = wk[0:NB, 8000:8512]

        def pe_values(pe):
            pe.wait_ge(nm_out, 8)
            for s in range(2):
                pe.wait_ge(w_loaded[s], 16)
                for t in range(QT + 1):
                    g = 9 * s + t
                    m = P if t < QT else NB
                    if g >= 2:
                        pe.wait_ge(psum_free, g - 1)
                    for k in range(KC):
                        ins = nc.tensor.matmul(ps[0:m, 3 * (g % 2), 0:256], hT[:, k, t * P:t * P + m], w[:, s, k, :],
                                               start=(k == 0), stop=(k == KC - 1))
                    ins.then_inc(psum_ready, 1)

        def act_values(act):
            for g in range(18):
                s, t = divmod(g, 9)
                act.wait_ge(psum_ready, g + 1)
                if t < QT:
                    ins = nc.scalar.activation(vf[:, t, s * 256:s * 256 + 256], ps[:, 3 * (g % 2), 0:256], ACT.Copy)
                else:
                    ins = nc.scalar.activation(vs[:, s * 256:s * 256 + 256], ps[0:NB, 3 * (g % 2), 0:256], ACT.Copy)
                ins.then_inc(psum_free, 1)

        gates_ready, gates_u, gates_exp, gates_done = (sem(n) for n in (
            "gates_ready", "gates_u", "gates_exp", "gates_done"))
        ga = [part(wk, 4200 + 144 * n, 9, 16) for n in range(8)]
        gbank = ps[:, 7, 0:144].rearrange("p (t n) -> p t n", n=16)
        G_G, G_GC, G_RQ, G_RK, G_RQE, G_RKB, G_B, G_BE, G_KD, G_EL, G_E = range(11)
        tile_at = [t * P for t in range(QT)] + [T - P]

        def pe_gate_sums(pe):
            pe.wait_ge(gates_done, 1)
            for t in range(QT):
                nc.tensor.matmul(ps[:, 7, 256 + 4 * t:260 + 4 * t], upper[:], gt[:, t, G_G, :], start=True, stop=True)
            for t in range(QT):
                nc.tensor.matmul(ps[:, 7, 288 + 4 * t:292 + 4 * t], ones[:], gt[:, t, G_G, :], start=True, stop=True)
            for t in range(QT):
                for u in range(t + 1):
                    ins = nc.tensor.matmul(ps[:, 7, 320 + 8 * t:328 + 8 * t], upper[:] if u == t else ones[:],
                                           lf[:, u, :], start=(u == 0), stop=(u == t))
            ins.then_inc(gates_ready, 1)

        def pe_gates(pe):
            pe.wait_ge(in_loaded, 80)
            for t in range(9):
                for k in range(KC):
                    ins = nc.tensor.matmul(gbank[:, t, :], hT[:, k, tile_at[t]:tile_at[t] + P], wgate[:, k, :],
                                           start=(k == 0), stop=(k == KC - 1))
            ins.then_inc(gates_ready, 1)

        def act_gates(act):
            act.wait_ge(in_loaded, 80)
            nc.scalar.activation(gcoef[:], v("gate_alog", 0, 16), ACT.Exp).then_inc(gates_exp, 1)
            act.wait_ge(gates_u, 1)
            nc.scalar.activation(ga[2], ga[2], ACT.Exp).then_inc(gates_exp, 1)
            nc.scalar.activation(ga[4], ga[0], ACT.Exp).then_inc(gates_exp, 1)

        def act_gate_sums(act):
            act.wait_ge(gates_u, 2)
            for src, dst in ((G_GC, G_E), (G_KD, G_KD), (G_EL, G_EL)):
                nc.scalar.activation(gt[:, :, dst, :], gt[:, :, src, :], ACT.Exp).then_inc(gates_exp, 1)

        def dve_gates(dve):
            link, vv = S["dve"].link, nc.vector
            dve.wait_ge(gates_ready, 1)
            dve.wait_ge(gates_exp, 1)
            y, ny, m, z, z2, h = ga[0], ga[1], ga[2], ga[3], ga[5], ga[6]
            bias = v("gate_bias", 0, 16).rearrange("p (a n) -> p a n", a=1).to_broadcast([P, 9, 16])
            link(vv.tensor_tensor(y, gbank, bias, ALU.add))
            link(vv.tensor_scalar(y[:, :, 4:16], y[:, :, 4:16], -1.0, None, ALU.mult))
            link(vv.tensor_scalar(ny, y, -1.0, None, ALU.mult))
            vv.tensor_tensor(m, y, ny, ALU.min).then_inc(gates_u, 1)
            dve.wait_ge(gates_exp, 3)
            link(vv.tensor_scalar(z, m, 2.0, None, ALU.add))
            link(vv.reciprocal(z, z))
            link(vv.tensor_tensor(z, z, m, ALU.mult))
            link(vv.tensor_tensor(z2, z, z, ALU.mult))
            link(vv.tensor_scalar(h, z2, 1.0 / 19, None, ALU.mult))
            for d in (17, 15, 13, 11, 9, 7, 5, 3):
                link(vv.scalar_tensor_tensor(out=h, in0=h, scalar=1.0 / d, in1=z2, op0=ALU.add, op1=ALU.mult))
            link(vv.scalar_tensor_tensor(out=h, in0=h, scalar=1.0, in1=z, op0=ALU.add, op1=ALU.mult))
            link(vv.tensor_scalar(ny, y, 0.0, None, ALU.max))
            link(vv.scalar_tensor_tensor(out=h, in0=h, scalar=2.0, in1=ny, op0=ALU.mult, op1=ALU.add))
            link(vv.tensor_scalar(lf[:], h[:, :, 8:16], -1.0, None, ALU.mult))
            link(vv.tensor_scalar(gcoef[:], gcoef[:], -1.0, None, ALU.mult))
            coef = gcoef[:, 0:4].rearrange("p (a n) -> p a n", a=1).to_broadcast([P, 9, 4])
            link(vv.tensor_scalar(ga[4], ga[4], 1.0, None, ALU.add))
            link(vv.reciprocal(gt[:, :, G_B, :], ga[4][:, :, 4:8]))
            vv.tensor_tensor(gt[:, :, G_G, :], h[:, :, 0:4], coef, ALU.mult).then_inc(gates_done, 1)
            dve.wait_ge(gates_ready, 2)
            dve.wait_ge(gates_done, 1)
            gc_ps = ps[:, 7, 256:288].rearrange("p (t n) -> p t n", n=4)
            tot_ps = ps[:, 7, 288:320].rearrange("p (t n) -> p t n", n=4)
            link(vv.tensor_copy(cf[:], ps[:, 7, 320:384].rearrange("p (t n) -> p t n", n=8)))
            link(vv.tensor_copy(gt[:, 0:QT, G_GC, :], gc_ps))
            link(vv.tensor_copy(gt[:, 0:QT, G_EL, :], tot_ps))
            link(vv.tensor_copy(gt[:, QT, G_GC, :], gt[:, QT, G_G, :]))
            link(vv.tensor_copy(gt[:, QT, G_EL, :], gt[:, QT, G_G, :]))
            vv.tensor_tensor(gt[:, :, G_KD, :], gt[:, :, G_EL, :], gt[:, :, G_GC, :], ALU.subtract).then_inc(gates_u, 1)
            dve.wait_ge(gates_exp, 6)
            link(vv.tensor_tensor(gt[:, :, G_BE, :], gt[:, :, G_B, :], gt[:, :, G_E, :], ALU.mult))

        fox_cst, fox_qk, fox_cb, fox_cbc, fox_s, fox_m, fox_e, fox_pt, fox_ptc, fox_o, fox_on, fox_ot, fox_otc = (
            sem("fox_" + n) for n in ("cst", "qk", "cb", "cbc", "s", "m", "e", "pt", "ptc", "o", "on", "ot", "otc"))
        f_neg = part(aTf, 0, 2, SEQ)
        f_pt = part(aTf, 2 * SEQ, 2, SEQ)
        f_q = part(wk, 0, SEQ)
        f_k = part(wk, SEQ, SEQ)
        f_s = part(wk, 2 * SEQ, 2, SEQ)
        f_o = part(wk, 4 * SEQ, QT, P)
        f_c = part(wk, 5 * SEQ, QT, 2)
        f_st = part(wk, 5 * SEQ + 16, 4, 16)
        NT = 2 * QT

        def blk(n):
            return n // QT, n % QT, (n % QT + 1) * P

        def pe_fox(pe):
            with pe.Fori(0, 4) as i:
                pe.wait_ge(fox_cst, i + 1)
                for h in range(2):
                    if h == 0:
                        pe.wait_ge(fox_otc, i + 1)
                    else:
                        pe.wait_ge(fox_cbc, i * 2 + 1)
                    for t in range(QT):
                        ins = nc.tensor.matmul(psf[:, t * P:t * P + P], f_c[:, t, h:h + 1].to_broadcast([P, P]),
                                               ident[:], start=True, stop=True)
                    ins.then_inc(fox_cb, 1)
                pe.wait_ge(fox_qk, i * 2 + 2)
                pe.wait_ge(fox_cbc, i * 2 + 2)

                def scores(n):
                    h, t, wd = blk(n)
                    if n >= 2:
                        pe.wait_ge(fox_m, i * NT + (n - 1))
                    for c0 in range(0, wd, 512):
                        cn = min(512, wd - c0)
                        ins = nc.tensor.matmul(psf[:, (n % 2) * 1024 + c0:(n % 2) * 1024 + c0 + cn],
                                               f_q[64 * h:64 * h + 64, t * P:t * P + P],
                                               f_k[64 * h:64 * h + 64, c0:c0 + cn], start=True, stop=True)
                    ins.then_inc(fox_s, 1)

                def turn(n):
                    h, t, wd = blk(n)
                    pe.wait_ge(fox_e, i * NT + (n + 1))
                    if n:
                        pe.wait_ge(fox_ptc, i * NT + n)
                    for c0 in range(0, wd, P):
                        ins = nc.tensor.transpose(psf[:, 2048 + c0:2048 + c0 + P], f_s[:, n % 2, c0:c0 + P], ident[:])
                    ins.then_inc(fox_pt, 1)

                def values(n):
                    h, t, wd = blk(n)
                    pe.wait_ge(fox_ptc, i * NT + (n + 1))
                    if n >= 2:
                        pe.wait_ge(fox_on, i * NT + (n - 1))
                    for kt in range(t + 1):
                        ins = nc.tensor.matmul(ps[:, 6 + n % 2, 0:64], f_pt[:, n % 2, kt * P:kt * P + P],
                                               vf[:, kt, ds(i * P + h * 64, 64)], start=(kt == 0), stop=(kt == t))
                    ins.then_inc(fox_o, 1)

                scores(0)
                scores(1)
                for n in range(NT):
                    turn(n)
                    if n + 2 < NT:
                        scores(n + 2)
                    if n:
                        values(n - 1)
                values(NT - 1)
                pe.wait_ge(fox_on, i * NT + NT)
                for t in range(QT):
                    ins = nc.tensor.transpose(psf[:, t * P:t * P + P], f_o[:, t, :], ident[:])
                ins.then_inc(fox_ot, 1)

        def act_fox(act):
            act.sem_inc(fox_otc, 1)
            with act.Fori(0, 4) as i:
                for h in range(2):
                    act.wait_ge(fox_cb, i * 2 + (h + 1))
                    nc.scalar.activation(f_neg[:, h, :], psf[:, 0:SEQ], ACT.Copy, scale=-1.0).then_inc(fox_cbc, 1)

                def exps(n):
                    h, t, wd = blk(n)
                    act.wait_ge(fox_m, i * NT + (n + 1))
                    nc.scalar.activation(f_s[:, n % 2, 0:wd], f_s[:, n % 2, 0:wd], ACT.Exp, bias=f_st[:, 1, n:n + 1],
                                         accum_out=f_st[:, 2, n:n + 1]).then_inc(fox_e, 1)

                exps(0)
                for n in range(NT):
                    if n + 1 < NT:
                        exps(n + 1)
                    h, t, wd = blk(n)
                    act.wait_ge(fox_pt, i * NT + (n + 1))
                    if n >= 2:
                        act.wait_ge(fox_o, i * NT + (n - 1))
                    nc.scalar.activation(f_pt[:, n % 2, 0:wd], psf[:, 2048:2048 + wd], ACT.Copy).then_inc(fox_ptc, 1)
                act.wait_ge(fox_ot, i + 1)
                nc.scalar.activation(aT[:, ds(i + 4, 1), 0:SEQ].rearrange("p a n -> p (a n)"), psf[:, 0:SEQ], ACT.Copy)\
                    .then_inc(fox_otc, 1)

        def pool_fox(pool):
            pool.wait_ge(*freed("q_fox", 1))
            pool.wait_ge(gates_exp, 6)
            with pool.Fori(0, 4) as i:
                pool.wait_ge(fox_otc, i + 1)
                nc.gpsimd.tensor_copy(f_c, cf[:, :, ds(i * 2, 2)]).then_inc(fox_cst, 1)
                nc.gpsimd.tensor_copy(f_q, qf[:, ds(i, 1), 0:SEQ].rearrange("p a n -> p (a n)")).then_inc(fox_qk, 1)
                nc.gpsimd.tensor_copy(f_k, kf[:, ds(i, 1), 0:SEQ].rearrange("p a n -> p (a n)")).then_inc(fox_qk, 1)

        def dve_fox(dve):
            PER = NT * 3
            with S["dve"].loop(4, PER) as i:
                link, vv = S["dve"].link, nc.vector

                def soft(n):
                    h, t, wd = blk(n)
                    dve.wait_ge(fox_s, i * NT + (n + 1))
                    dve.wait_ge(fox_cbc, i * 2 + 2)
                    if n >= 2:
                        dve.wait_ge(fox_pt, i * NT + (n - 1))
                    link(vv.tensor_tensor(f_s[:, n % 2, 0:wd], psf[:, (n % 2) * 1024:(n % 2) * 1024 + wd],
                                          f_neg[:, h, 0:wd], ALU.add))
                    link(vv.tensor_tensor(f_s[:, n % 2, t * P:wd], f_s[:, n % 2, t * P:wd], neg_qk[:], ALU.add))
                    vv.tensor_reduce(f_st[:, 1, n:n + 1], f_s[:, n % 2, 0:wd], AX.X, ALU.max, negate=True)\
                        .then_inc(fox_m, 1)

                def out(n):
                    h, t, wd = blk(n)
                    dve.wait_ge(fox_o, i * NT + (n + 1))
                    link(vv.reciprocal(f_st[:, 3, n:n + 1], f_st[:, 2, n:n + 1]))
                    if n == 0:
                        dve.wait_ge(fox_otc, i + 1)
                    vv.tensor_scalar(f_o[:, t, h * 64:h * 64 + 64], ps[:, 6 + n % 2, 0:64],
                                     f_st[:, 3, n:n + 1], None, ALU.mult).then_inc(fox_on, 1)

                soft(0)
                soft(1)
                for n in range(NT):
                    if n + 2 < NT:
                        soft(n + 2)
                    if n:
                        out(n - 1)
                out(NT - 1)

        fs_names = ("small", "turned", "lf", "lft", "lftot", "lfc", "bias", "biasc", "qb", "qbc", "ring0", "ring1", "free",
                    "snp", "snc", "back", "sn", "mx", "mt", "mc", "mb", "sh", "ex", "sum", "tot", "pr", "vring0", "vring1", "pvc", "out")
        fs = {n: sem("fs_" + n) for n in fs_names}
        xTf = xT[:, :, :].rearrange("p a b -> p (a b)")
        s_ring = part(xTf, 0, 2, 4, 512)
        s_qb = part(xTf, 4096, NB, 512)
        s_pr = part(xTf, 4096, NB, NPG, HB)
        s_o = part(xTf, 5120, NB, 8)
        s_pv = part(xTf, 5184, 4, NB)
        s_sn = part(xTf, 8192, NB, HB)
        s_q, s_k, s_v = (part(wk, o, 4, NB) for o in (6240, 6272, 7768))
        s_prod = part(wk, 512, 2048)
        s_sc = part(wk, 2560, NB, NPG, HB)
        s_lft = part(wk, 3584, 1024)
        s_lf = part(wk, 4608, HB, P)
        s_tot = part(wk, 5632, HB)
        s_qk = part(wk, 5648, 32)
        s_mx, s_mb, s_sum, s_rs, s_cq = (part(wk, 5764 + 64 * n, NB, HB) for n in range(5))
        s_mc = part(wk, 6100, 1)

        def heads_even_odd(ap, odd):
            return ap.rearrange("p b (c t) -> p t c b", t=2)[:, odd]

        def pool_fox_rows(pool):
            pool.wait_ge(fox_otc, 5)
            for n, src in ((0, qf), (1, kf)):
                dst = (s_q, s_k)[n]
                nc.gpsimd.tensor_copy(dst, src[:, :, SEQ:T]).then_inc(fs["small"], 1)
            pool.wait_ge(in_loaded, 80)
            pool.indirect_dma_start(out=s_lft, out_offset=None, in_=fpool.rearrange("g t h -> g (t h)"),
                                    in_offset=bass.IndirectOffsetOnAxis(ap=pagec[:, 0:1].bitcast(mybir.dt.uint32), axis=0))\
                .then_inc(fs["lf"], 16)

        def load_pages(eng, src, r, s, done):
            for g in range(4):
                pg = eng.value_load(pages[0:1, ds(r * 8 + (4 * s + g), 1)], min_val=0, max_val=src.shape[0] - 1)
                eng.dma_start(s_ring[:, s, g, :], src[ds(pg, 1)].rearrange("a p n -> p (a n)"))\
                    .then_inc(fs[f"{done}{s}"], 16)

        def pool_key_pages(pool):
            with pool.Fori(0, 16) as r:
                for s in range(2):
                    pool.wait_ge(fs["free"], r * 2 + (s + 1))
                    load_pages(pool, kpool, r, s, "ring")

        def pe_fox_rows(pe):
            pe.wait_ge(fox_otc, 5)
            pe.wait_ge(fs["small"], 2)

            def queries(half):
                for b in range(4):
                    for c in range(4):
                        ins = nc.tensor.matmul(ps[:, b, c * P:(c + 1) * P],
                                               s_q[:, c, 4 * half + b:4 * half + b + 1].to_broadcast([P, P]), ident[:],
                                               start=True, stop=True)
                ins.then_inc(fs["qb"], 1)

            queries(0)
            for c in range(4):
                ins = nc.tensor.transpose(ps[:, 7, c * NB:(c + 1) * NB], vs[:, c * P:(c + 1) * P], ident[0:NB, 0:NB])
            ins.then_inc(fs["turned"], 1)
            pe.wait_ge(fs["qbc"], 1)
            queries(1)
            pe.wait_ge(fs["lf"], 16)
            for h in range(HB):
                ins = nc.tensor.transpose(psf[:, 2048 + h * P:2048 + (h + 1) * P],
                                          s_lft.rearrange("p (t h) -> p h t", h=HB)[:, h, :], ident[:])
            ins.then_inc(fs["lft"], 1)
            pe.wait_ge(fs["lftot"], 1)
            pe.wait_ge(fs["lfc"], 1)
            for h in range(HB):
                to = psf[:, 2048 + h * P:2048 + (h + 1) * P]
                nc.tensor.matmul(to, later[:], s_lf[:, h, :], start=True, stop=False)
                nc.tensor.matmul(to, s_tot[:, h:h + 1].to_broadcast([P, P]), page_later[:], start=False, stop=True)
            for h in range(HB):
                ins = nc.tensor.matmul(ps[:, 6, h * NB:(h + 1) * NB], lf[:, QT, h:h + 1].to_broadcast([P, P]),
                                       ident[:, P - NB:P], start=True, stop=True)
            ins.then_inc(fs["bias"], 1)
            pe.wait_ge(fs["snp"], 1)
            pe.wait_ge(fs["qbc"], 2)
            for t in range(2):
                ins = nc.tensor.matmul(ps[:, 1 + 2 * t, 0:32], ones[64 * t:64 * t + 64, :], s_qk[64 * t:64 * t + 64, :],
                                       start=True, stop=True)
            ins.then_inc(fs["sn"], 1)
            pe.wait_ge(fs["biasc"], 2)
            pe.wait_ge(fs["snc"], 1)

        def pe_fox_soft(pe):
            pe.wait_ge(*freed("z", 1))
            pe.wait_ge(fs["mx"], 1)
            nc.tensor.transpose(ps[0:64, 2, 0:P], s_mx.rearrange("p b h -> p (b h)"), ident[:]).then_inc(fs["mt"], 1)
            pe.wait_ge(fs["mc"], 1)
            nc.tensor.matmul(ps[:, 3, 0:64], s_mc[0:64, :].to_broadcast([64, P]), ident[0:64, 0:64], start=True, stop=True)\
                .then_inc(fs["mb"], 1)
            pe.wait_ge(fs["sum"], 1)
            nc.tensor.matmul(ps[:, 2, 128:192], ones[:], s_sum.rearrange("p b h -> p (b h)"), start=True, stop=True)\
                .then_inc(fs["tot"], 1)

        s_pad = part(wk, 8000, 2, NPG, 2 * HB)
        s_out = part(xTf, 5248, 512)[0:2 * HB]

        def pool_fox_values(pool, i):
            pool.wait_ge(fs["free"], i * 8 + 34)
            for e in range(2):
                nc.gpsimd.tensor_copy(s_pad[:, e, :, HB * e:HB * e + HB],
                                      s_pr[:, ds(i * 2 + e, 1)].rearrange("p a g h -> p (a g) h")).then_inc(fs["small"], 1)

        def pe_fox_values(pe, i, e, q):
            if (e, q) == (0, 0):
                pe.wait_ge(fs["small"], i * 2 + 4)
            pe.wait_ge(fs[f"vring{q % 2}"], i * 256 + 64 * (2 * e + q // 2 + 1))
            for g in range(4):
                pg = 4 * q + g
                ins = nc.tensor.matmul(ps[0:2 * HB, 6, :], s_pad[:, e, pg, :], s_ring[:, q % 2, g, :],
                                       start=(e == 0 and pg == 0), stop=(e == 1 and pg == NPG - 1))
            ins.then_inc(fs["free"], 1)

        def pe_fox_turn(pe, i):
            pe.wait_ge(fs["pvc"], i * 2 + 1)
            for c in range(4):
                ins = nc.tensor.matmul(ps[:, 7, c * 2 * HB:(c + 1) * 2 * HB], s_out[:, c * P:(c + 1) * P],
                                       ident[0:2 * HB, 0:2 * HB], start=True, stop=True)
            ins.then_inc(fs["turned"], 1)

        def act_fox_rows(act):
            act.wait_ge(fs["qb"], 1)
            nc.scalar.activation(s_qb[:, 0:4, :], ps[:, 0:4, :], ACT.Copy).then_inc(fs["qbc"], 1)
            act.wait_ge(fs["lft"], 1)
            nc.scalar.activation(s_lf.rearrange("p h t -> p (h t)"), psf[:, 2048:3072], ACT.Copy).then_inc(fs["lfc"], 1)
            act.wait_ge(fs["qb"], 2)
            nc.scalar.activation(s_qb[:, 4:8, :], ps[:, 0:4, :], ACT.Copy).then_inc(fs["qbc"], 1)
            act.wait_ge(fs["bias"], 1)
            act.wait_ge(fs["lftot"], 1)
            nc.scalar.activation(s_lft, psf[:, 2048:3072], ACT.Copy).then_inc(fs["biasc"], 1)
            nc.scalar.activation(s_cq, ps[:, 6, 0:64].rearrange("p (h b) -> p b h", b=NB), ACT.Copy).then_inc(fs["biasc"], 1)

        def act_fox_soft(act):
            act.wait_ge(fs["sh"], 1)
            nc.scalar.activation(s_sc, s_sc, ACT.Exp).then_inc(fs["ex"], 1)
            nc.scalar.activation(s_sn, s_sn, ACT.Exp).then_inc(fs["ex"], 1)

        def act_fox_values(act, i):
            act.wait_ge(fs["free"], i * 8 + 42)
            nc.scalar.activation(s_out, ps[0:2 * HB, 6, :], ACT.Copy).then_inc(fs["pvc"], 1)

        def act_fox_turned(act, i):
            act.wait_ge(fs["turned"], i + 2)
            for c in range(4):
                ins = nc.scalar.activation(s_o[:, ds(i * 2, 2), 2 * c:2 * c + 2],
                                           ps[:, 7, c * 2 * HB:(c + 1) * 2 * HB].rearrange("p (e h) -> p e h", e=2)
                                           [:, :, 2 * c:2 * c + 2], ACT.Copy)
            ins.then_inc(fs["pvc"], 1)

        def dve_fox_rows(dve):
            link, vv = S["dve"].link, nc.vector
            dve.wait_ge(fs["turned"], 1)
            link(vv.tensor_copy(s_v, ps[:, 7, 0:32].rearrange("p (c b) -> p c b", b=NB)))
            dve.wait_ge(fs["small"], 2)
            vv.tensor_tensor(s_qk, s_q.rearrange("p c b -> p (c b)"), s_k.rearrange("p c b -> p (c b)"), ALU.mult)\
                .then_inc(fs["snp"], 1)
            dve.wait_ge(fs["lf"], 16)
            vv.tensor_reduce(s_tot, s_lft.rearrange("p (t h) -> p h t", h=HB), AX.X, ALU.add).then_inc(fs["lftot"], 1)
            dve.wait_ge(fs["sn"], 1)
            for t in range(2):
                ins = vv.tensor_copy(heads_even_odd(s_sn, t), ps[:, 1 + 2 * t, 0:32].rearrange("p (c b) -> p c b", b=NB))
                if t == 0:
                    link(ins)
            ins.then_inc(fs["snc"], 1)

        def dve_key_scores(dve, i, j, link):
            vv = nc.vector
            for s in range(2):
                q = 2 * (j % 2) + s
                dve.wait_ge(fs[f"ring{s}"], i * 256 + 64 * (j + 1))
                dve.wait_ge(fs["free"], i * 8 + (2 * j + s + 2))
                link(vv.tensor_tensor(s_prod.rearrange("p (g n) -> p g n", g=4), s_ring[:, s, :, :],
                                      s_qb[:, ds(i * 2 + j // 2, 1), :].to_broadcast([P, 4, 512]), ALU.mult))
                vv.tensor_reduce(s_sc[:, ds(i * 2 + j // 2, 1), 4 * q:4 * q + 4, :].rearrange("p a g h -> p (a g h)"),
                                 s_prod.rearrange("p (x n) -> p x n", n=DHB), AX.X, ALU.add).then_inc(fs["free"], 1)

        def dve_fox_soft(dve):
            link, vv = S["dve"].link, nc.vector
            dve.wait_ge(fs["free"], 34)
            dve.wait_ge(fs["biasc"], 2)
            link(vv.tensor_tensor(s_sc, s_sc, s_lft.rearrange("p (h b g) -> p b g h", h=HB, b=NB), ALU.add))
            cq = s_cq.rearrange("p b (a h) -> p b a h", a=1).to_broadcast([P, NB, NPG, HB])
            link(vv.tensor_tensor(s_sc, s_sc, cq, ALU.add))
            vv.tensor_reduce(s_mx, s_sc.rearrange("p b g h -> p b h g"), AX.X, ALU.max).then_inc(fs["mx"], 1)
            dve.wait_ge(fs["mt"], 1)
            vv.tensor_reduce(s_mc[0:64, :], ps[0:64, 2, 0:P], AX.X, ALU.max).then_inc(fs["mc"], 1)
            dve.wait_ge(fs["mb"], 1)
            link(vv.tensor_tensor(s_mb, ps[:, 3, 0:64].rearrange("p (b h) -> p b h", h=HB), s_sn, ALU.max))
            mb = s_mb.rearrange("p b (a h) -> p b a h", a=1).to_broadcast([P, NB, NPG, HB])
            link(vv.tensor_tensor(s_sn, s_sn, s_mb, ALU.subtract))
            vv.tensor_tensor(s_sc, s_sc, mb, ALU.subtract).then_inc(fs["sh"], 1)
            dve.wait_ge(fs["ex"], 1)
            vv.tensor_reduce(s_sum, s_sc.rearrange("p b g h -> p b h g"), AX.X, ALU.add).then_inc(fs["sum"], 1)
            dve.wait_ge(fs["ex"], 2)
            dve.wait_ge(fs["tot"], 1)
            link(vv.tensor_tensor(s_rs, ps[:, 2, 128:192].rearrange("p (b h) -> p b h", h=HB), s_sn, ALU.add))
            link(vv.reciprocal(s_rs, s_rs))
            link(vv.tensor_tensor(s_sn, s_sn, s_rs, ALU.mult))
            rs = s_rs.rearrange("p b (a h) -> p b a h", a=1).to_broadcast([P, NB, NPG, HB])
            vv.tensor_tensor(s_pr, s_sc, rs, ALU.mult).then_inc(fs["pr"], 1)

        def dve_fox_out(dve):
            link, vv = S["dve"].link, nc.vector
            dve.wait_ge(fs["pvc"], NB)
            for t in range(2):
                half = slice(64 * t, 64 * t + 64)
                link(vv.tensor_tensor(s_pv[half], s_v[half], heads_even_odd(s_sn, t)[half], ALU.mult))
                vv.tensor_tensor(aT[half, 4:8, SEQ:T], s_pv[half], s_o.rearrange("p b (c t) -> p t c b", t=2)[half, t],
                                 ALU.add).then_inc(fs["out"], 1)

        conv_done, conv_st, conv_pad, conv_silu = (sem("conv_" + n) for n in ("done", "st", "pad", "silu"))
        c_raw = part(wk, 6400, T + 3)
        c_tail = part(wk, 7800, 12, 3 + NB)
        c_st = part(wk, 7932, 12, 3, NB)

        def pool_conv(pool):
            pool.wait_ge(stored, 16 * 5)
            pool.wait_ge(fs["turned"], 1)
            nc.gpsimd.memset(c_raw[:, 0:3], 0.0).then_inc(conv_pad, 1)
            pool.dma_start(c_st, st_gconv_in).then_inc(conv_st, 16)

        def act_conv(act):
            g0 = GROUP0["conv"]
            act.wait_ge(conv_pad, 1)
            with act.Fori(0, 3) as i:
                for j in range(4):
                    st = (g0 + j) % 2
                    act.wait_ge(psum_ready, i * 4 + (g0 + j + 1))
                    nc.scalar.activation(c_tail[:, ds(i * 4 + j, 1), :].rearrange("p a n -> p (a n)"),
                                         ps[:, 3 * st + 2, N3 - NB - 3:N3], ACT.Copy)
                    nc.scalar.activation(thirds(c_raw[:, 3:T + 3]), psum_set(st), ACT.Copy).then_inc(psum_free, 1)
                    act.wait_ge(conv_done, i * 4 + (j + 1))
                    chunk = big[:, ds(i * 4 + j, 1), :].rearrange("p a n -> p (a n)")
                    nc.scalar.activation(chunk, chunk, ACT.Silu).then_inc(conv_silu, 1)

        def dve_conv(dve):
            vv, g0, w0 = nc.vector, GROUP0["conv"], VOFF["conv_a"][0]
            dve.wait_ge(stored, 16 * 5)
            dve.wait_ge(conv_st, 16)
            dve.wait_ge(fs["qbc"], 2)
            dve.sem_inc(fs["free"], 2)
            with S["dve"].loop(3, 4 * 9) as i:
                link = S["dve"].link
                for j in range(4):
                    dve.wait_ge(psum_free, i * 4 + (g0 + j + 1))
                    chunk = big[:, ds(i * 4 + j, 1), :].rearrange("p a n -> p (a n)")
                    for t in range(CA):
                        tap = vec[:, ds(i * 16 + (w0 + 4 * j + t), 1)]
                        row = c_st[:, ds(i * 4 + j, 1), t, :].rearrange("p a n -> p (a n)") if t < 3 else c_raw[:, SEQ + 3:]
                        if t == 0:
                            link(vv.tensor_scalar(chunk[:, SEQ:T], row, tap, None, ALU.mult))
                            link(vv.tensor_scalar(chunk[:, 0:SEQ], c_raw[:, 0:SEQ], tap, None, ALU.mult))
                            continue
                        link(vv.scalar_tensor_tensor(out=chunk[:, SEQ:T], in0=row, scalar=tap, in1=chunk[:, SEQ:T],
                                                     op0=ALU.mult, op1=ALU.add))
                        ins = vv.scalar_tensor_tensor(out=chunk[:, 0:SEQ], in0=c_raw[:, t:t + SEQ], scalar=tap,
                                                      in1=chunk[:, 0:SEQ], op0=ALU.mult, op1=ALU.add)
                        if t < 3:
                            link(ins)
                    ins.then_inc(conv_done, 1)
                    dve_key_scores(dve, i, j, link)
            for j in range(4):
                dve_key_scores(dve, 3, j, S["dve"].link)

        l2_sq, l2_ps, l2_rt = sem("l2_sq"), sem("l2_ps"), sem("l2_rt")
        l2_n = [0]
        l_st, l_rc = part(wk, 2100, 72), part(wk, 2180, 72)

        def act_squares(act, src, heads, scale):
            n0 = l2_n[0]
            for h in range(heads):
                if h >= 2:
                    act.wait_ge(l2_ps, n0 + h - 1)
                nc.scalar.activation(sq[:, h % 2, :], src[:, h, :], ACT.Square).then_inc(l2_sq, 1)
            act.wait_ge(l2_ps, n0 + heads)
            nc.scalar.activation(l_st[:, 0:9 * heads], ps[:, 6, 0:9 * heads], ACT.Sqrt, bias=eps[:, 0:1], scale=scale)\
                .then_inc(l2_rt, 1)

        def pe_squares(pe, n0, heads):
            for h in range(heads):
                pe.wait_ge(l2_sq, n0 + h + 1)
                for t in range(9):
                    ins = nc.tensor.matmul(ps[:, 6, h * 9 + t:h * 9 + t + 1], sq[:, h % 2, tile_at[t]:tile_at[t] + P],
                                           ones[:, 0:1], start=True, stop=True)
                ins.then_inc(l2_ps, 1)

        def dve_norm_gates(dve):
            link, vv = S["dve"].link, nc.vector
            dve.wait_ge(l2_rt, 1)
            link(vv.reciprocal(l_rc, l_st))
            rc = l_rc.rearrange("p (k h t) -> p k t h", k=2, t=9)
            link(vv.tensor_scalar(gt[:, :, G_RQ, :], rc[:, 0], float(P) ** -0.5, None, ALU.mult))
            link(vv.tensor_copy(gt[:, :, G_RK, :], rc[:, 1]))
            link(vv.tensor_tensor(gt[:, :, G_RQE, :], gt[:, :, G_RQ, :], gt[:, :, G_E, :], ALU.mult))
            vv.tensor_tensor(gt[:, :, G_RKB, :], gt[:, :, G_RK, :], gt[:, :, G_B, :], ALU.mult).then_inc(l2_rt, 1)

        gd = {n: sem("gd_" + n) for n in ("st", "bc", "n", "p", "dt", "ex", "kt", "vt", "kb", "lt", "l", "lc", "ed",
                                          "b", "x", "xc", "e", "u", "uc", "ws", "vn", "o", "oc", "s")}
        Q8 = 2 * HA * P

        def quad(buf, n):
            return part(buf, n * Q8, 2 * HA, P)

        kn, kb, qn, qg, vS, ktok, vb, kbg = (quad(hTf, n) for n in range(8))
        kd, DT, AT, LT, L_, E_, D_ = (quad(wk, n) for n in range(7))
        X_, B_, u_, wT, vn = DT, (LT, kn), kb, L_, D_
        S_ = part(wk, 7168, HA, P)
        cst = part(wk, 7680, 2, 11, 4)
        P01, P23, P45, P67 = (psf[:, 1024 * n:1024 * n + 1024].rearrange("p (x n) -> p x n", n=P) for n in range(4))

        def cc(kind, x):
            return cst[:, x // HA, kind, x % HA:x % HA + 1]

        def per_token(kind):
            return cst[:, :, kind, :].rearrange("p a (h n) -> p a h n", n=1).to_broadcast([P, 2, HA, P])

        def split(ap):
            return ap.rearrange("p (a h) n -> p a h n", a=2)

        def over8(m):
            return m.rearrange("p (a n) -> p a n", a=1).to_broadcast([P, 2 * HA, P])

        def pool_gdn(pool):
            pool.wait_ge(*freed("z", 1))
            pool.wait_ge(l2_rt, 2)
            pool.wait_ge(fs["pr"], 1)
            S["pool"].link(nc.gpsimd.memset(s_pad, 0.0))
            with pool.Fori(0, QT // 2) as i:
                pool.wait_ge(gd["s"], i * 2 + 1)
                pool_fox_values(pool, i)
                nc.gpsimd.tensor_copy(cst, gt[:, ds(i * 2, 2), :, :]).then_inc(gd["st"], 1)
                nc.gpsimd.tensor_copy(split(vS), big[:, 8:12, ds(i * 256, 256)].rearrange("p h (a n) -> p a h n", a=2))\
                    .then_inc(gd["st"], 1)
                pool.wait_ge(gd["kt"], i + 1)
                pool.wait_ge(gd["st"], i * 2 + 2)
                nc.gpsimd.tensor_tensor(split(kbg), split(ktok), per_token(G_BE), ALU.mult).then_inc(gd["kb"], 1)
                nc.gpsimd.tensor_tensor(split(kd), split(ktok), per_token(G_KD), ALU.mult).then_inc(gd["kb"], 1)
                for s in range(1, 7):
                    if s == 1:
                        pool.wait_ge(gd["ed"], i * 7 + 1)
                    elif s >= 3:
                        pool.wait_ge(gd["x"], i * 6 + (s - 2))
                    nc.gpsimd.tensor_tensor(B_[s % 2], L_, over8(lev[:, s, :]), ALU.mult).then_inc(gd["b"], 1)

        V_AT = {1: ((0, 0), (0, 1)), 2: ((0, 2), (0, 3)), 3: ((1, 0), (1, 1)), 4: ((1, 2), (1, 3))}

        def pe_gdn(pe):
            mm = nc.tensor.matmul

            def each(op, done, xs=range(2 * HA)):
                for x in xs:
                    ins = op(x)
                ins.then_inc(gd[done], 1)

            with pe.Fori(0, QT // 2) as i:
                pe.wait_ge(gd["st"], i * 2 + 2)
                pe.wait_ge(gd["oc"], i * 2 + 1)
                for to, kind in ((P01, G_RQ), (P23, G_RK), (P45, G_RQE), (P67, G_RKB)):
                    each(lambda x: mm(to[:, x, :], cc(kind, x).to_broadcast([P, P]), ident[:], start=True, stop=True), "bc")
                pe.wait_ge(gd["n"], i * 4 + 4)
                each(lambda x: mm(P45[:, x, :], cc(G_G, x).to_broadcast([P, P]), upper[:], start=True, stop=True), "p")
                each(lambda x: nc.tensor.transpose(P67[:, x, :], kn[:, x, :], ident[:]), "p")
                each(lambda x: mm(P23[:, x, :], kn[:, x, :], qn[:, x, :], start=True, stop=True), "p")
                each(lambda x: mm(P01[:, x, :], kn[:, x, :], kb[:, x, :], start=True, stop=True), "p")
                pe.wait_ge(gd["kt"], i + 1)
                each(lambda x: nc.tensor.transpose(P67[:, x, :], vS[:, x, :], ident[:]), "vt")
                pe.wait_ge(gd["lt"], i + 1)
                each(lambda x: nc.tensor.transpose(P01[:, x, :], LT[:, x, :], ident[:]), "l")
                for s in range(1, 7):
                    pe.wait_ge(gd["b"], i * 6 + s)
                    pe.wait_ge(gd["ed"], i * 7 + s)
                    each(lambda x: mm(P01[:, x, :], B_[s % 2][:, x, :], E_[:, x, :], start=True, stop=True), "x")
                    if s in V_AT:
                        pe_fox_values(pe, i, *V_AT[s][0])
                    if s == 6:
                        pe_fox_turn(pe, i)
                    pe.wait_ge(gd["xc"], i * 6 + s)
                    if s < 6:
                        for x in range(2 * HA):
                            mm(P45[:, x, :], X_[:, x, :], D_[:, x, :], start=True, stop=True)
                    each(lambda x: mm(P23[:, x, :], D_[:, x, :], X_[:, x, :], start=True, stop=True), "e")
                    if s in V_AT:
                        pe_fox_values(pe, i, *V_AT[s][1])
                pe.wait_ge(gd["ed"], i * 7 + 7)
                pe.wait_ge(gd["kb"], i * 2 + 2)
                for x in range(2 * HA):
                    mm(P01[:, x, :], E_[:, x, :], vb[:, x, :], start=True, stop=True)
                each(lambda x: mm(P23[:, x, :], kbg[:, x, :], E_[:, x, :], start=True, stop=True), "u")
                pe.wait_ge(gd["uc"], i * 2 + 2)
                for a in range(2):
                    hs = range(4 * a, 4 * a + 4)
                    pe.wait_ge(gd["s"], i * 2 + (a + 1))
                    each(lambda x: mm(P45[:, x % 4, :], wT[:, x, :], S_[:, x % 4, :], start=True, stop=True), "ws", hs)
                    pe.wait_ge(gd["vn"], i * 2 + (a + 1))
                    pe.wait_ge(gd["oc"], i * 2 + (a + 1))
                    pe.wait_ge(fs["pvc"], i * 2 + 2)
                    for x in hs:
                        mm(P67[:, x % 4, :], kd[:, x, :], vn[:, x, :], start=True, stop=True)
                        mm(P45[:, 4 + x % 4, :], S_[:, x % 4, :], qg[:, x, :], start=True, stop=False)
                        ins = mm(P45[:, 4 + x % 4, :], vn[:, x, :], AT[:, x, :], start=False, stop=True)
                    ins.then_inc(gd["o"], 1)

        def act_gdn(act):
            act.sem_inc(gd["oc"], 1)
            with act.Fori(0, QT // 2) as i:
                act.wait_ge(gd["p"], i * 4 + 2)
                nc.scalar.activation(ktok, P67, ACT.Copy).then_inc(gd["kt"], 1)
                act.wait_ge(gd["dt"], i + 1)
                nc.scalar.activation(DT, DT, ACT.Exp).then_inc(gd["ex"], 1)
                act.wait_ge(gd["l"], i + 1)
                nc.scalar.activation(L_, P01, ACT.Copy).then_inc(gd["lc"], 1)
                for s in range(1, 7):
                    act.wait_ge(gd["x"], i * 6 + s)
                    nc.scalar.activation(X_, P01, ACT.Copy).then_inc(gd["xc"], 1)
                    if s == 5:
                        act_fox_values(act, i)
                    if s == 6:
                        act_fox_turned(act, i)
                act.wait_ge(gd["u"], i + 1)
                nc.scalar.activation(u_, P01, ACT.Copy).then_inc(gd["uc"], 1)
                nc.scalar.activation(wT, P23, ACT.Copy).then_inc(gd["uc"], 1)
                for a in range(2):
                    act.wait_ge(gd["o"], i * 2 + (a + 1))
                    nc.scalar.activation(big[:, 8:12, ds(i * 256 + a * P, P)], P45[:, 4:8, :], ACT.Copy)\
                        .then_inc(gd["oc"], 1)

        def dve_gdn(dve):
            vv = nc.vector
            link = S["dve"].link
            dve.wait_ge(l2_rt, 2)
            vv.memset(S_, 0.0).then_inc(gd["s"], 1)
            with S["dve"].loop(QT // 2, 16) as i:
                link = S["dve"].link
                dve.wait_ge(gd["s"], i * 2 + 1)
                for n, (to, src, lo, bc) in enumerate(((qn, big, 0, P01), (kn, big, 4, P23), (qg, big, 0, P45),
                                                      (kb, big, 4, P67))):
                    dve.wait_ge(gd["bc"], i * 4 + (n + 1))
                    x = src[:, lo:lo + 4, ds(i * 256, 256)].rearrange("p h (a n) -> p a h n", a=2)
                    vv.tensor_tensor(split(to), x, split(bc), ALU.mult).then_inc(gd["n"], 1)
                dve.wait_ge(gd["p"], i * 4 + 1)
                for x in range(2 * HA):
                    ins = vv.scalar_tensor_tensor(out=DT[:, x, :], in0=P45[:, x, :], scalar=cc(G_GC, x), in1=neg_ji[:],
                                                  op0=ALU.subtract, op1=ALU.add)
                    if x < 2 * HA - 1:
                        link(ins)
                ins.then_inc(gd["dt"], 1)
                dve.wait_ge(gd["p"], i * 4 + 4)
                dve.wait_ge(gd["ex"], i + 1)
                link(vv.tensor_tensor(AT, P23, DT, ALU.mult))
                link(vv.tensor_tensor(DT, DT, over8(strict[:, :]), ALU.mult))
                vv.tensor_tensor(LT, P01, DT, ALU.mult).then_inc(gd["lt"], 1)
                dve.wait_ge(gd["vt"], i + 1)
                link(vv.tensor_tensor(split(vb), split(P67), per_token(G_B), ALU.mult))
                dve.wait_ge(gd["lt"], i + 1)
                link(vv.tensor_tensor(E_, LT, over8(lev0T[:, :]), ALU.mult))
                link(vv.tensor_tensor(E_, over8(ident[:, :]), E_, ALU.subtract))
                dve.wait_ge(gd["lc"], i + 1)
                link(vv.tensor_tensor(D_, L_, over8(lev[:, 0, :]), ALU.mult))
                vv.tensor_tensor(D_, over8(ident[:, :]), D_, ALU.subtract).then_inc(gd["ed"], 1)
                for s in range(1, 7):
                    dve.wait_ge(gd["e"], i * 6 + s)
                    dve.wait_ge(gd["ed"], i * 7 + s)
                    if s < 6:
                        vv.tensor_tensor(D_, D_, P45, ALU.subtract)
                    vv.tensor_tensor(E_, E_, P23, ALU.subtract).then_inc(gd["ed"], 1)
                for a in range(2):
                    dve.wait_ge(gd["ws"], i * 2 + (a + 1))
                    dve.wait_ge(gd["uc"], i * 2 + 2)
                    vv.tensor_tensor(vn[:, 4 * a:4 * a + 4, :], u_[:, 4 * a:4 * a + 4, :], P45[:, 0:4, :], ALU.subtract)\
                        .then_inc(gd["vn"], 1)
                    dve.wait_ge(gd["o"], i * 2 + (a + 1))
                    for h in range(HA):
                        ins = vv.scalar_tensor_tensor(out=S_[:, h, :], in0=S_[:, h, :], scalar=cc(G_EL, 4 * a + h),
                                                      in1=P67[:, h, :], op0=ALU.mult, op1=ALU.add)
                        if h < HA - 1 and a == 0:
                            link(ins)
                    ins.then_inc(gd["s"], 1)

        gs = {n: sem("gs_" + n) for n in ("st", "cb", "n", "ps", "vn", "vr", "out")}
        NS = HA * NB
        st = part(hTf, 0, NB, HA, P)
        g_cb = part(wk, 4400, 6, HA, NB)
        g_q, g_k, g_vb, g_qk, g_vn = (part(wk, 4600 + 32 * n, HA, NB) for n in range(5))
        g_pair = part(wk, 4800, HA, NB, 2)
        KINDS = (G_RQ, G_RK, G_RQE, G_BE, G_B, G_EL)

        def pool_gdn_rows(pool):
            pool.wait_ge(gd["s"], QT + 1)
            store(pool, gdn_p, S_)
            pool.dma_start(st.rearrange("p b h n -> p (b h) n"), st_gdn.rearrange("b h p n -> p (b h) n"))\
                .then_inc(gs["st"], 16)
            pool.wait_ge(fs["out"], 2)
            pool.dma_start(xT[:], xT_in).then_inc(fs["back"], 16)

        def pe_gdn_rows(pe):
            pe.wait_ge(gd["oc"], QT + 1)
            for n, kind in enumerate(KINDS):
                for h in range(HA):
                    ins = nc.tensor.matmul(ps[:, 7, (n * HA + h) * NB:(n * HA + h + 1) * NB],
                                           gt[:, QT, kind, h:h + 1].to_broadcast([P, P]), ident[:, P - NB:P],
                                           start=True, stop=True)
            ins.then_inc(gs["cb"], 1)
            pe.wait_ge(gs["st"], 16)
            pe.wait_ge(gs["n"], 1)
            for h in range(HA):
                for b in range(NB):
                    nc.tensor.matmul(ps[:, 6, 2 * (h * NB + b):2 * (h * NB + b) + 2], st[:, b, h, :], g_pair[:, h, b, :],
                                     start=True, stop=True)
            nc.tensor.matmul(ps[:, 7, 256:288], ones[:], g_qk.rearrange("p h b -> p (h b)"), start=True, stop=True)\
                .then_inc(gs["ps"], 1)
            pe.wait_ge(gs["vn"], 1)
            for h in range(HA):
                for b in range(NB):
                    x = b * HA + h
                    ins = nc.tensor.matmul(psf[:, x * P:x * P + P], g_vn[:, h, b:b + 1].to_broadcast([P, P]), ident[:],
                                           start=True, stop=True)
            ins.then_inc(gs["vr"], 1)

        def dve_gdn_rows(dve):
            link, vv = S["dve"].link, nc.vector
            dve.wait_ge(gs["cb"], 1)
            link(vv.tensor_copy(g_cb, ps[:, 7, 0:192].rearrange("p (n h b) -> p n h b", n=6, b=NB)))
            cols = big[:, :, SEQ:T]
            link(vv.tensor_tensor(g_q, cols[:, 0:4], g_cb[:, 0], ALU.mult))
            link(vv.tensor_tensor(g_k, cols[:, 4:8], g_cb[:, 1], ALU.mult))
            link(vv.tensor_tensor(g_pair[:, :, :, 1], cols[:, 0:4], g_cb[:, 2], ALU.mult))
            link(vv.tensor_tensor(g_pair[:, :, :, 0], g_k, g_cb[:, 3], ALU.mult))
            link(vv.tensor_tensor(g_vb, cols[:, 8:12], g_cb[:, 4], ALU.mult))
            vv.tensor_tensor(g_qk, g_q, g_k, ALU.mult).then_inc(gs["n"], 1)
            dve.wait_ge(gs["ps"], 1)
            pr = ps[:, 6, 0:2 * NS].rearrange("p (h b t) -> p h b t", b=NB, t=2)
            qk = ps[:, 7, 256:288].rearrange("p (h b) -> p h b", b=NB)
            link(vv.tensor_tensor(g_vn, g_vb, pr[:, :, :, 0], ALU.subtract))
            link(vv.tensor_tensor(g_qk, qk, g_vn, ALU.mult))
            vv.tensor_tensor(cols[:, 8:12], g_qk, pr[:, :, :, 1], ALU.add).then_inc(gs["vn"], 1)
            dve.wait_ge(gs["vr"], 1)

            def decay(x):
                b, h = divmod(x, HA)
                return vv.tensor_scalar(st[:, b, h, :], st[:, b, h, :], g_cb[:, 5, h, b:b + 1], None, ALU.mult)

            def update(x):
                b, h = divmod(x, HA)
                return vv.scalar_tensor_tensor(out=st[:, b, h, :], in0=psf[:, x * P:x * P + P], scalar=g_k[:, h, b:b + 1],
                                               in1=st[:, b, h, :], op0=ALU.mult, op1=ALU.add)

            lag = S["dve"].lag
            lag(decay(0))
            for x in range(1, NS):
                lag(decay(x))
                lag(update(x - 1))
            link(update(NS - 1))
            dve.sem_inc(gs["out"], 1)

        gn = {n: sem("gn_" + n) for n in ("rc", "bc", "u")}
        n_t = part(wk, 2300, 2, T)

        def pe_head_norm(pe):
            pe.wait_ge(gs["out"], 1)
            pe_squares(pe, 8, HA)
            pe.wait_ge(gn["rc"], 1)
            for h in range(HA):
                if h >= 2:
                    pe.wait_ge(gn["u"], h - 1)
                base = 1536 * (h % 2)
                for t in range(9):
                    cnt = P if t < QT else NB
                    ins = nc.tensor.matmul(psf[:, base + t * P:base + t * P + cnt],
                                           l_rc[:, h * 9 + t:h * 9 + t + 1].to_broadcast([P, P]), ident[:, P - cnt:P],
                                           start=True, stop=True)
                ins.then_inc(gn["bc"], 1)

        def dve_head_norm(dve):
            link, vv = S["dve"].link, nc.vector
            dve.wait_ge(l2_rt, 3)
            vv.reciprocal(l_rc[:, 0:36], l_st[:, 0:36]).then_inc(gn["rc"], 1)
            for h in range(HA):
                dve.wait_ge(gn["bc"], h + 1)
                if h >= 2:
                    dve.wait_ge(gn["u"], h - 1)
                link(vv.scalar_tensor_tensor(out=n_t[:, h % 2], in0=big[:, 8 + h, :], scalar=v("gnorm"),
                                             in1=psf[:, 1536 * (h % 2):1536 * (h % 2) + T], op0=ALU.mult, op1=ALU.mult))
                vv.tensor_tensor(aT[:, h, :], aT[:, h, :], n_t[:, h % 2], ALU.mult).then_inc(gn["u"], 1)

        def residual(dve, name, pairs):
            dve.wait_ge(psum_free, GROUP0[name])
            epilogue(dve, name, pairs, lambda i, j, st: nc.vector.tensor_tensor(
                at_chunk(xT, i * 4 + j), at_chunk(xT, i * 4 + j), psum_set(st), ALU.add))

        q32 = la[:, 0:XW].rearrange("p (c t) -> p c t", c=KC)
        m_raw, m_n = part(la, 0, KC, NMEM), part(la, 2048, KC, NMEM)
        m_k, m_v = part(la, XW, KC, NMEM), part(la, XW + 2048, 2, D)
        x_ring = part(la, 12352, 2, 2, D)
        xa = {n: sem("xa_" + n) for n in ("mem", "q", "qs", "s", "m", "e", "p", "t", "tc", "o", "oc", "col",
                                          "qb", "qbc", "oh", "free", "mx", "mt", "mc", "mb", "sh", "ex", "sum", "tot", "pr", "pv",
                                          "pvc", "ring0", "ring1", "vr0", "vr1")}
        x_q = part(la, 2 * XW, 2, KC, P)
        x_p = part(la, 12352, 2, HX, NMEM)
        x_t = part(la, 14400, 2, KC, P)
        x_st = part(la, 18576, 2, 3, HX)
        k_ring, r_prod, r_qb = part(xTf, 0, 2, 2, D), part(xTf, 4 * D, 2, D), part(xTf, 6 * D, 2, D)
        r_pad = part(la, 2 * XW, NB, 2, NB * HX)
        r_out = part(la, 2 * XW + 512, D)[0:NB * HX]
        r_sc = part(la, 18624, NB, 2, HX)
        r_mx, r_mb, r_sum, r_rs = (part(la, 18720 + 32 * n, NB, HX) for n in range(4))
        r_mc, r_col = part(la, 18860, 1), part(la, 18870, 2, KC)

        cat_hi, cat_lo, mix_free = sem("cat_hi"), sem("cat_lo"), sem("mix_free")

        def act_cat(act):
            act.wait_ge(mix_free, 1)
            for c in range(KC):
                nc.scalar.activation(h_hi[:, c, :], aT[:, c, :], ACT.Copy).then_inc(cat_hi, 1)

        def dve_cat(dve):
            for c in range(KC):
                dve.wait_ge(cat_hi, c + 1)
                nc.vector.tensor_tensor(h_lo[:, c, :], aT[:, c, :], h_hi[:, c, :].bitcast(F32), ALU.subtract)\
                    .then_inc(cat_lo, 1)

        v_slots = [k_ring[:, 0], k_ring[:, 1], x_ring[:, 0], x_ring[:, 1]]
        V_SEMS = ("ring0", "ring1", "vr0", "vr1")

        def pe_memory(pe, l):
            for name in (f"mk{l}", f"mv{l}"):
                t0, g0 = TILE0[name], GROUP0[name]
                with pe.Fori(0, 2) as i:
                    for j in range(4):
                        pe.wait_ge(w_loaded[j % 2], i * 32 + 16 * (NPAIRS + (t0 + j) // 2 + 1))
                        pe.wait_ge(psum_free, i * 4 + (g0 + j - 1))
                        if name[1] == "k":
                            for k in range(KC):
                                ins = nc.tensor.matmul(ps[:, 3 * (j % 2), 0:NMEM], w_raw[:, j % 2, k, :], m_n[:, k, :],
                                                       start=(k == 0), stop=(k == KC - 1))
                        else:
                            for m in range(2):
                                for k in range(KC):
                                    ins = nc.tensor.matmul(ps[:, 3 * (j % 2), m * P:(m + 1) * P],
                                                           m_n[:, k, m * P:(m + 1) * P], w_raw[:, j % 2, k, :],
                                                           start=(k == 0), stop=(k == KC - 1))
                        ins.then_inc(psum_ready, 1)

        def pool_cross(pool, l):
            pool.dma_start(m_raw, memT_in).then_inc(xa["mem"], 16)
            if l == 0:
                pool_split(pool, 2, TILE0["out"] + 8)
            pool_hand_back(pool, f"mk{l}")
            pool_hand_back(pool, f"mv{l}")
            pool.wait_ge(*freed(f"mv{l}", 2))
            store(pool, mkT[l].rearrange("(c p) m -> p c m", p=P), m_k)
            store(pool, mv[l].rearrange("(t p) n -> p t n", p=P), m_v)
            pool.wait_ge(nm_out, OUT0[X_NORM[l]] + 8)
            store(pool, x_spill, xT[:])
            split_tiles(pool, f"xq{l}")
            xo = TILE0[f"xo{l}"]
            pool_split(pool, xo, xo + 2)
            pool.wait_ge(stored, 16 * n_stored[0])

            def key_row(b, e):
                pool.dma_start(k_ring[:, e], cmk[l, b].rearrange("a (t p) n -> p (a t) n", p=P))\
                    .then_inc(xa[f"ring{e}"], 16)

            for e in range(2):
                key_row(ds(e, 1), e)
            pool.wait_ge(*freed(f"xq{l}", 2))
            for e in range(2):
                nc.gpsimd.tensor_copy(x_q[:, e], q32[:, :, e * P:(e + 1) * P]).then_inc(xa["qs"], 1)
            with pool.Fori(0, 3) as r:
                for e in range(2):
                    pool.wait_ge(xa["s"], r * 2 + (8 * l + e + 1))
                    nc.gpsimd.tensor_copy(x_q[:, e], q32[:, :, ds(r * 256 + (2 + e) * P, P)]).then_inc(xa["qs"], 1)
                    pool.wait_ge(xa["free"], r * 2 + (8 * l + e + 1))
                    key_row(ds(r * 2 + (2 + e), 1), e)
            for b in range(NB):
                if b < 2:
                    pool.wait_ge(xa["free"], 8 * l + 7 + b)
                elif b < 4:
                    pool.wait_ge(xa["oc"], 8 * l + 10)
                else:
                    pool.wait_ge(xa["pv"], 9 * l + b - 3)
                pool.dma_start(v_slots[b % 4], cmv[l, b].rearrange("(t p) n -> p t n", p=P))\
                    .then_inc(xa[V_SEMS[b % 4]], 16)
            pool.wait_ge(xa["pv"], 9 * l + 6)
            pool.dma_start(xT[:], x_spill).then_inc(fs["back"], 16)
            pool_split(pool, xo + 2, xo + 8)
            split_tiles(pool, f"up{l}0", f"down{l}{FF_GROUPS - 1}")

        def pe_cross(pe, l):
            mm = nc.tensor.matmul

            def scores(r, e, ahead=0):
                n = 8 * l + e + ahead
                pe.wait_ge(xa["qs"], r * 2 + (n + 1))
                pe.wait_ge(xa["e"], r * 2 + (n + 1))
                for h in range(HX):
                    for c in range(2):
                        ins = mm(psf[:, e * 1024 + h * 256:e * 1024 + h * 256 + 256], x_q[:, e, 2 * h + c, :],
                                 m_k[:, 2 * h + c, :], start=(c == 0), stop=(c == 1))
                ins.then_inc(xa["s"], 1)

            def query(r, e):
                pe.wait_ge(xa["col"], r * 2 + (8 * l + e + 1))
                pe.wait_ge(xa["tc"], r * 2 + (8 * l + e + 2))
                for c in range(KC):
                    ins = mm(psf[:, 2048 + c * P:2048 + (c + 1) * P], r_col[:, e, c:c + 1].to_broadcast([P, P]), ident[:],
                             start=True, stop=True)
                ins.then_inc(xa["qb"], 1)

            def turn(r, e):
                pe.wait_ge(xa["q"], r * 2 + (8 * l + e + 1))
                pe.wait_ge(xa["p"], r * 2 + (8 * l + e + 1))
                pe.wait_ge(xa["tc"], r * 2 + (8 * l + e + 1))
                for h in range(HX):
                    for m in range(2):
                        ins = nc.tensor.transpose(psf[:, 2048 + (2 * h + m) * P:2048 + (2 * h + m + 1) * P],
                                                  x_p[:, e, h, m * P:(m + 1) * P], ident[:])
                ins.then_inc(xa["t"], 1)

            def values(r, e):
                pe.wait_ge(xa["tc"], r * 2 + (8 * l + e + 2))
                pe.wait_ge(xa["oc"], r * 2 + (8 * l + e + 2))
                for c in range(KC):
                    for m in range(2):
                        ins = mm(psf[:, 3072 + c * P:3072 + (c + 1) * P], m_v[:, m, c * P:(c + 1) * P],
                                 x_t[:, e, 2 * (c // 2) + m, :], start=(m == 0), stop=(m == 1))
                ins.then_inc(xa["o"], 1)

            pe.wait_ge(*freed(f"xq{l}", 2))
            scores(0, 0)
            with pe.Fori(0, 3) as r:
                turn(r, 0)
                scores(r, 1)
                query(r, 0)
                values(r, 0)
                turn(r, 1)
                scores(r, 0, 2)
                query(r, 1)
                values(r, 1)
            turn(3, 0)
            scores(3, 1)
            query(3, 0)
            values(3, 0)
            turn(3, 1)
            query(3, 1)
            values(3, 1)
            pe.wait_ge(xa["oc"], 8 * l + 10)
            pe.wait_ge(xa["q"], 8 * l + 9)
            pe.wait_ge(xa["mx"], l + 1)
            nc.tensor.transpose(ps[0:32, 2, 0:P], r_mx.rearrange("p b h -> p (b h)"), ident[:]).then_inc(xa["mt"], 1)
            pe.wait_ge(xa["mc"], l + 1)
            mm(ps[:, 3, 0:32], r_mc[0:32, :].to_broadcast([32, P]), ident[0:32, 0:32], start=True, stop=True)\
                .then_inc(xa["mb"], 1)
            pe.wait_ge(xa["sum"], l + 1)
            mm(ps[:, 2, 128:160], ones[:], r_sum.rearrange("p b h -> p (b h)"), start=True, stop=True).then_inc(xa["tot"], 1)
            pe.wait_ge(xa["pr"], l + 1)
            for b in range(NB):
                pe.wait_ge(xa[V_SEMS[b % 4]], 16 * (b // 4 + ((6 * l + 5) if b % 4 < 2 else (2 * l + 1))))
                for m in range(2):
                    for n in range(2):
                        ins = mm(ps[0:NB * HX, 4 + n, :], r_pad[:, b, m, :], v_slots[b % 4][:, m, n * 512:(n + 1) * 512],
                                 start=(b == 0 and m == 0), stop=(b == NB - 1 and m == 1))
                ins.then_inc(xa["pv"], 1)
            pe.wait_ge(xa["pvc"], 2 * l + 1)
            for c in range(KC):
                ins = nc.tensor.transpose(ps[:, 6, c * NB * HX:(c + 1) * NB * HX], r_out[:, c * P:(c + 1) * P],
                                          ident[0:NB * HX, 0:NB * HX])
            ins.then_inc(xa["pv"], 1)
            pe.wait_ge(xa["pvc"], 2 * l + 2)

        def own(h):
            return ps[:, 6, 0:256].rearrange("p (c b h) -> p c b h", b=NB, h=HX)[:, 2 * h:2 * h + 2, :, h]

        def act_cross(act, l):
            if l == 0:
                for k, n in (("e", 2), ("tc", 1), ("oc", 2), ("q", 1)):
                    act.sem_inc(xa[k], n)
            def exps(r, e, ahead=0):
                act.wait_ge(xa["m"], r * 2 + (8 * l + e + ahead + 1))
                for h in range(HX):
                    ins = nc.scalar.activation(x_p[:, e, h, :], psf[:, e * 1024 + h * 256:e * 1024 + h * 256 + 256],
                                               ACT.Exp, bias=x_st[:, e, 0, h:h + 1], accum_out=x_st[:, e, 1, h:h + 1])
                ins.then_inc(xa["e"], 1)

            def turned(r, e):
                act.wait_ge(xa["t"], r * 2 + (8 * l + e + 1))
                nc.scalar.activation(x_t[:, e], psf[:, 2048:3072].rearrange("p (a n) -> p a n", n=P), ACT.Copy)\
                    .then_inc(xa["tc"], 1)

            def out(r, e):
                act.wait_ge(xa["o"], r * 2 + (8 * l + e + 1))
                nc.scalar.activation(h_hi[:, :, ds(r * 256 + e * P, P)],
                                     psf[:, 3072:4096].rearrange("p (c n) -> p c n", n=P), ACT.Copy).then_inc(xa["oh"], 1)

            def column(r, e):
                act.wait_ge(xa["qbc"], r * 2 + (8 * l + e + 1))
                nc.scalar.activation(r_col[:, e], q32[:, :, ds(r * 2 + (SEQ + e), 1)].rearrange("p c a -> p (c a)"),
                                     ACT.Copy).then_inc(xa["col"], 1)

            def query(r, e):
                act.wait_ge(xa["qb"], r * 2 + (8 * l + e + 1))
                nc.scalar.activation(r_qb[:, e], psf[:, 2048:3072], ACT.Copy).then_inc(xa["q"], 1)

            act.wait_ge(xa["ring1"], 16 * (6 * l + 1))
            exps(0, 0)
            with act.Fori(0, 3) as r:
                for e in range(2):
                    column(r, e)
                    turned(r, e)
                    exps(r, 1 - e, 2 * e)
                    query(r, e)
                    out(r, e)
            column(3, 0)
            turned(3, 0)
            exps(3, 1)
            query(3, 0)
            out(3, 0)
            column(3, 1)
            turned(3, 1)
            query(3, 1)
            out(3, 1)
            act.wait_ge(xa["sh"], l + 1)
            nc.scalar.activation(r_sc, r_sc, ACT.Exp).then_inc(xa["ex"], 1)
            act.wait_ge(xa["pv"], 9 * l + 8)
            nc.scalar.activation(r_out, psf[0:NB * HX, 2048:3072], ACT.Copy).then_inc(xa["pvc"], 1)
            act.wait_ge(xa["pv"], 9 * l + 9)
            for h in range(HX):
                ins = nc.scalar.activation(h_hi[:, 2 * h:2 * h + 2, SEQ:T], own(h), ACT.Copy)
            ins.then_inc(xa["oh"], 1)

        def dve_cross(dve, l):
            vv = nc.vector
            def soft(r, e, ahead=0):
                n = 8 * l + e + ahead
                dve.wait_ge(xa["s"], r * 2 + (n + 1))
                vv.tensor_reduce(x_st[:, e, 0, :], psf[:, e * 1024:e * 1024 + 1024].rearrange("p (h n) -> p h n", h=HX),
                                 AX.X, ALU.max, negate=True).then_inc(xa["m"], 1)
                dve.wait_ge(xa["e"], r * 2 + (n + 3))
                S["dve"].link(vv.reciprocal(x_st[:, e, 2, :], x_st[:, e, 1, :]))
                rs = x_st[:, e, 2, :].rearrange("p (h n) -> p h n", n=1).to_broadcast([P, HX, NMEM])
                vv.tensor_tensor(x_p[:, e], x_p[:, e], rs, ALU.mult).then_inc(xa["p"], 1)

            def rest(r, e):
                cols = slice(None), slice(None), ds(r * 256 + e * P, P)
                dve.wait_ge(xa["oh"], r * 2 + (9 * l + e + 1))
                vv.tensor_tensor(h_lo[cols], psf[:, 3072:4096].rearrange("p (c n) -> p c n", n=P),
                                 h_hi[cols].bitcast(F32), ALU.subtract).then_inc(xa["oc"], 1)

            def row(r, e):
                dve.wait_ge(xa["q"], r * 2 + (8 * l + e + 2))
                dve.wait_ge(xa[f"ring{e}"], r * 16 + 16 * (6 * l + 1))
                dve.wait_ge(xa["qbc"], r * 2 + (8 * l + e + 2))
                S["dve"].link(vv.tensor_tensor(r_prod, k_ring[:, e],
                                               r_qb[:, e].rearrange("p (a n) -> p a n", a=1).to_broadcast([P, 2, D]), ALU.mult))
                dve.sem_inc(xa["free"], 1)
                vv.tensor_reduce(r_sc[:, ds(r * 2 + e, 1), :, :].rearrange("p a m h -> p (a m h)"),
                                 r_prod.rearrange("p m (h n) -> p (m h) n", n=DHX), AX.X, ALU.add).then_inc(xa["qbc"], 1)

            if l == 0:
                dve.sem_inc(xa["qbc"], 2)
            soft(0, 0)
            with S["dve"].loop(3, 4) as r:
                for e in range(2):
                    soft(r, 1 - e, 2 * e)
                    rest(r, e)
                    row(r, e)
            soft(3, 1)
            rest(3, 0)
            row(3, 0)
            rest(3, 1)
            row(3, 1)
            link = S["dve"].link
            dve.wait_ge(xa["qbc"], 8 * l + 10)
            vv.tensor_reduce(r_mx, r_sc.rearrange("p b m h -> p b h m"), AX.X, ALU.max).then_inc(xa["mx"], 1)
            dve.wait_ge(xa["mt"], l + 1)
            vv.tensor_reduce(r_mc[0:32, :], ps[0:32, 2, 0:P], AX.X, ALU.max).then_inc(xa["mc"], 1)
            dve.wait_ge(xa["mb"], l + 1)
            link(vv.tensor_copy(r_mb, ps[:, 3, 0:32].rearrange("p (b h) -> p b h", h=HX)))

            def over_mem(x):
                return x.rearrange("p b (a h) -> p b a h", a=1).to_broadcast([P, NB, 2, HX])

            vv.tensor_tensor(r_sc, r_sc, over_mem(r_mb), ALU.subtract).then_inc(xa["sh"], 1)
            dve.wait_ge(xa["ex"], l + 1)
            vv.tensor_reduce(r_sum, r_sc.rearrange("p b m h -> p b h m"), AX.X, ALU.add).then_inc(xa["sum"], 1)
            dve.wait_ge(xa["tot"], l + 1)
            link(vv.reciprocal(r_rs, ps[:, 2, 128:160].rearrange("p (b h) -> p b h", h=HX)))
            link(vv.memset(r_pad, 0.0))
            for b in range(NB):
                ins = vv.tensor_tensor(r_pad[:, b, :, HX * b:HX * b + HX], r_sc[:, b],
                                       r_rs[:, b:b + 1, :].to_broadcast([P, 2, HX]), ALU.mult)
            ins.then_inc(xa["pr"], 1)
            dve.wait_ge(xa["oh"], 9 * l + 9)
            for h in range(HX):
                ins = vv.tensor_tensor(h_lo[:, 2 * h:2 * h + 2, SEQ:T], own(h),
                                       h_hi[:, 2 * h:2 * h + 2, SEQ:T].bitcast(F32), ALU.subtract)
            ins.then_inc(xa["pvc"], 1)

        ff_sq, ff_hi, ff_lo = sem("ff_sq"), sem("ff_hi"), sem("ff_lo")

        def act_up(act, l, g):
            name = f"up{l}{g}"
            g0 = GROUP0[name]
            n0 = 8 * (FF_GROUPS * l + g)
            act.wait_ge(psum_free, g0)
            if n0 == 0:
                act.sem_inc(ff_lo, 2)
            with act.Fori(0, 2) as i:
                for j in range(4):
                    act.wait_ge(ff_lo, i * 4 + (n0 + j + 1))
                    act.wait_ge(psum_ready, i * 4 + (g0 + j + 1))
                    nc.scalar.activation(thirds(tt[:, j % 2]), psum_set(j % 2), ACT.Relu).then_inc(psum_free, 1)
                    act.wait_ge(ff_sq, i * 4 + (n0 + j + 1))
                    nc.scalar.activation(a_hi[:, ds(i * 4 + j, 1), :].rearrange("p a n -> p (a n)"), tt[:, j % 2], ACT.Copy)\
                        .then_inc(ff_hi, 1)

        def dve_up(dve, l, g):
            g0 = GROUP0[f"up{l}{g}"]
            n0 = 8 * (FF_GROUPS * l + g)
            with dve.Fori(0, 2) as i:
                for j in range(4):
                    dve.wait_ge(psum_free, i * 4 + (g0 + j + 1))
                    nc.vector.tensor_tensor(tt[:, j % 2], tt[:, j % 2], tt[:, j % 2], ALU.mult).then_inc(ff_sq, 1)
                    dve.wait_ge(ff_hi, i * 4 + (n0 + j + 1))
                    chunk = slice(None), ds(i * 4 + j, 1), slice(None)
                    nc.vector.tensor_tensor(a_lo[chunk].rearrange("p a n -> p (a n)"), tt[:, j % 2],
                                            a_hi[chunk].rearrange("p a n -> p (a n)").bitcast(F32), ALU.subtract)\
                        .then_inc(ff_lo, 1)

        def by_chunk(sem_, base):
            return lambda pe, k: pe.wait_ge(sem_, base + k + 1)

        def at_once(*pairs):
            return lambda pe, k: after(*pairs)(pe) if k == 0 else None

        def pe_mlp(pe, l):
            for g in range(FF_GROUPS):
                pe_product3(pe, f"up{l}{g}", 2, h_hi, h_lo, by_chunk(nm_out, OUT0[F_NORM[l]]))
                pe_product3(pe, f"down{l}{g}", 2, a_hi, a_lo, by_chunk(ff_lo, 8 * (FF_GROUPS * l + g) + 2))

        cm = {n: sem("cm_" + n) for n in ("pad", "st", "glu", "diag", "used", "pv", "out", "sum", "by_pe", "by_act", "xc")}
        GW = CC - 1 + T
        glu = part(la, 0, KC, GW)
        d_sg = part(la, KC * GW, 2, T)
        d_st = part(la, KC * GW + 2 * T, KC, NB, CC - 1)
        d_y = part(la, 12480, 2, SEQ)
        d_tmp = part(la, 14528, 2, NB, CC - 1)
        d_s8 = part(la, 15008, 2, NB)
        d_diag = part(la, 15040, 2, P)
        d_tail = part(la, 18600, KC, CC - 1 + NB)
        glu_y = glu[:, :, 0:T]

        def pool_conformer(pool):
            pool.wait_ge(nm_out, 40)
            nc.gpsimd.memset(glu[:, :, 0:CC - 1], 0.0).then_inc(cm["pad"], 1)
            pool.dma_start(d_st, st_cconv_in).then_inc(cm["st"], 16)

        def pool_gates(pool):
            t0 = TILE0["pw1"] + 2
            with S["pool"].loop(4, 4) as i:
                for h in range(2):
                    for s in range(2):
                        split_tile(pool, s, i * 2 + h, t0)
                    pool.wait_ge(psum_free, i * 4 + (GROUP0["pw1"] + 2 * h + 2))
                    x = glu[:, ds(i * 2 + h, 1), CC - 1:].rearrange("p a n -> p (a n)")
                    nc.gpsimd.tensor_tensor(x, x, d_sg[:, h, :], ALU.mult).then_inc(cm["glu"], 1)

        def pe_conv(pe):
            pe.wait_ge(*freed("pw1", 4))
            pe.wait_ge(cm["glu"], 10)

            def tap(t, h, n, start, stop):
                pe.wait_ge(cm["diag"], n)
                x = glu[:, 6 + h, ds(t, SEQ)]
                for half in range(2):
                    ins = nc.tensor.matmul(ps[:, 2 * h + half, :], d_diag[:, h, :], x[:, half * 512:half * 512 + 512],
                                           start=start, stop=stop)
                return ins

            for h in range(2):
                tap(0, h, h + 1, True, False).then_inc(cm["used"], 1)
            with pe.Fori(0, CC - 2) as t:
                for h in range(2):
                    tap(t + 1, h, t * 2 + (h + 3), False, False).then_inc(cm["used"], 1)
            for h in range(2):
                tap(CC - 1, h, 2 * CC - 1 + h, False, True).then_inc(cm["used"], 1)

        def act_conv_taps(act):
            w0 = VOFF["w_dw"][0]
            for h in range(2):
                nc.scalar.activation(d_diag[:, h, :], ident[:], ACT.Copy, scale=vec[:, w0 + (6 + h) * CC:w0 + (6 + h) * CC + 1])\
                    .then_inc(cm["diag"], 1)
            with act.Fori(0, CC - 1) as t:
                for h in range(2):
                    act.wait_ge(cm["used"], t * 2 + (h + 1))
                    nc.scalar.activation(d_diag[:, h, :], ident[:], ACT.Copy,
                                         scale=vec[:, ds(t + (w0 + (6 + h) * CC + 1), 1)]).then_inc(cm["diag"], 1)
            for h in range(2):
                act.wait_ge(cm["used"], 2 * CC - 1 + h)
                nc.scalar.activation(glu[:, 6 + h, 0:SEQ], psf[:, 1024 * h:1024 * h + SEQ], ACT.Identity,
                                     bias=v("b_dw", 6 + h)).then_inc(cm["pv"], 1)

        def act_pw1(act):
            g0 = GROUP0["pw1"]
            b0 = VOFF["b_pw1"][0]
            act.wait_ge(psum_free, g0)
            act.wait_ge(cm["pad"], 1)
            act.wait_ge(nm_out, 40)
            with act.Fori(0, 4) as i:
                for j in range(4):
                    act.wait_ge(psum_ready, i * 4 + (g0 + j + 1))
                    h = j // 2
                    if j % 2 == 0:
                        nc.scalar.activation(thirds(glu[:, ds(i * 2 + h, 1), CC - 1:].rearrange("p a n -> p (a n)")),
                                             psum_set(0), ACT.Identity, bias=vec[:, ds(i * 2 + (b0 + h), 1)])\
                            .then_inc(psum_free, 1)
                    else:
                        act.wait_ge(cm["glu"], i * 2 + (h + 1))
                        nc.scalar.activation(thirds(d_sg[:, h, :]), psum_set(1), ACT.Sigmoid,
                                             bias=vec[:, ds(i * 2 + (b0 + 8 + h), 1)]).then_inc(psum_free, 1)

        def dve_conformer(dve):
            vv, g0 = nc.vector, GROUP0["pw1"]
            w0, bd = VOFF["w_dw"][0], VOFF["b_dw"][0]
            dve.sem_inc(cm["glu"], 2)
            dve.wait_ge(cm["st"], 16)
            w_tap = lambda c, t: vec[:, ds(c * CC + (w0 + t), 1)]

            def rows(c, h, step):
                wrow = vec[:, ds(c * CC + w0, CC - 1)].rearrange("p (a n) -> p a n", a=1).to_broadcast([P, NB, CC - 1])
                x = glu[:, ds(c, 1), :].rearrange("p a n -> p (a n)")
                if step == 0:
                    return vv.tensor_tensor(d_tmp[:, h], d_st[:, ds(c, 1)].rearrange("p a b n -> p (a b) n"), wrow, ALU.mult)
                if step == 1:
                    return vv.tensor_reduce(d_s8[:, h], d_tmp[:, h], AX.X, ALU.add)
                if step == 2:
                    return vv.scalar_tensor_tensor(out=d_s8[:, h], in0=x[:, CC - 1 + SEQ:], scalar=w_tap(c, CC - 1),
                                                   in1=d_s8[:, h], op0=ALU.mult, op1=ALU.add)
                return vv.tensor_scalar(d_tail[:, ds(c, 1), :].rearrange("p a n -> p (a n)"), x[:, SEQ:GW], 1.0, None,
                                        ALU.mult)

            def put_rows(c, h):
                x = glu[:, ds(c, 1), :].rearrange("p a n -> p (a n)")
                return vv.tensor_scalar(x[:, SEQ:T], d_s8[:, h], vec[:, ds(c + bd, 1)], None, ALU.add)

            with S["dve"].loop(3, 2 * 36) as i:
                lag = S["dve"].lag
                dve.wait_ge(cm["glu"], i * 2 + 4)
                for step in range(4):
                    for h in range(2):
                        lag(rows(i * 2 + h, h, step))
                for t in range(CC):
                    for h in range(2):
                        c = i * 2 + h
                        x = glu[:, ds(c, 1), :].rearrange("p a n -> p (a n)")
                        if t == 0:
                            lag(vv.tensor_scalar(d_y[:, h], x[:, 0:SEQ], w_tap(c, 0), vec[:, ds(c + bd, 1)], ALU.mult, ALU.add))
                        else:
                            ins = vv.scalar_tensor_tensor(out=d_y[:, h] if t < CC - 1 else x[:, 0:SEQ], in0=x[:, t:t + SEQ],
                                                          scalar=w_tap(c, t), in1=d_y[:, h], op0=ALU.mult, op1=ALU.add)
                            lag(ins) if (t, h) != (CC - 1, 1) else S["dve"].link(ins)
                lag(put_rows(i * 2, 0))
                S["dve"].link(put_rows(i * 2 + 1, 1))
                dve.sem_inc(cm["out"], 2)
            lag = S["dve"].lag
            dve.wait_ge(cm["glu"], 10)
            for step in range(4):
                for h in range(2):
                    lag(rows(6 + h, h, step))
            for h in range(2):
                dve.wait_ge(cm["pv"], h + 1)
                S["dve"].link(put_rows(6 + h, h))
            dve.sem_inc(cm["out"], 2)
            dve.wait_ge(cm["pv"], 2)
            link = S["dve"].link
            dve.wait_ge(cm["out"], 8)
            link(vv.tensor_tensor(acc1, glu_y[:, 0, :], glu_y[:, 1, :], ALU.add))
            for c in range(2, KC):
                ins = vv.tensor_tensor(acc1, acc1, glu_y[:, c, :], ALU.add)
                if c < KC - 1:
                    link(ins)
            ins.then_inc(cm["sum"], 1)
            dve.wait_ge(cm["by_act"], 2)
            for c in range(KC):
                vv.tensor_tensor(glu_y[:, c, :], glu_y[:, c, :], rbc1, ALU.subtract).then_inc(cm["xc"], 1)

        def pe_mean(pe):
            pe.wait_ge(cm["pv"], 2)
            pe.wait_ge(cm["sum"], 1)
            tl = tiles_of(T)
            for j, (at, cnt, skip, _) in enumerate(tl):
                ins = nc.tensor.matmul(ps[:, 6, j:j + 1], acc1[:, at:at + P], ones[:, 0:1], start=True, stop=True)
            ins.then_inc(cm["by_pe"], 1)
            pe.wait_ge(cm["by_act"], 1)
            for j, (at, cnt, skip, to) in enumerate(tl):
                ins = nc.tensor.matmul(psf[:, to:to + cnt], sm[:, j:j + 1].to_broadcast([P, P]), ident[:, skip:skip + cnt],
                                       start=True, stop=True)
            ins.then_inc(cm["by_pe"], 1)

        def act_mean(act):
            act.wait_ge(cm["by_pe"], 1)
            nc.scalar.activation(sm[:, 0:9], ps[:, 6, 0:9], ACT.Copy, scale=1.0 / D).then_inc(cm["by_act"], 1)
            act.wait_ge(cm["by_pe"], 2)
            nc.scalar.activation(rbc1, psf[:, 0:T], ACT.Copy).then_inc(cm["by_act"], 1)

        copy_to = lambda dst, scale=1.0: (lambda i, j, st: nc.scalar.activation(at_chunk(dst, i * 4 + j), psum_set(st),
                                                                             ACT.Copy, scale=scale))

        def act_memory(act, l):
            act.wait_ge(psum_free, GROUP0[f"mk{l}"])
            epilogue(act, f"mk{l}", 2, lambda i, j, st: nc.scalar.activation(
                m_k[:, ds(i * 4 + j, 1), :].rearrange("p a n -> p (a n)"), ps[:, 3 * st, 0:NMEM], ACT.Copy))
            epilogue(act, f"mv{l}", 2, lambda i, j, st: nc.scalar.activation(
                m_v[:, :, ds(i * 512 + j * P, P)], ps[:, 3 * st, 0:256].rearrange("p (m n) -> p m n", m=2), ACT.Copy))

        block = ctx.enter_context(nc.Block())

        @block.sync
        def _(sp):
            sp_loads(sp)

        @block.gpsimd
        def _(pool):
            S["pool"] = Steps(pool, pool_steps)
            pool_consts(pool)
            pool_fox(pool)
            store(pool, fkT.rearrange("(c p) t -> p c t", p=P), kf)
            store(pool, fv[0:SEQ, :].rearrange("(t p) n -> p t n", p=P), vf)
            store(pool, fv[SEQ:T, :], vs)
            store(pool, flf[0:SEQ, :].rearrange("(t p) n -> p t n", p=P), lf[:, 0:QT, :])
            store(pool, flf[SEQ:T, :], lf[P - NB:P, QT, :])
            pool_fox_rows(pool)
            pool_conv(pool)
            pool_key_pages(pool)
            pool.wait_ge(conv_silu, 12)
            store(pool, gkeep, st_gconv_in.rearrange("p c j b -> p c (j b)")[:, :, NB:])
            store(pool, ckeep.rearrange("p c (b j) -> p c b j", b=NB), st_cconv_in[:, :, :, 1:])
            store(pool, gconv, c_tail)
            pool_gdn(pool)
            pool_gdn_rows(pool)
            pool.wait_ge(gs["out"], 1)
            store(pool, gdn_s, st.rearrange("p b h n -> p (b h) n"))
            pool.wait_ge(gn["u"], 4)
            pool.wait_ge(stored, 16 * n_stored[0])
            pool.sem_inc(mix_free, 1)
            pool_split(pool, 0, 2)
            pool.wait_ge(cat_lo, 8)
            pool_cross(pool, 0)
            pool_split(pool, TILE0["pw1"], TILE0["pw1"] + 2)
            pool_conformer(pool)
            pool_gates(pool)
            pool.wait_ge(cm["out"], 8)
            store(pool, cconv, d_tail)
            pool_split(pool, TILE0["pw2"] + 2, TILE0["pw2"] + 8)
            pool.wait_ge(stored, 16 * n_stored[0])
            pool.wait_ge(nm_out, 48)
            pool_cross(pool, 1)
            for c in range(0, KC, 2):
                pool.wait_ge(nm_out, OUT0[9] + c + 2)
                store(pool, yT.rearrange("p (c t) -> p c t", c=KC)[:, c:c + 2], y_out[:, c:c + 2])
            pool.wait_ge(stored, 16 * n_stored[0])

        @block.scalar
        def _(act):
            S["act"] = Steps(act, act_steps)
            act.wait_ge(consts_ready, 1)

            def once(*pairs):
                return lambda eng, c: after(*pairs)(eng) if c == 0 else None

            def behind(name):
                return lambda eng, c: eng.wait_ge(psum_free, GROUP0[name] + c + 1)

            act_norm(act, 0, xT, T, once((in_loaded, 80)))
            act_values(act)
            act_gates(act)
            epilogue(act, "k_fox", 1, copy_to(kf))
            act_gate_sums(act)
            epilogue(act, "q_fox", 1, copy_to(qf, float(DHB) ** -0.5))
            act_fox(act)
            act_fox_rows(act)
            act_conv(act)
            epilogue(act, "z", 1, lambda i, j, st: nc.scalar.activation(at_chunk(aT, i * 4 + j), psum_set(st), ACT.Silu))
            act_fox_soft(act)
            act_squares(act, big, 8, 1.0)
            act_gdn(act)
            l2_n[0] = 8
            act.wait_ge(gs["vn"], 1)
            act_squares(act, big[:, 8:12, :], HA, 1.0 / P)
            act_cat(act)

            def cross(l):
                act_norm(act, X_NORM[l], xT, T, behind(("out", "pw2")[l]))
                act_norm(act, M_NORM[l], m_raw, NMEM, once((xa["mem"], 16 * (l + 1))))
                act_scale(act, X_NORM[l])
                act_memory(act, l)
                epilogue(act, f"xq{l}", 2, copy_to(q32, float(DHX) ** -0.5))
                act_cross(act, l)

            def mlp(l):
                act_norm(act, F_NORM[l], xT, T, behind(f"xo{l}"))
                act_scale(act, F_NORM[l])
                for g in range(FF_GROUPS):
                    act_up(act, l, g)

            cross(0)
            mlp(0)
            act_norm(act, 4, xT, T, behind("down03"))
            act_scale(act, 4)
            act_pw1(act)
            act_conv_taps(act)
            act_mean(act)
            act_norm(act, 5, glu_y, T, lambda eng, c: eng.wait_ge(cm["xc"], c + 1))
            act_scale(act, 5)
            cross(1)
            mlp(1)
            act_norm(act, 9, xT, T, behind("down13"))

        @block.vector
        def _(dve):
            S["dve"] = Steps(dve, dve_steps)
            dve.wait_ge(consts_ready, 1)
            dve_norm(dve, 0, T)
            dve_scale(dve, 0, xT, hT, T, "norm_mix0")
            dve_gates(dve)
            dve_fox(dve)
            dve_fox_rows(dve)
            dve_conv(dve)
            dve_fox_soft(dve)
            dve_norm_gates(dve)
            dve_gdn(dve)
            dve_fox_out(dve)
            dve_gdn_rows(dve)
            dve_head_norm(dve)
            dve_cat(dve)

            def cross(l):
                if l == 0:
                    dve.wait_ge(fs["back"], 16)
                dve_norm(dve, X_NORM[l], T, ("out", "pw2")[l])
                dve_norm(dve, M_NORM[l], NMEM)
                dve_scale(dve, M_NORM[l], m_raw, m_n, NMEM, f"norm_mem{l}")
                dve_scale(dve, X_NORM[l], xT, None, T, f"norm_x{l}")
                dve_cross(dve, l)

            def mlp(l):
                dve.wait_ge(fs["back"], 16 * (l + 2))
                dve_norm(dve, F_NORM[l], T, f"xo{l}")
                dve_scale(dve, F_NORM[l], xT, None, T, f"norm_f{l}")
                for g in range(FF_GROUPS):
                    dve_up(dve, l, g)
                    if g < FF_GROUPS - 1:
                        residual(dve, f"down{l}{g}", 2)
                dve_norm(dve, (4, 9)[l], T, f"down{l}{FF_GROUPS - 1}")

            cross(0)
            mlp(0)
            dve_scale(dve, 4, xT, None, T, "norm_mix1")
            dve_conformer(dve)
            dve_norm(dve, 5, T)
            dve_scale(dve, 5, glu_y, None, T, "ln_g")
            cross(1)
            mlp(1)
            dve_scale(dve, 9, xT, y_out, T, "norm_out")

        @block.tensor
        def _(pe):
            pe.wait_ge(consts_ready, 1)
            pe_norm(pe, 0, T)
            pe_values(pe)
            pe_gates(pe)
            pe_product(pe, "k_fox", 1, hT, T, after())
            pe_gate_sums(pe)
            pe_product(pe, "q_fox", 1, hT, T, after())
            pe_fox(pe)
            pe_fox_rows(pe)
            pe_product(pe, "conv", 3, hT, T, after())
            pe_product(pe, "z", 1, hT, T, after())
            pe_fox_soft(pe)
            pe_squares(pe, 0, 8)
            pe_gdn(pe)
            pe_gdn_rows(pe)
            pe_head_norm(pe)
            pe_product3(pe, "out", 2, h_hi, h_lo, by_chunk(cat_lo, 0))

            def cross(l):
                pe_norm(pe, X_NORM[l], T)
                pe_norm(pe, M_NORM[l], NMEM)
                pe.wait_ge(nm_out, OUT0[M_NORM[l]] + 8)
                pe.wait_ge(nm_cp, M_NORM[l] + 1)
                pe_memory(pe, l)
                pe_product3(pe, f"xq{l}", 2, h_hi, h_lo, by_chunk(nm_out, OUT0[X_NORM[l]]))
                pe_cross(pe, l)
                pe_product3(pe, f"xo{l}", 2, h_hi, h_lo, at_once((xa["oc"], 8 * l + 10), (xa["pvc"], 2 * l + 2)))
                pe_norm(pe, F_NORM[l], T)

            cross(0)
            pe_mlp(pe, 0)
            pe_norm(pe, 4, T)
            pe_product3(pe, "pw1", 4, h_hi, h_lo, by_chunk(nm_out, OUT0[4]))
            pe_conv(pe)
            pe_mean(pe)
            pe_norm(pe, 5, T)
            pe_product3(pe, "pw2", 2, h_hi, h_lo, by_chunk(nm_out, OUT0[5]))
            cross(1)
            pe_mlp(pe, 1)
            pe_norm(pe, 9, T)


def kernel(**inputs):
    import numpy as np
    import concourse.bacc as bacc
    from concourse.bass_utils import run_bass_kernel_spmd

    a = {k: np.asarray(x) for k, x in inputs.items()}

    def cols(x, c):
        return x.reshape(c, P).T

    def featmajor(x):
        return x.T.reshape(-1, P, x.shape[0]).transpose(1, 0, 2)

    def tiles(wm):
        n = wm.shape[1] // 256
        return wm.reshape(KC, P, n, 256).transpose(2, 1, 0, 3).reshape(n, P, KC * 256)

    def tiles_b(wm):
        n = wm.shape[1] // P
        return wm.reshape(KC, P, n, P).transpose(2, 1, 0, 3).reshape(n, P, KC * P)

    def rows(x):
        return np.broadcast_to(x[None, :], (P, x.shape[0]))

    w_in = a["w_in_e"][0]
    o_z, o_a, o_b, o_q, o_k, o_v, o_f = 1536, 2048, 2052, 2056, 2568, 3080, 3592
    gates = w_in[:, list(range(o_a, o_q)) + list(range(o_f, o_f + HB))]
    z4, z8 = np.zeros(4, np.float32), np.zeros(8, np.float32)
    vecs = np.concatenate(
        [cols(a[n][l], 8) for n in ("norm_mix", "norm_x", "norm_f", "norm_mem") for l in range(2)]
        + [cols(a["norm_out"], 8), cols(a["b_pw1"][0], 16)] + [cols(a[n][0], 8) for n in ("b_dw", "ln_g", "ln_b")]
        + [a["gnorm_a"][0][:, None], a["conv_a"][0].reshape(CA, 12, P).transpose(2, 1, 0).reshape(P, 48),
           a["w_dw"][0].reshape(CC, KC, P).transpose(2, 1, 0).reshape(P, KC * CC),
           rows(np.concatenate([a["dt_bias"][0], z4, a["b_f"][0]])), rows(np.concatenate([a["a_log"][0], z4, z8]))], axis=1)
    pw1 = tiles_b(a["w_pw1"][0])
    pw1 = np.stack([pw1[:8], pw1[8:]], 1).reshape(pw1.shape)
    stream = [tiles(w_in[:, o_v:o_v + 512]), tiles(w_in[:, o_k:o_k + 512]), tiles(w_in[:, o_q:o_q + 512]),
              tiles(w_in[:, :1536]), tiles(w_in[:, o_z:o_z + 512])]
    stream_b = [tiles_b(a["w_out_e"][0])]
    for l in range(2):
        if l:
            stream_b += [pw1, tiles_b(a["w_pw2"][0])]
        stream_b += [tiles_b(a["w_xkv"][l]), tiles_b(a["w_xq"][l]), tiles_b(a["w_xo"][l])]
        for g in range(FF_GROUPS):
            stream_b += [tiles_b(a["w_up"][l][:, g * D:g * D + D]), tiles_b(a["w_down"][l][g * D:g * D + D])]
    arrays = {
        "xT_in": np.concatenate([featmajor(a["x_prompt"][0]), featmajor(a["x_sample"][:, 0])], axis=2),
        "memT_in": featmajor(a["mem_prompt"][0]),
        "vecs_in": vecs,
        "wall": np.concatenate(stream, axis=0),
        "wallb": np.concatenate(stream_b, axis=0),
        "wgate_in": gates.reshape(KC, P, 16).transpose(1, 0, 2),
        "st_gconv_in": a["state_gdn_conv"][0].transpose(2, 1, 0).reshape(12, P, 3, NB).transpose(1, 0, 2, 3),
        "st_cconv_in": a["state_cfm_conv"][0].transpose(2, 0, 1).reshape(KC, P, NB, CC - 1).transpose(1, 0, 2, 3),
        "pages_in": a["page_table"].reshape(1, NB * NPG),
        "kpool": a["cache_fox_k"][0].reshape(-1, PAGE, 512),
        "vpool": a["cache_fox_v"][0].reshape(-1, PAGE, 512),
        "fpool": a["cache_fox_logf"][0],
        "st_gdn": a["state_gdn"][0],
        "cmk": a["cache_mem_k"].reshape(2, NB, NMEM, D),
        "cmv": a["cache_mem_v"].reshape(2, NB, NMEM, D),
    }
    outs = {"yT": (P, KC * T), "fkT": (512, T), "fv": (T, 512), "flf": (T, HB), "gdn_p": (P, HA, P),
            "gconv": (P, 12, 3 + NB), "gkeep": (P, 12, 2 * NB), "gdn_s": (P, NB * HA, P), "cconv": (P, KC, 30 + NB), "ckeep": (P, KC, NB * 29),
            "mkT": (2, D, NMEM), "mv": (2, NMEM, D)}
    nc = bacc.Bacc("TRN2", target_bir_lowering=False, num_devices=1)
    arrays = {k: np.ascontiguousarray(x) for k, x in arrays.items()}
    args = {k: nc.dram_tensor(k, x.shape, mybir.dt.from_np(x.dtype), kind="ExternalInput").ap() for k, x in arrays.items()}
    args.update({k: nc.dram_tensor(k, s, F32, kind="ExternalOutput").ap() for k, s in outs.items()})
    args["x_spill"] = nc.dram_tensor("x_spill", (P, KC, T), F32, kind="Internal").ap()
    build(nc, **args)
    r = run_bass_kernel_spmd(nc, [arrays], core_ids=[0]).results[0]

    y = r["yT"].reshape(P, KC, T).transpose(2, 1, 0).reshape(T, D)
    fk = r["fkT"].T.reshape(T, HB, DHB)
    fv_ = r["fv"].reshape(T, HB, DHB)
    gconv = r["gconv"].transpose(2, 1, 0).reshape(3 + NB, 12 * P)
    cconv = r["cconv"].transpose(2, 1, 0).reshape(30 + NB, D)
    gkeep = r["gkeep"].reshape(P, 12, 2, NB).transpose(3, 2, 1, 0).reshape(NB, 2, 12 * P)
    ckeep = r["ckeep"].reshape(P, KC, NB, 29).transpose(2, 3, 1, 0).reshape(NB, 29, D)
    return (y[:SEQ][None], y[SEQ:][:, None], fk[:SEQ][None, None], fv_[:SEQ][None, None], r["flf"][:SEQ][None, None],
            fk[SEQ:][None, :, None], fv_[SEQ:][None, :, None], r["flf"][SEQ:][None, :, None],
            r["gdn_p"].transpose(1, 0, 2)[None, None], gconv[None, None, :3],
            r["gdn_s"].reshape(P, NB, HA, P).transpose(1, 2, 0, 3)[None], np.concatenate([gkeep, gconv[3:][:, None]], axis=1)[None],
            cconv[None, None, :30], np.concatenate([ckeep, cconv[30:][:, None]], axis=1)[None],
            r["mkT"].transpose(0, 2, 1).reshape(2, 1, NMEM, HX, DHX), r["mv"].reshape(2, 1, NMEM, HX, DHX))
```
